# Optimizing a Trainium2 kernel written in Bass

```python
import jax
import jax.numpy as jnp
from jax import lax
import numpy as np

D_MODEL = 1024
BATCH = 1
SEQ = 512
DEPTH = 2

HEAD_DIM = 64
N_HEADS_MIX = D_MODEL // HEAD_DIM
H_MOBA = N_HEADS_MIX // 4
H_NSA = N_HEADS_MIX // 2
H_SB = N_HEADS_MIX - H_MOBA - H_NSA
D_MIX = N_HEADS_MIX * HEAD_DIM
ROT_DIM = HEAD_DIM // 4
ROPE_THETA = 500000.0
Q_BLOCK = 128
MOBA_BLOCK = 256
MOBA_TOPK = 3
NSA_KV_HEADS = 2
NSA_GROUP = H_NSA // NSA_KV_HEADS
NSA_CMP_LEN = 32
NSA_CMP_STRIDE = 16
NSA_CMP_HIDDEN = 256
NSA_SLC_BLOCK = 64
NSA_SLC_TOPN = 16
NSA_WINDOW = 512
NSA_FORCE_SCORE = 1e4
MEM_TOKENS = 256
X_HEADS = 4
X_HEAD_DIM = D_MODEL // X_HEADS
D_FF = 2816
CONV_WIDTH = 3
MAX_POS_OFFSET = 4096
EPS = 1e-6
NEG = -1e30
PROJ_SIZES = (H_MOBA * HEAD_DIM,) * 3 + (H_NSA * HEAD_DIM,) + (NSA_KV_HEADS * HEAD_DIM,) * 6 + (3 * H_NSA,) + (H_SB * HEAD_DIM,) * 3
D_PROJ = sum(PROJ_SIZES)

kernel_name = 'hybrid_moba_nsa_stickbreaking_block'

def rms_norm(x, g):
    xf = x.astype(jnp.float32)
    y = xf * lax.rsqrt(jnp.mean(xf * xf, axis=-1, keepdims=True) + EPS)
    return (y * g.astype(jnp.float32)).astype(x.dtype)

def rope_partial(x, pos):
    half = ROT_DIM // 2
    inv_freq = ROPE_THETA ** (-jnp.arange(half, dtype=jnp.float32) / half)
    ang = pos.astype(jnp.float32)[:, None, :, None] * inv_freq
    cos = jnp.cos(ang).astype(x.dtype)
    sin = jnp.sin(ang).astype(x.dtype)
    x1 = x[..., :half]
    x2 = x[..., half:ROT_DIM]
    return jnp.concatenate([x1 * cos - x2 * sin, x2 * cos + x1 * sin, x[..., ROT_DIM:]], axis=-1)

def masked_softmax(s, mask):
    s = jnp.where(mask, s.astype(jnp.float32), NEG)
    return jax.nn.softmax(s, axis=-1) * mask

def heads(t, n):
    B, S, _ = t.shape
    return t.reshape(B, S, n, HEAD_DIM).transpose(0, 2, 1, 3)

def chunks_to_seq(o):
    nq, B, H, Q, D = o.shape
    return o.transpose(1, 2, 0, 3, 4).reshape(B, H, nq * Q, D)

def moba_attention(q, k, v):
    B, H, S, D = q.shape
    L = MOBA_BLOCK
    nb = -(-S // L)
    pad = nb * L - S
    kp = jnp.pad(k, ((0, 0), (0, 0), (0, pad), (0, 0))).reshape(B, H, nb, L, D)
    vp = jnp.pad(v, ((0, 0), (0, 0), (0, pad), (0, 0))).reshape(B, H, nb, L, D)
    k_mean = jnp.mean(kp, axis=3)
    kk = max(1, min(MOBA_TOPK, nb - 1))
    scale = D ** -0.5
    bi = jnp.arange(B)[:, None, None, None]
    hi = jnp.arange(H)[None, :, None, None]
    blk = jnp.arange(nb)

    def chunk(c):
        q0 = c * Q_BLOCK
        qpos = q0 + jnp.arange(Q_BLOCK)
        qc = lax.dynamic_slice_in_dim(q, q0, Q_BLOCK, axis=2)
        own = q0 // L
        gate = jnp.einsum('bhqd,bhnd->bhqn', qc, k_mean).astype(jnp.float32)
        gate = jnp.where(blk < own, gate, NEG)
        _, idx = lax.top_k(gate, kk)
        valid = idx < own
        k_sel = kp[bi, hi, idx]
        v_sel = vp[bi, hi, idx]
        s_sel = jnp.einsum('bhqd,bhqnld->bhqnl', qc, k_sel).reshape(B, H, Q_BLOCK, kk * L)
        m_sel = jnp.broadcast_to(valid[..., None], (B, H, Q_BLOCK, kk, L)).reshape(B, H, Q_BLOCK, kk * L)
        k_own = lax.dynamic_index_in_dim(kp, own, axis=2, keepdims=False)
        v_own = lax.dynamic_index_in_dim(vp, own, axis=2, keepdims=False)
        s_own = jnp.einsum('bhqd,bhld->bhql', qc, k_own)
        kpos = own * L + jnp.arange(L)
        m_own = jnp.broadcast_to(kpos[None, :] <= qpos[:, None], (B, H, Q_BLOCK, L))
        s = jnp.concatenate([s_sel, s_own], axis=-1) * scale
        m = jnp.concatenate([m_sel, m_own], axis=-1)
        p = masked_softmax(s, m).astype(v.dtype)
        p_sel = p[..., :kk * L].reshape(B, H, Q_BLOCK, kk, L)
        p_own = p[..., kk * L:]
        return jnp.einsum('bhqnl,bhqnld->bhqd', p_sel, v_sel) + jnp.einsum('bhql,bhld->bhqd', p_own, v_own)

    return chunks_to_seq(lax.map(chunk, jnp.arange(S // Q_BLOCK)))

def nsa_num_cmp(S):
    return (S - NSA_CMP_LEN) // NSA_CMP_STRIDE + 1

def nsa_compress(x, pe, w1, w2):
    B, G, S, D = x.shape
    nc = nsa_num_cmp(S)
    idx = np.arange(nc)[:, None] * NSA_CMP_STRIDE + np.arange(NSA_CMP_LEN)[None, :]
    blocks = (x[:, :, idx] + pe).reshape(B, G, nc, NSA_CMP_LEN * D)
    return jax.nn.gelu(blocks @ w1) @ w2

def nsa_overlap(S):
    nc = nsa_num_cmp(S)
    nsb = S // NSA_SLC_BLOCK
    cs = np.arange(nc) * NSA_CMP_STRIDE
    ce = cs + NSA_CMP_LEN
    bs = np.arange(nsb) * NSA_SLC_BLOCK
    be = bs + NSA_SLC_BLOCK
    ov = (cs[:, None] < be[None, :]) & (ce[:, None] > bs[None, :])
    return jnp.asarray(ov.astype(np.float32))

def nsa_attention(q, kc, vc, ks, vs, kw, vw, gates):
    B, H, S, D = q.shape
    G, R = NSA_KV_HEADS, NSA_GROUP
    nc = kc.shape[2]
    nsb = S // NSA_SLC_BLOCK
    topn = min(NSA_SLC_TOPN, nsb)
    SL = NSA_SLC_BLOCK
    cmp_end = jnp.asarray(np.arange(nc) * NSA_CMP_STRIDE + NSA_CMP_LEN - 1)
    overlap = nsa_overlap(S)
    ksb = ks.reshape(B, G, nsb, SL, D)
    vsb = vs.reshape(B, G, nsb, SL, D)
    kwp = jnp.pad(kw, ((0, 0), (0, 0), (NSA_WINDOW, 0), (0, 0)))
    vwp = jnp.pad(vw, ((0, 0), (0, 0), (NSA_WINDOW, 0), (0, 0)))
    scale = D ** -0.5
    bi = jnp.arange(B)[:, None, None, None]
    gi = jnp.arange(G)[None, :, None, None]
    jb = jnp.arange(nsb)

    def chunk(c):
        q0 = c * Q_BLOCK
        qpos = q0 + jnp.arange(Q_BLOCK)
        qg = lax.dynamic_slice_in_dim(q, q0, Q_BLOCK, axis=2).reshape(B, G, R, Q_BLOCK, D)
        gc = lax.dynamic_slice_in_dim(gates, q0, Q_BLOCK, axis=2).reshape(B, G, R, Q_BLOCK, 3)
        s_c = jnp.einsum('bgrqd,bgnd->bgrqn', qg, kc) * scale
        p_c = masked_softmax(s_c, cmp_end[None, :] <= qpos[:, None])
        o_c = jnp.einsum('bgrqn,bgnd->bgrqd', p_c.astype(vc.dtype), vc)
        imp = jnp.einsum('bgrqn,nj->bgqj', p_c, overlap)
        cur = (qpos // SL)[:, None]
        forced = (jb == 0) | (jb == cur) | (jb == cur - 1)
        imp = jnp.where(forced, NSA_FORCE_SCORE, imp)
        imp = jnp.where(jb <= cur, imp, NEG)
        _, sidx = lax.top_k(imp, topn)
        k_sel = ksb[bi, gi, sidx]
        v_sel = vsb[bi, gi, sidx]
        kpos = sidx[..., None] * SL + jnp.arange(SL)
        m_s = (kpos <= qpos[:, None, None])[:, :, None].reshape(B, G, 1, Q_BLOCK, topn * SL)
        s_s = jnp.einsum('bgrqd,bgqnld->bgrqnl', qg, k_sel).reshape(B, G, R, Q_BLOCK, topn * SL) * scale
        p_s = masked_softmax(s_s, m_s).reshape(B, G, R, Q_BLOCK, topn, SL)
        o_s = jnp.einsum('bgrqnl,bgqnld->bgrqd', p_s.astype(vs.dtype), v_sel)
        k_win = lax.dynamic_slice_in_dim(kwp, q0, Q_BLOCK + NSA_WINDOW, axis=2)
        v_win = lax.dynamic_slice_in_dim(vwp, q0, Q_BLOCK + NSA_WINDOW, axis=2)
        wpos = q0 - NSA_WINDOW + jnp.arange(Q_BLOCK + NSA_WINDOW)
        dlt = qpos[:, None] - wpos[None, :]
        m_w = (dlt >= 0) & (dlt < NSA_WINDOW) & (wpos >= 0)[None, :]
        s_w = jnp.einsum('bgrqd,bgkd->bgrqk', qg, k_win) * scale
        p_w = masked_softmax(s_w, m_w)
        o_w = jnp.einsum('bgrqk,bgkd->bgrqd', p_w.astype(vw.dtype), v_win)
        o = gc[..., 0:1] * o_c + gc[..., 1:2] * o_s + gc[..., 2:3] * o_w
        return o.reshape(B, H, Q_BLOCK, D)

    return chunks_to_seq(lax.map(chunk, jnp.arange(S // Q_BLOCK)))

def stick_breaking_attention(q, k, v):
    B, H, S, D = q.shape
    scale = D ** -0.5
    kpos = jnp.arange(S)

    def chunk(c):
        q0 = c * Q_BLOCK
        qpos = q0 + jnp.arange(Q_BLOCK)
        qc = lax.dynamic_slice_in_dim(q, q0, Q_BLOCK, axis=2)
        z = jnp.einsum('bhqd,bhkd->bhqk', qc, k).astype(jnp.float32) * scale
        causal = kpos[None, :] < qpos[:, None]
        sp = jnp.where(causal, jax.nn.softplus(z), 0.0)
        tail = lax.cumsum(sp, axis=3, reverse=True) - sp
        a = jnp.where(causal, jnp.exp(jax.nn.log_sigmoid(z) - tail), 0.0)
        return jnp.einsum('bhqk,bhkd->bhqd', a.astype(v.dtype), v)

    return chunks_to_seq(lax.map(chunk, jnp.arange(S // Q_BLOCK)))

def hybrid_mixer(h, pos, w_in, w_out, cmp_pe_k, cmp_pe_v, cmp_wk1, cmp_wk2, cmp_wv1, cmp_wv2):
    B, S, _ = h.shape
    proj = h @ w_in
    cuts = [int(c) for c in np.cumsum(PROJ_SIZES)[:-1]]
    (mq, mk, mv, nq, nkc, nvc, nks, nvs, nkw, nvw, ng, sq, sk, sv) = jnp.split(proj, cuts, axis=-1)
    o_moba = moba_attention(rope_partial(heads(mq, H_MOBA), pos), rope_partial(heads(mk, H_MOBA), pos), heads(mv, H_MOBA))
    nc = nsa_num_cmp(S)
    pos_end = pos[:, np.arange(nc) * NSA_CMP_STRIDE + NSA_CMP_LEN - 1]
    kc = rope_partial(nsa_compress(heads(nkc, NSA_KV_HEADS), cmp_pe_k, cmp_wk1, cmp_wk2), pos_end)
    vc = nsa_compress(heads(nvc, NSA_KV_HEADS), cmp_pe_v, cmp_wv1, cmp_wv2)
    gates = jax.nn.sigmoid(ng).reshape(B, S, H_NSA, 3).transpose(0, 2, 1, 3)
    o_nsa = nsa_attention(rope_partial(heads(nq, H_NSA), pos), kc, vc,
                          rope_partial(heads(nks, NSA_KV_HEADS), pos), heads(nvs, NSA_KV_HEADS),
                          rope_partial(heads(nkw, NSA_KV_HEADS), pos), heads(nvw, NSA_KV_HEADS), gates)
    o_sb = stick_breaking_attention(heads(sq, H_SB), heads(sk, H_SB), heads(sv, H_SB))
    o = jnp.concatenate([o_moba, o_nsa, o_sb], axis=1)
    return o.transpose(0, 2, 1, 3).reshape(B, S, D_MIX) @ w_out

def cross_attention(h, m, wq, wk, wv, wo):
    B, S, _ = h.shape
    M = m.shape[1]
    q = (h @ wq).reshape(B, S, X_HEADS, X_HEAD_DIM)
    k = (m @ wk).reshape(B, M, X_HEADS, X_HEAD_DIM)
    v = (m @ wv).reshape(B, M, X_HEADS, X_HEAD_DIM)
    s = jnp.einsum('bshd,bmhd->bhsm', q, k).astype(jnp.float32) * (X_HEAD_DIM ** -0.5)
    p = jax.nn.softmax(s, axis=-1).astype(v.dtype)
    o = jnp.einsum('bhsm,bmhd->bshd', p, v).reshape(B, S, D_MODEL)
    return o @ wo

def conv_ffn(h, w_up, conv_w, conv_b, w_down):
    u = h @ w_up
    a, b = u[..., :D_FF], u[..., D_FF:]
    a = lax.conv_general_dilated(a, conv_w[:, None, :].astype(a.dtype), window_strides=(1,),
                                 padding=[(CONV_WIDTH - 1, 0)], dimension_numbers=('NWC', 'WIO', 'NWC'),
                                 feature_group_count=D_FF) + conv_b
    return (jax.nn.gelu(a) * b) @ w_down

def setup_inputs(seed: int = 0) -> dict:
    key = jax.random.key(seed)
    ks = jax.random.split(key, 28)
    f32 = jnp.float32

    def w(k, shape, fan_in):
        return jax.random.normal(k, shape, f32) * fan_in ** -0.5

    def gain(k, n=D_MODEL):
        return 1.0 + 0.02 * jax.random.normal(k, (DEPTH, n), f32)

    x = jax.random.normal(ks[0], (BATCH, SEQ, D_MODEL), f32)
    mem = jax.random.normal(ks[1], (BATCH, MEM_TOKENS, D_MODEL), f32)
    offset = jax.random.randint(ks[2], (BATCH, 1), 0, MAX_POS_OFFSET, dtype=jnp.int32)
    positions = offset + jnp.arange(SEQ, dtype=jnp.int32)[None, :]
    cmp_in = NSA_CMP_LEN * HEAD_DIM
    return {
        'x': x,
        'mem': mem,
        'positions': positions,
        'norm_mix_pre': gain(ks[3]),
        'norm_mix_post': gain(ks[4]),
        'w_in': w(ks[5], (DEPTH, D_MODEL, D_PROJ), D_MODEL),
        'w_out': w(ks[6], (DEPTH, D_MIX, D_MODEL), D_MIX),
        'cmp_pe_k': 0.02 * jax.random.normal(ks[7], (DEPTH, NSA_CMP_LEN, HEAD_DIM), f32),
        'cmp_pe_v': 0.02 * jax.random.normal(ks[8], (DEPTH, NSA_CMP_LEN, HEAD_DIM), f32),
        'cmp_wk1': w(ks[9], (DEPTH, cmp_in, NSA_CMP_HIDDEN), cmp_in),
        'cmp_wk2': w(ks[10], (DEPTH, NSA_CMP_HIDDEN, HEAD_DIM), NSA_CMP_HIDDEN),
        'cmp_wv1': w(ks[11], (DEPTH, cmp_in, NSA_CMP_HIDDEN), cmp_in),
        'cmp_wv2': w(ks[12], (DEPTH, NSA_CMP_HIDDEN, HEAD_DIM), NSA_CMP_HIDDEN),
        'norm_x_pre': gain(ks[13]),
        'norm_x_post': gain(ks[14]),
        'norm_mem': gain(ks[15]),
        'x_wq': w(ks[16], (DEPTH, D_MODEL, D_MODEL), D_MODEL),
        'x_wk': w(ks[17], (DEPTH, D_MODEL, D_MODEL), D_MODEL),
        'x_wv': w(ks[18], (DEPTH, D_MODEL, D_MODEL), D_MODEL),
        'x_wo': w(ks[19], (DEPTH, D_MODEL, D_MODEL), D_MODEL),
        'norm_ffn_pre': gain(ks[20]),
        'norm_ffn_post': gain(ks[21]),
        'ffn_w_up': w(ks[22], (DEPTH, D_MODEL, 2 * D_FF), D_MODEL),
        'ffn_conv_w': w(ks[23], (DEPTH, CONV_WIDTH, D_FF), CONV_WIDTH),
        'ffn_conv_b': 0.01 * jax.random.normal(ks[24], (DEPTH, D_FF), f32),
        'ffn_w_down': w(ks[25], (DEPTH, D_FF, D_MODEL), D_FF),
    }

def reference(x, mem, positions, norm_mix_pre, norm_mix_post, w_in, w_out, cmp_pe_k, cmp_pe_v,
              cmp_wk1, cmp_wk2, cmp_wv1, cmp_wv2, norm_x_pre, norm_x_post, norm_mem,
              x_wq, x_wk, x_wv, x_wo, norm_ffn_pre, norm_ffn_post, ffn_w_up, ffn_conv_w, ffn_conv_b, ffn_w_down):
    h = x
    for l in range(DEPTH):
        a = rms_norm(h, norm_mix_pre[l])
        mix = hybrid_mixer(a, positions, w_in[l], w_out[l], cmp_pe_k[l], cmp_pe_v[l],
                           cmp_wk1[l], cmp_wk2[l], cmp_wv1[l], cmp_wv2[l])
        h = h + rms_norm(mix, norm_mix_post[l])
        a = rms_norm(h, norm_x_pre[l])
        m = rms_norm(mem, norm_mem[l])
        h = h + rms_norm(cross_attention(a, m, x_wq[l], x_wk[l], x_wv[l], x_wo[l]), norm_x_post[l])
        a = rms_norm(h, norm_ffn_pre[l])
        h = h + rms_norm(conv_ffn(a, ffn_w_up[l], ffn_conv_w[l], ffn_conv_b[l], ffn_w_down[l]), norm_ffn_post[l])
    return h


_drawn_inputs = setup_inputs


def setup_inputs(seed=0):
    import zlib

    import numpy as np

    out = dict(_drawn_inputs(seed))
    spreads = {}
    factors = {'norm_mix_post': 2.865,
     'cmp_pe_k': 8.0,
     'cmp_pe_v': 5.165,
     'norm_x_pre': 3.428,
     'norm_x_post': 3.253,
     'norm_ffn_pre': 3.031,
     'norm_ffn_post': 4.19,
     'ffn_conv_b': 8.0}
    for name, (base, spread) in spreads.items():
        noise = np.random.default_rng([zlib.crc32(name.encode()), seed]).standard_normal(out[name].shape)
        drawn = base * np.exp(spread * noise) if base else spread * noise
        out[name] = jnp.asarray(drawn.astype(out[name].dtype))
    for name, factor in factors.items():
        out[name] = (out[name] * factor).astype(out[name].dtype)
    return out
```

```python
import numpy as np
import concourse.bass as bass
from concourse import mybir
from contextlib import ExitStack

F32 = mybir.dt.float32
F32R = mybir.dt.float32r
I32 = mybir.dt.int32
ACT = mybir.ActivationFunctionType
ALU = mybir.AluOpType
AX = mybir.AxisListType

P = 128
D = 1024
S = 512
T = S // P
KD = D // P
DEPTH = 2
HD = 64
NPROJ = 2840
FF = 2816
NF = FF // P
MEM = 256
EPS = 1e-6
NEG = -1e30
NCMP = 31
CMPP = 32

MQ, MK, MV = 0, 256, 512
NQ, NKC, NVC, NKS, NVS, NKW, NVW = 768, 1280, 1408, 1536, 1664, 1792, 1920
NG, SQ, SK, SV = 2048, 2072, 2328, 2584

RING = 3
UW = 2048
U_IN, U_CMP, U_OUT, U_XK, U_XV, U_XQ, U_XO, U_UP, U_DOWN = 0, 12, 16, 20, 24, 28, 32, 36, 58
UNITS = 69
assert UNITS % RING == 0
IN_W = [512] * 5 + [280]

ITEMS = [(h, "moba") for h in range(4)] + [(4 + h, k) for h in range(8) for k in ("cmp", "sel", "win")]
NI = T * len(ITEMS)
SB_OFF = [0, 512, 896, 1152]
SB_W = [512, 384, 256, 128]
SB_ALL = 1280


def item_keys(i):
    return CMPP if ITEMS[i % len(ITEMS)][1] == "cmp" else P * (i // len(ITEMS) + 1)


def item_rows(i):
    return CMPP if ITEMS[i % len(ITEMS)][1] == "cmp" else P


def item_width(i):
    return P if ITEMS[i % len(ITEMS)][1] == "cmp" else P * (i // len(ITEMS) + 1)


def blk_bank(b):
    return b if b < 4 else (4, 5, 6, 7, 0, 1)[(b - 4) % 6]


def row_broadcast(vec, l):
    return vec[l].unsqueeze(0).broadcast_to([P, vec.shape[1]])


class Signal:

    def __init__(self, sem, per_layer, start=0):
        self.sem, self.per_layer, self.start, self.seen = sem, per_layer, start, 0

    def at(self, l, n):
        return l * self.per_layer + (n + self.start)


def build(nc, x, mem, positions, norm_mix_pre, norm_mix_post, w_in, w_out, cmp_pe_k, cmp_pe_v,
          cmp_wk1, cmp_wk2, cmp_wv1, cmp_wv2, norm_x_pre, norm_x_post, norm_mem,
          x_wq, x_wk, x_wv, x_wo, norm_ffn_pre, norm_ffn_post, ffn_w_up, ffn_conv_w, ffn_conv_b,
          ffn_w_down, out):
    ctx = ExitStack()
    with ctx:
        place = [(nc.sbuf_base + 63) // 64 * 64]

        def region(nbytes):
            at = place[0]
            place[0] += (nbytes + 31) // 32 * 32
            assert place[0] <= nc.sbuf_usable_end, place
            return at

        def view(name, shape, dt, offset):
            return nc.alloc_sbuf_tensor_at(name, shape, dt, offset=offset)

        def new(name, shape, dt=F32):
            return view(name, shape, dt, region(int(np.prod(shape[1:])) * 4))

        raw = new("raw", [P, RING, UW])
        w_hi = new("w_hi", [P, RING, UW], F32R)
        w_lo = new("w_lo", [P, RING, UW], F32R)
        h = new("h", [P, T, D])
        X = region(2 * KD * S * 4)
        a_hi = view("a_hi", [P, KD, S], F32R, X)
        a_lo = view("a_lo", [P, KD, S], F32R, X + KD * S * 4)
        qT = view("qT", [P, 8, S], F32, X)
        kT = view("kT", [P, 6, S], F32, X + KD * S * 4)
        Y = region(T * NPROJ * 4)
        proj = view("proj", [P, T, NPROJ], F32, Y)
        m_hi = view("m_hi", [P, KD, MEM], F32R, Y)
        m_lo = view("m_lo", [P, KD, MEM], F32R, Y + 8192)
        xqT = view("xqT", [P, KD, S], F32, Y + 16384)
        xkT = view("xkT", [P, KD, MEM], F32, Y + 32768)
        gain_row = view("gain_row", [P, D], F32, Y + 40960)
        gT = view("gT", [P, NF, S], F32, Y)
        R = region(T * D * 4)
        rows = view("rows", [P, T, D], F32, R)
        rope_tmp = view("rope_tmp", [P, 4, T * 64], F32, R)
        twice = view("twice", [P, T, 4, 2, HD], F32, R + 4096)
        xb = view("xb", [P, 16 * 62], F32, R)
        xb_hi = view("xb_hi", [P, 16 * 62], F32R, R + 3968)
        xb_lo = view("xb_lo", [P, 16 * 62], F32R, R + 7936)
        w2 = view("w2", [P, 2, 2, HD], F32, R + 11904)
        cg = view("cg", [P, 2, 256], F32, R + 12928)
        cgT = view("cgT", [P, 2, 62], F32, R + 14976)
        kc_rows = view("kc_rows", [32, 2, HD], F32, R + 15488)
        rope_tmp2 = view("rope_tmp2", [32, 4, 16], F32, R + 16000)
        vec_rows = view("vec_rows", [P, 2, P], F32, R + 8192)
        vec_a, vec_b = vec_rows[:, 0, :], vec_rows[:, 1, :]
        M = region(2 * D * 4)
        mem_rows = view("mem_rows", [P, 2, D], F32, M)
        xv = view("xv", [P, 2, D], F32, M)
        gain_row_ffn = view("gain_row_ffn", [P, D], F32, M)
        W = region(6 * S * 4)
        prob = view("prob", [P, 3, S], F32, W)
        probT = view("probT", [P, 3, S], F32, W + 3 * S * 4)
        sb_sp = view("sb_sp", [P, SB_ALL], F32, W)
        sb_tmp = view("sb_tmp", [P, SB_ALL], F32, W + SB_ALL * 4)
        xprob = view("xprob", [P, 2, MEM], F32, W)
        xprobT = view("xprobT", [P, 2, 2, S], F32, W + 4096)
        conv = view("conv", [P, 3, S], F32, W)
        gel = view("gel", [P, 3, S], F32, W + 3 * S * 4)
        stage = view("stage", [P, 5, P], F32, W)

        ident = new("ident", [P, P])
        ident_r = new("ident_r", [P, P], F32R)
        causal = new("causal", [P, P], F32R)
        strictT = new("strictT", [P, P], F32R)
        strict_mul = new("strict_mul", [P, P])
        neg_tri = new("neg_tri", [P, P])
        neg_ones = new("neg_ones", [P, P])
        cmp_mask = new("cmp_mask", [P, T, CMPP], F32R)
        cmp_valid = new("cmp_valid", [P, T])
        vecs = new("vecs", [P, 152])
        sums = new("sums", [P, 40])
        est = new("est", [P, 40])
        rstd = new("rstd", [P, 40])
        nt = new("nt", [P, 2])
        eps_t = new("eps_t", [P, 1])
        cos_t = new("cos_t", [P, 5, 8])
        sin_t = new("sin_t", [P, 5, 8])
        kcT = new("kcT", [P, CMPP])
        vc_rows = new("vc_rows", [32, 2, HD])
        gates = new("gates", [P, T, 24])
        neg_max = new("neg_max", [P, 8])
        den = new("den", [P, 8])
        rden = new("rden", [P, 8])
        pos_i = view("pos_i", [P, 5], I32, R)
        pos_f = view("pos_f", [P, 5], F32, R + 32)
        ang = view("ang", [P, 2, 40], F32, R + 64)
        turns = view("turns", [P, 2, 40], F32, R + 64 + 320)

        banks = ctx.enter_context(nc.psum_tensor("banks", [P, 8 * 512], F32))

        def bank(b, n=512, at=0, rows_=P):
            return banks[0:rows_, b * 512 + at:b * 512 + at + n]

        signals = {}

        def signal(name, per_layer, start=0):
            s = Signal(ctx.enter_context(nc.semaphore(name)), per_layer, start)
            signals[name] = s
            return s

        def plain(name):
            return ctx.enter_context(nc.semaphore(name))

        pro_x, pro_pos, pro_const, pro_rope, pro_dve, pro_act, pro_pool = (
            plain(n) for n in ("pro_x", "pro_pos", "pro_const", "pro_rope", "pro_dve", "pro_act", "pro_pool"))
        stored = plain("stored")
        dve_chain, act_chain = plain("dve_chain"), plain("act_chain")
        raw_landed = [plain(f"raw_landed{i}") for i in range(RING)]
        hi_made = signal("hi_made", UNITS)
        lo_made = signal("lo_made", UNITS, RING)
        unit_used = signal("unit_used", UNITS, RING)
        vecs_landed = signal("vecs_landed", 128)
        w2_landed = signal("w2_landed", 32)
        mem_landed = signal("mem_landed", 16)
        gain_landed = [signal(f"gain_landed{i}", 16) for i in range(3)]
        vecs_T = signal("vecs_T", 2)
        vecs_ready = signal("vecs_ready", 2)
        pre_est = signal("pre_est", 12)
        post_est = signal("post_est", 12)
        mem_est = signal("mem_est", 2)
        mem_normed = signal("mem_normed", 2)
        h_done = signal("h_done", 12, 1)
        rows_done = signal("rows_done", 12)
        aT_psum = signal("aT_psum", 32)
        aT_hi = signal("aT_hi", 32)
        aT_lo = signal("aT_lo", 32)
        mT_psum = signal("mT_psum", KD)
        mT_hi = signal("mT_hi", KD)
        mT_lo = signal("mT_lo", KD)
        proj_psum = signal("proj_psum", 18)
        proj_act = signal("proj_act", 12)
        proj_dve = signal("proj_dve", 12)
        roped = signal("roped", 4)
        gated = signal("gated", 1)
        blk_psum = signal("blk_psum", 18)
        blk_act = signal("blk_act", 7)
        blk_dve = signal("blk_dve", 7)
        xb_ready = signal("xb_ready", 2)
        cmp_gelu = signal("cmp_gelu", 2)
        cgT_psum = signal("cgT_psum", 2)
        cgT_ready = signal("cgT_ready", 2)
        cmp2_psum = signal("cmp2_psum", 2)
        kc_roped = signal("kc_roped", 1)
        vc_ready = signal("vc_ready", 1)
        kcT_psum = signal("kcT_psum", 1)
        kcT_ready = signal("kcT_ready", 1)
        sb_z = signal("sb_z", 4)
        sb_l = signal("sb_l", 4)
        sb_masked = signal("sb_masked", 4)
        sb_log = signal("sb_log", 4)
        sb_prob = signal("sb_prob", 4)
        sb_pv = signal("sb_pv", 4)
        sb_rows = signal("sb_rows", 1)
        qk = signal("qk", NI)
        maxed = signal("maxed", NI)
        exped = signal("exped", NI)
        scaled = signal("scaled", NI)
        pT_psum = signal("pT_psum", NI)
        pT_act = signal("pT_act", NI // 2)
        pT_dve = signal("pT_dve", NI // 2)
        pv = signal("pv", NI)
        o_rows = signal("o_rows", T)
        out_psum = signal("out_psum", 9)
        xk_ready = signal("xk_ready", 4)
        xv_psum = signal("xv_psum", 3)
        xv_ready = signal("xv_ready", 4)
        xq_psum = signal("xq_psum", 4)
        xq_ready = signal("xq_ready", 8)
        xs = signal("xs", 16)
        xmaxed = signal("xmaxed", 16)
        xexped = signal("xexped", 16)
        xscaled = signal("xscaled", 16)
        xpT_psum = signal("xpT_psum", 16)
        xpT_ready = signal("xpT_ready", 16)
        xo_psum = signal("xo_psum", 8)
        xo_hi = signal("xo_hi", 8)
        xo_lo = signal("xo_lo", 8)
        up_psum = signal("up_psum", 2 * 11)
        conved = signal("conved", NF)
        gelued = signal("gelued", NF)
        gT_done = signal("gT_done", NF)
        g_hi = signal("g_hi", 11)
        g_lo = signal("g_lo", 11)

        made = {}

        def inc(ins, s):
            made[id(s)] = made.get(id(s), 0) + 1
            return ins.then_inc(s.sem, 1)

        def unit_source(l, u):
            if u < U_CMP:
                c, kh = divmod(u, 2)
                return w_in[l].rearrange("(k p) n -> p k n", p=P)[:, 4 * kh:4 * kh + 4, 512 * c:512 * c + IN_W[c]]
            if u < U_OUT:
                w = (cmp_wk1, cmp_wv1)[(u - U_CMP) // 2]
                kh = (u - U_CMP) % 2
                return w[l].rearrange("(k p) n -> p k n", p=P)[:, 8 * kh:8 * kh + 8, :]
            for w, first, last in ((w_out, U_OUT, U_XK), (x_wv, U_XV, U_XQ), (x_wo, U_XO, U_UP), (ffn_w_down, U_DOWN, UNITS)):
                if first <= u < last:
                    k = 2 * (u - first)
                    return w[l].rearrange("(k p) n -> p k n", p=P)[:, k:k + 2, :]
            for w, first, last in ((x_wk, U_XK, U_XV), (x_wq, U_XQ, U_XO)):
                if first <= u < last:
                    m = 256 * (u - first)
                    return w[l].rearrange("(k p) n -> p k n", p=P)[:, :, m:m + 256]
            m = 256 * ((u - U_UP) // 2) + FF * ((u - U_UP) % 2)
            return ffn_w_up[l].rearrange("(k p) n -> p k n", p=P)[:, :, m:m + 256]

        def unit_view(buf, u):
            if u < U_CMP:
                n = IN_W[u // 2]
                return buf[:, u % RING, 0:4 * n].rearrange("p (k n) -> p k n", k=4)
            two = U_OUT <= u < U_XK or U_XV <= u < U_XQ or U_XO <= u < U_UP or u >= U_DOWN
            return buf[:, u % RING, :].rearrange("p (k n) -> p k n", k=2 if two else 8)

        def unit_width(u):
            return 4 * IN_W[u // 2] if u < U_CMP else UW

        def wait_unit(eng, l, u):
            eng.wait_ge(unit_used.sem, unit_used.at(l, u + 1))

        def wait_proj(eng, l, c, t):
            if t < 3:
                eng.wait_ge(proj_psum.sem, proj_psum.at(l, 3 * c + t + 1))
            else:
                wait_unit(eng, l, U_IN + 2 * c + 1)

        def wait_out(eng, l, post, t):
            if t < 3:
                eng.wait_ge(out_psum.sem, out_psum.at(l, 3 * post + t + 1))
            else:
                wait_unit(eng, l, (U_XK, U_UP, UNITS)[post] - 1)

        def wait_xv(eng, l, b):
            if b < 3:
                eng.wait_ge(xv_psum.sem, xv_psum.at(l, b + 1))
            else:
                wait_unit(eng, l, U_XQ - 1)

        def wait_cols(eng, l, done, n, u, m):
            if m == 0:
                eng.wait_ge(done.sem, done.at(l, n + 1))
            else:
                wait_unit(eng, l, u)

        def proj_parts(c, t):
            b = c % 2 * 4 + t
            pairs = proj[:, t, NQ:NQ + 512].rearrange("p (m g d) -> p g m d", g=2, d=HD)
            if c == 1:
                return [(bank(b, 256), proj[:, t, MV:MV + 256]),
                        (bank(b, 256, 256).rearrange("p (m d) -> p m d", d=HD), pairs[:, 0])]
            if c == 2:
                return [(bank(b, 256).rearrange("p (m d) -> p m d", d=HD), pairs[:, 1]),
                        (bank(b, 256, 256).rearrange("p (m d) -> p m d", d=HD).unsqueeze(2).broadcast_to([P, 4, 2, HD]),
                         twice[:, t])]
            return [(bank(b, IN_W[c]), proj[:, t, 512 * c:512 * c + IN_W[c]])]

        block = ctx.enter_context(nc.Block())

        @block.sync
        def _(sp):
            sp.dma_start(h[:], x[0].rearrange("(t p) d -> p t d", p=P)).then_inc(pro_x, 16)
            with sp.Fori(0, DEPTH) as l:
                for u in range(UNITS):
                    sp.wait_ge(lo_made.sem, l * UNITS + (u + 1))
                    sp.dma_start(unit_view(raw, u), unit_source(l, u)).then_inc(raw_landed[u % RING], 16)
            sp.wait_ge(h_done.sem, h_done.at(DEPTH, 0))
            sp.dma_start(out[0].rearrange("(t p) d -> p t d", p=P), h[:]).then_inc(stored, 16)
            sp.wait_ge(stored, 16)

        @block.gpsimd
        def _(pool):
            def link(ins, n):
                ins.then_inc(pro_pool, 1)
                pool.wait_ge(pro_pool, n)
            link(pool.memset(stage[:, 0:4, :], 0.0), 1)
            pool.memset(vec_rows[:], 0.0).then_inc(pro_pool, 1)
            pool.memset(ident[:], 0.0).then_inc(pro_pool, 1)
            pool.memset(strict_mul[:], 1.0).then_inc(pro_pool, 1)
            pool.memset(neg_tri[:], -1.0).then_inc(pro_pool, 1)
            pool.memset(neg_ones[:], -1.0).then_inc(pro_pool, 1)
            pool.memset(kcT[:], 0.0).then_inc(pro_pool, 1)
            link(pool.memset(cmp_valid[:], 1.0), 8)
            pool.affine_select(out=ident[:], in_=ident[:], compare_op=ALU.not_equal, fill=1.0, base=0,
                               pattern=[[-1, P]], channel_multiplier=1).then_inc(pro_pool, 1)
            pool.affine_select(out=stage[:, 1, :], in_=stage[:, 1, :], compare_op=ALU.is_ge, fill=NEG, base=0,
                               pattern=[[-1, P]], channel_multiplier=1).then_inc(pro_pool, 1)
            pool.affine_select(out=stage[:, 2, :], in_=stage[:, 2, :], compare_op=ALU.is_ge, fill=NEG, base=-1,
                               pattern=[[1, P]], channel_multiplier=-1).then_inc(pro_pool, 1)
            pool.affine_select(out=stage[:, 3, :].rearrange("p (t j) -> p t j", t=T),
                               in_=stage[:, 3, :].rearrange("p (t j) -> p t j", t=T),
                               compare_op=ALU.is_ge, fill=NEG, base=-31,
                               pattern=[[P, T], [-16, CMPP]], channel_multiplier=1).then_inc(pro_pool, 1)
            pool.affine_select(out=strict_mul[:], in_=strict_mul[:], compare_op=ALU.is_ge, fill=0.0, base=-1,
                               pattern=[[1, P]], channel_multiplier=-1).then_inc(pro_pool, 1)
            pool.affine_select(out=neg_tri[:], in_=neg_tri[:], compare_op=ALU.is_ge, fill=0.0, base=0,
                               pattern=[[-1, P]], channel_multiplier=1).then_inc(pro_pool, 1)
            link(pool.affine_select(out=cmp_valid[:], in_=cmp_valid[:], compare_op=ALU.is_ge, fill=0.0, base=-31,
                                    pattern=[[P, T]], channel_multiplier=1), 15)
            pool.tensor_copy(ident_r[:], ident[:]).then_inc(pro_pool, 1)
            pool.tensor_copy(causal[:], stage[:, 1, :]).then_inc(pro_pool, 1)
            pool.tensor_copy(strictT[:], stage[:, 2, :]).then_inc(pro_pool, 1)
            pool.tensor_copy(cmp_mask[:].rearrange("p t j -> p (t j)"), stage[:, 3, :]).then_inc(pro_pool, 1)
            pool.wait_ge(pro_pool, 19)
            pool.memset(nt[:, 0:1], 0.0).then_inc(lo_made.sem, RING)
            pool.memset(nt[:, 1:2], 0.0).then_inc(unit_used.sem, RING)
            pool.memset(den[:], 0.0).then_inc(pro_const, 1)
            with pool.Fori(0, DEPTH) as l:
                for u in range(UNITS):
                    n = unit_width(u)
                    pool.wait_ge(hi_made.sem, hi_made.at(l, u + 1))
                    inc(pool.tensor_tensor(w_lo[:, u % RING, 0:n], raw[:, u % RING, 0:n],
                                           w_hi[:, u % RING, 0:n].bitcast(F32), ALU.subtract), lo_made)

        @block.scalar
        def _(act):
            count = [0]

            def link(ins):
                count[0] += 1
                ins.then_inc(act_chain, 1)
                act.wait_ge(act_chain, count[0])

            def rms_estimate(src, junk, c, done):
                link(act.activation(junk, src, ACT.Square, accum_out=sums[:, c:c + 1]))
                link(act.activation(est[:, c:c + 1], sums[:, c:c + 1], ACT.Ln, scale=1.0 / D, bias=eps_t[:]))
                inc(act.activation(est[:, c:c + 1], est[:, c:c + 1], ACT.Exp, scale=-0.5), done)

            act.dma_start(pos_i[:, 0:4], positions.rearrange("b (t p) -> p (b t)", p=P), allow_slow_non_contiguous=True).then_inc(pro_pos, 16)
            act.wait_ge(pro_dve, 1)
            act.dma_start(pos_i[0:NCMP, 4:5],
                          positions[:, 16:S].rearrange("b (j c) -> (b j) c", c=16)[:, 15:16], allow_slow_non_contiguous=True).then_inc(pro_pos, 16)
            act.wait_ge(pro_rope, 1)
            act.activation(sin_t[:].rearrange("p a b -> p (a b)"), ang[:, 0, :], ACT.Sin).then_inc(pro_act, 1)
            act.activation(cos_t[:].rearrange("p a b -> p (a b)"), ang[:, 1, :], ACT.Sin).then_inc(pro_act, 1)
            act.wait_ge(pro_act, 2)
            act.wait_ge(pro_x, 16)
            act.wait_ge(pro_const, 1)

            act.preload_act_table_set("natural_log_exp_and_others")
            with act.Fori(0, DEPTH) as l:
                next_unit = [0]

                def cast_to(n):
                    while next_unit[0] < min(n, UNITS):
                        u = next_unit[0]
                        w = unit_width(u)
                        act.wait_ge(raw_landed[u % RING], l * (16 * UNITS // RING) + 16 * (u // RING + 1))
                        act.wait_ge(unit_used.sem, l * UNITS + (u + 1))
                        inc(act.activation(w_hi[:, u % RING, 0:w], raw[:, u % RING, 0:w], ACT.Copy), hi_made)
                        next_unit[0] += 1

                def hi_parts(inst, gain):
                    for k in range(KD):
                        act.wait_ge(aT_psum.sem, aT_psum.at(l, KD * inst + k + 1))
                        scale = vecs[:, gain + k:gain + k + 1] if gain is not None else 1.0
                        inc(act.activation(a_hi[:, k, :], bank(4 + k % 4), ACT.Copy, scale=scale), aT_hi)

                def post_and_pre(post, pre, casts=(0, 0, 0, 0, 0)):
                    for t in range(T + 1):
                        cast_to(casts[t])
                        if t < T:
                            wait_out(act, l, post, t)
                            rms_estimate(banks[:, 1024 * t:1024 * t + 1024], rows[:, t, :], 12 + T * post + t, post_est)
                        if pre is not None and t:
                            act.wait_ge(h_done.sem, h_done.at(l, T * post + t))
                            rms_estimate(h[:, t - 1, :], rows[:, t - 1, :], T * pre + t - 1, pre_est)

                act.wait_ge(h_done.sem, h_done.at(l, 0))
                g = 0
                for vec in (norm_mix_pre, norm_x_pre, norm_mem, norm_ffn_pre):
                    act.dma_start(vec_a[g:g + 8, :], vec[l].rearrange("(k p) -> k p", p=P)).then_inc(vecs_landed.sem, 16)
                    g += 8
                for vec in (cmp_pe_k, cmp_pe_v):
                    act.dma_start(vec_a[g:g + 16, :], vec[l].rearrange("(q a) d -> q (a d)", a=2)).then_inc(vecs_landed.sem, 16)
                    g += 16
                act.dma_start(vec_b[0:66, :], ffn_conv_w[l].rearrange("w (f p) -> (w f) p", p=P)).then_inc(vecs_landed.sem, 16)
                act.dma_start(vec_b[66:88, :], ffn_conv_b[l].rearrange("(f p) -> f p", p=P)).then_inc(vecs_landed.sem, 16)
                act.dma_start(mem_rows[:], mem[0].rearrange("(t p) d -> p t d", p=P)).then_inc(mem_landed.sem, 16)
                cast_to(2)
                act.wait_ge(vecs_ready.sem, vecs_ready.at(l, 2))
                for t in range(T):
                    rms_estimate(h[:, t, :], rows[:, t, :], t, pre_est)
                hi_parts(0, 0)

                for c in range(6):
                    cast_to(2 * c + 4)
                    for t in (0, 1):
                        wait_proj(act, l, c, t)
                        for src, dst in proj_parts(c, t):
                            ins = act.activation(dst, src, ACT.Copy)
                        inc(ins, proj_act)
                act.wait_ge(proj_act.sem, proj_act.at(l, 12))
                act.wait_ge(proj_dve.sem, proj_dve.at(l, 12))
                inc(act.activation(gates[:], proj[:, :, NG:NG + 24], ACT.Exp, scale=-1.0), gated)
                act.wait_ge(blk_psum.sem, blk_psum.at(l, 4))
                for i, w in enumerate((cmp_wk2, cmp_wv2)):
                    act.dma_start(w2[:, i], w[l].rearrange("(c p) n -> p c n", p=P)).then_inc(w2_landed.sem, 16)

                for b in range(4, 18, 2):
                    act.wait_ge(blk_psum.sem, blk_psum.at(l, b + 1))
                    i = b - 4
                    dst = qT[:, i, :] if i < 8 else kT[:, i - 8, :]
                    inc(act.activation(dst, bank(blk_bank(b)), ACT.Copy, scale=HD ** -0.5 if i < 8 else 1.0), blk_act)
                for i in range(2):
                    cast_to(U_CMP + 2 + 2 * i + 2)
                    wait_unit(act, l, U_CMP + 2 * i + 1)
                    inc(act.activation(cg[0:62, i, :], bank(4 + i, 256, 0, 62), ACT.Gelu_apprx_tanh), cmp_gelu)

                cast_to(U_OUT + 3)
                act.preload_act_table_set("natural_log_exp_and_others")
                act.wait_ge(mem_landed.sem, mem_landed.at(l, 16))
                for t in range(2):
                    if t == 0:
                        act.wait_ge(kcT_ready.sem, kcT_ready.at(l, 1))
                    rms_estimate(mem_rows[:, t, :], rows[:, t, :], 32 + t, mem_est)

                for hh in range(4):
                    act.wait_ge(sb_z.sem, sb_z.at(l, hh + 1))
                    if hh:
                        act.wait_ge(sb_pv.sem, sb_pv.at(l, hh))
                    for k in range(T):
                        ins = act.activation(sb_tmp[:, SB_OFF[k]:SB_OFF[k] + SB_W[k]], bank(k, SB_W[k]), ACT.Abs)
                    link(ins)
                    link(act.activation(sb_tmp[:], sb_tmp[:], ACT.Exp, scale=-1.0))
                    inc(act.activation(sb_tmp[:], sb_tmp[:], ACT.Ln, bias=1.0), sb_l)
                    act.wait_ge(sb_log.sem, sb_log.at(l, hh + 1))
                    for k in range(T):
                        ins = act.activation(sb_tmp[:, SB_OFF[k]:SB_OFF[k] + SB_W[k]], bank(k, SB_W[k]), ACT.Exp)
                    inc(ins, sb_prob)
                act.wait_ge(sb_pv.sem, sb_pv.at(l, 4))
                inc(act.activation(rows[:, :, 768:1024],
                                   banks[:, 6 * 512:8 * 512].rearrange("p (t n) -> p t n", t=T), ACT.Copy), sb_rows)

                def copy_T(i):
                    if i % 2 == 0:
                        n = item_width(i)
                        act.wait_ge(pT_psum.sem, pT_psum.at(l, i + 1))
                        if i >= 3:
                            act.wait_ge(pv.sem, pv.at(l, i - 2))
                        r = item_rows(i)
                        inc(act.activation(probT[0:r, i % 3, 0:n], bank(3 + i % 3, n, 0, r), ACT.Copy), pT_act)

                for i in range(NI + 2):
                    if i < NI:
                        n = item_keys(i)
                        act.wait_ge(maxed.sem, maxed.at(l, i + 1))
                        if i >= 3:
                            act.wait_ge(pT_psum.sem, pT_psum.at(l, i - 2))
                        inc(act.activation(prob[:, i % 3, 0:n], bank(i % 3, n), ACT.Exp,
                                           bias=neg_max[:, i % 8:i % 8 + 1], accum_out=den[:, i % 8:i % 8 + 1]), exped)
                    if i >= 2:
                        copy_T(i - 2)
                hi_parts(1, None)
                act.dma_start(gain_row[:], row_broadcast(norm_mix_post, l)).then_inc(gain_landed[0].sem, 16)
                for k in range(KD):
                    act.wait_ge(mT_psum.sem, mT_psum.at(l, k // 2 * 2 + 2))
                    inc(act.activation(m_hi[:, k, :], bank(k // 2, MEM, k % 2 * MEM), ACT.Copy,
                                       scale=vecs[:, 16 + k:17 + k]), mT_hi)
                cast_to(U_OUT + 5)
                post_and_pre(0, 1, (0, U_XK + 2, U_XK + 2, U_XK + 3, U_XK + 3))
                for u in range(4):
                    cast_to(U_XK + u + 3)
                for u in range(4):
                    cast_to(U_XV + u + 3)
                hi_parts(2, 8)
                act.dma_start(gain_row[:], row_broadcast(norm_x_post, l)).then_inc(gain_landed[1].sem, 16)
                for u in range(4):
                    cast_to(U_XQ + u + 3)
                def copy_xT(i):
                    act.wait_ge(xpT_psum.sem, xpT_psum.at(l, i + 1))
                    if i // 4 >= 2:
                        act.wait_ge(xo_psum.sem, xo_psum.at(l, 2 * (i // 4 - 1)))
                    inc(act.activation(xprobT[:, i // 4 % 2, :, P * (i % 4):P * (i % 4) + P],
                                       bank(2 + i % 2, MEM).rearrange("p (m q) -> p m q", m=2), ACT.Copy), xpT_ready)

                def hi_o(j):
                    act.wait_ge(xo_psum.sem, xo_psum.at(l, j + 1))
                    inc(act.activation(a_hi[:, j, :], bank(4 + j % 4), ACT.Copy), xo_hi)

                for i in range(16):
                    act.wait_ge(xmaxed.sem, xmaxed.at(l, i + 1))
                    if i >= 2:
                        act.wait_ge(xpT_psum.sem, xpT_psum.at(l, i - 1))
                    inc(act.activation(xprob[:, i % 2, :], bank(i % 2, MEM), ACT.Exp,
                                       bias=neg_max[:, i % 8:i % 8 + 1], accum_out=den[:, i % 8:i % 8 + 1]), xexped)
                    if i:
                        copy_xT(i - 1)
                    if i % 4 == 2 and i > 4:
                        hi_o(2 * (i // 4) - 2)
                        hi_o(2 * (i // 4) - 1)
                copy_xT(15)
                hi_o(6)
                hi_o(7)
                act.wait_ge(xo_psum.sem, xo_psum.at(l, 8))
                act.dma_start(gain_row_ffn[:], row_broadcast(norm_ffn_post, l)).then_inc(gain_landed[2].sem, 16)
                cast_to(U_XO + 5)
                post_and_pre(1, 2, (0, U_UP + 2, U_UP + 2, U_UP + 3, U_UP + 3))
                hi_parts(3, 24)

                for f in range(NF):
                    if f % 2 == 0:
                        cast_to(U_UP + f + 4)
                    act.wait_ge(conved.sem, conved.at(l, f + 1))
                    if f >= 3:
                        act.wait_ge(gT_done.sem, gT_done.at(l, f - 2))
                    inc(act.activation(gel[:, f % 3, :], conv[:, f % 3, :], ACT.Gelu_apprx_tanh,
                                       bias=vecs[:, 130 + f:131 + f]), gelued)
                act.preload_act_table_set("natural_log_exp_and_others")
                for i in range(11):
                    act.wait_ge(gT_done.sem, gT_done.at(l, 2 * i + 2))
                    act.wait_ge(unit_used.sem, unit_used.at(l, U_DOWN if i < 4 else U_DOWN + i - 3))
                    inc(act.activation(a_hi[:, 2 * i % 8:2 * i % 8 + 2, :], gT[:, 2 * i:2 * i + 2, :], ACT.Copy), g_hi)
                    cast_to(U_DOWN + i + 3)
                post_and_pre(2, None)
                act.sem_clear(act_chain)
                count[0] = 0

        @block.vector
        def _(dve):
            count = [0]

            def link(ins):
                count[0] += 1
                ins.then_inc(dve_chain, 1)
                dve.wait_ge(dve_chain, count[0])

            dve.memset(eps_t[:], EPS)
            dve.memset(pos_i[:, 4:5], 0).then_inc(pro_dve, 1)
            dve.wait_ge(pro_pos, 32)
            link(dve.tensor_copy(pos_f[:], pos_i[:]))
            for j in range(8):
                freq = float(np.float32(500000.0) ** np.float32(-j / 8))
                ins = dve.tensor_scalar(ang[:, 0, :].rearrange("p (t j) -> p t j", j=8)[:, :, j], pos_f[:], freq, None, ALU.mult)
            link(ins)
            link(dve.tensor_copy(ang[:, 1, :], ang[:, 0, :]))
            inv = float(1 / (2 * np.pi))
            link(dve.tensor_scalar(turns[:, 0, :], ang[:, 0, :], inv, None, ALU.mult))
            link(dve.tensor_scalar(turns[:, 1, :], ang[:, 0, :], inv, 0.25, ALU.mult, ALU.add))
            big = 12582912.0
            link(dve.tensor_scalar(turns[:], turns[:], big, None, ALU.add))
            link(dve.tensor_scalar(turns[:], turns[:], big, None, ALU.subtract))
            c1 = 6.28125
            c2 = float(np.float32(round((2 * np.pi - c1) * 2 ** 19) / 2 ** 19))
            c3 = float(2 * np.pi - c1 - c2)
            for c in (c1, c2, c3):
                link(dve.scalar_tensor_tensor(ang[:], turns[:], -c, ang[:], ALU.mult, ALU.add))
            link(dve.tensor_scalar(ang[:, 1, :], ang[:, 1, :], float(np.pi / 2), None, ALU.add))
            dve.tensor_scalar(ang[:], ang[:], 3.1415925, -3.1415925, ALU.min, ALU.max).then_inc(pro_rope, 1)
            dve.wait_ge(pro_act, 2)
            dve.wait_ge(pro_x, 16)
            dve.wait_ge(pro_const, 1)

            def newton(c):
                link(dve.tensor_scalar(sums[:, c:c + 1], sums[:, c:c + 1], -0.5 / D, -0.5 * EPS, ALU.mult, ALU.add))
                link(dve.scalar_tensor_tensor(rstd[:, c:c + 1], est[:, c:c + 1], sums[:, c:c + 1], est[:, c:c + 1], ALU.mult, ALU.mult))
                link(dve.scalar_tensor_tensor(rstd[:, c:c + 1], rstd[:, c:c + 1], 1.5, est[:, c:c + 1], ALU.add, ALU.mult))

            def rope(dst, cs, sn, tmp):
                x1, x2 = dst[..., 0:8], dst[..., 8:16]
                dve.tensor_tensor(tmp[0], x1, cs, ALU.mult)
                dve.tensor_tensor(tmp[1], x2, sn, ALU.mult)
                dve.tensor_tensor(tmp[2], x2, cs, ALU.mult)
                link(dve.tensor_tensor(tmp[3], x1, sn, ALU.mult))
                dve.tensor_tensor(x1, tmp[0], tmp[1], ALU.subtract)
                return dve.tensor_tensor(x2, tmp[2], tmp[3], ALU.add)

            dve.sem_clear(dve_chain)
            count[0] = 0
            dve.memset(sums[:], 0.0).then_inc(h_done.sem, 1)
            with dve.Fori(0, DEPTH) as l:
                for i, (v, n) in enumerate(((vec_a, 64), (vec_b, 88))):
                    dve.wait_ge(vecs_T.sem, vecs_T.at(l, i + 1))
                    inc(dve.tensor_copy(vecs[:, 64 * i:64 * i + n], bank(i, n)), vecs_ready)

                def pre_norm(pre, t):
                    dve.wait_ge(pre_est.sem, pre_est.at(l, T * pre + t + 1))
                    newton(T * pre + t)
                    inc(dve.tensor_scalar(rows[:, t, :], h[:, t, :], rstd[:, T * pre + t:T * pre + t + 1], None, ALU.mult), rows_done)

                def lo_parts(inst, gain):
                    for k in range(KD):
                        dve.wait_ge(aT_hi.sem, aT_hi.at(l, KD * inst + k + 1))
                        if gain is None:
                            ins = dve.tensor_tensor(a_lo[:, k, :], bank(4 + k % 4), a_hi[:, k, :].bitcast(F32), ALU.subtract)
                        else:
                            ins = dve.scalar_tensor_tensor(a_lo[:, k, :], bank(4 + k % 4), vecs[:, gain + k:gain + k + 1],
                                                           a_hi[:, k, :].bitcast(F32), ALU.mult, ALU.subtract)
                        inc(ins, aT_lo)

                def post_and_pre(post, pre, gain):
                    dve.wait_ge(gain_landed[post].sem, gain_landed[post].at(l, 16))
                    for t in range(T + 1):
                        if t < T:
                            c = 12 + T * post + t
                            dve.wait_ge(post_est.sem, post_est.at(l, T * post + t + 1))
                            newton(c)
                            link(dve.scalar_tensor_tensor(rows[:, t, :], banks[:, 1024 * t:1024 * t + 1024], rstd[:, c:c + 1],
                                                          gain[:], ALU.mult, ALU.mult))
                            inc(dve.tensor_tensor(h[:, t, :], h[:, t, :], rows[:, t, :], ALU.add), h_done)
                        if pre is not None and t:
                            pre_norm(pre, t - 1)

                for t in range(T):
                    pre_norm(0, t)
                lo_parts(0, 0)

                def rope_heads(col, n, table_heads):
                    dve.wait_ge(proj_act.sem, proj_act.at(l, 2 * ((col + 64 * n - 1) // 512) + 2))
                    dst = proj[:, :, col:col + 64 * n].rearrange("p t (m d) -> p t m d", d=HD)
                    shape = [P, T, n, 8]
                    cs = cos_t[:, 0:4, :].unsqueeze(2).broadcast_to(shape)
                    sn = sin_t[:, 0:4, :].unsqueeze(2).broadcast_to(shape)
                    tmp = [rope_tmp[:, i, 0:T * n * 8].rearrange("p (t m d) -> p t m d", t=T, d=8) for i in range(4)]
                    inc(rope(dst, cs, sn, tmp), roped)
                    dve.wait_ge(roped.sem, roped.at(l, table_heads))

                for c in range(6):
                    for t in (2, 3):
                        wait_proj(dve, l, c, t)
                        for src, dst in proj_parts(c, t):
                            ins = dve.tensor_copy(dst, src)
                        inc(ins, proj_dve)
                    dve.wait_ge(proj_dve.sem, proj_dve.at(l, 2 * c + 2))
                    if c == 0:
                        rope_heads(MQ, 8, 1)
                    if c == 2:
                        rope_heads(NQ, 8, 2)
                    if c == 3:
                        rope_heads(NKS, 2, 3)
                        rope_heads(NKW, 2, 4)
                dve.wait_ge(gated.sem, gated.at(l, 1))
                link(dve.tensor_scalar(gates[:], gates[:], 1.0, None, ALU.add))
                link(dve.reciprocal(gates[:], gates[:]))

                for i in range(2):
                    dve.wait_ge(blk_psum.sem, blk_psum.at(l, 4))
                    if i:
                        wait_unit(dve, l, U_CMP + 1)
                    for g in range(2):
                        for a in range(2):
                            pp = slice(64 * a, 64 * a + 64)
                            src = banks[pp, 512 * (2 * i + g):512 * (2 * i + g) + 512].rearrange("p (j r) -> p r j", r=16)
                            dst = xb[pp, :].rearrange("p (q g j) -> p q g j", q=16, g=2)
                            for half in range(2):
                                q = slice(8 * half, 8 * half + 8)
                                pe = vecs[pp, 32 + 16 * i + 8 * half:40 + 16 * i + 8 * half].unsqueeze(2).broadcast_to([64, 8, NCMP])
                                ins = dve.tensor_tensor(dst[:, q, g, :], src[:, a:16:2, half:half + NCMP], pe, ALU.add)
                    link(ins)
                    link(dve.tensor_copy(xb_hi[:], xb[:]))
                    inc(dve.tensor_tensor(xb_lo[:], xb[:], xb_hi[:].bitcast(F32), ALU.subtract), xb_ready)
                    if i == 0:
                        for b in range(5, 18, 2):
                            dve.wait_ge(blk_psum.sem, blk_psum.at(l, b + 1))
                            j = b - 4
                            if j < 8:
                                inc(dve.tensor_scalar(qT[:, j, :], bank(blk_bank(b)), HD ** -0.5, None, ALU.mult), blk_dve)
                            else:
                                inc(dve.tensor_copy(kT[:, j - 8, :], bank(blk_bank(b))), blk_dve)
                for i in range(2):
                    dve.wait_ge(cgT_psum.sem, cgT_psum.at(l, i + 1))
                    if i:
                        dve.wait_ge(cmp2_psum.sem, cmp2_psum.at(l, 1))
                    inc(dve.tensor_copy(cgT[:], bank(6, 256).rearrange("p (c j) -> p c j", c=2)[:, :, 0:62]), cgT_ready)
                    dve.wait_ge(cmp2_psum.sem, cmp2_psum.at(l, i + 1))
                    src = bank(7, 128, 0, NCMP).rearrange("p (g d) -> p g d", g=2)
                    if i == 0:
                        link(dve.tensor_copy(kc_rows[0:NCMP], src))
                        shape = [NCMP, 2, 8]
                        cs = cos_t[0:NCMP, 4:5, :].broadcast_to(shape)
                        sn = sin_t[0:NCMP, 4:5, :].broadcast_to(shape)
                        tmp = [rope_tmp2[0:NCMP, i, :].rearrange("p (g d) -> p g d", g=2) for i in range(4)]
                        inc(rope(kc_rows[0:NCMP], cs, sn, tmp), kc_roped)
                    else:
                        inc(dve.tensor_copy(vc_rows[0:NCMP], src), vc_ready)
                dve.wait_ge(kcT_psum.sem, kcT_psum.at(l, 1))
                inc(dve.tensor_copy(kcT[:, 0:NCMP], bank(6, NCMP)), kcT_ready)

                for t in range(2):
                    dve.wait_ge(mem_est.sem, mem_est.at(l, t + 1))
                    newton(32 + t)
                    inc(dve.tensor_scalar(mem_rows[:, t, :], mem_rows[:, t, :], rstd[:, 32 + t:33 + t], None, ALU.mult), mem_normed)

                for hh in range(4):
                    dve.wait_ge(sb_l.sem, sb_l.at(l, hh + 1))
                    for k in range(T):
                        s = slice(SB_OFF[k], SB_OFF[k] + SB_W[k])
                        ins = dve.scalar_tensor_tensor(sb_sp[:, s], bank(k, SB_W[k]), 0.0, sb_tmp[:, s], ALU.max, ALU.add)
                    link(ins)
                    for k in range(T):
                        s = slice(SB_OFF[k], SB_OFF[k] + P)
                        ins = dve.tensor_tensor(sb_sp[:, s], sb_sp[:, s], strict_mul[:], ALU.mult)
                    inc(ins, sb_masked)

                def scale(i):
                    t, (head, kind) = i // len(ITEMS), ITEMS[i % len(ITEMS)]
                    n = item_keys(i)
                    dve.wait_ge(exped.sem, exped.at(l, i + 1))
                    link(dve.reciprocal(rden[:, i % 8:i % 8 + 1], den[:, i % 8:i % 8 + 1]))
                    r = rden[:, i % 8:i % 8 + 1]
                    if kind == "moba":
                        ins = dve.tensor_scalar(prob[:, i % 3, 0:n], prob[:, i % 3, 0:n], r, None, ALU.mult)
                    else:
                        c = 3 * (head - 4) + ("cmp", "sel", "win").index(kind)
                        if kind == "cmp":
                            link(dve.tensor_tensor(r, r, cmp_valid[:, t:t + 1], ALU.mult))
                        ins = dve.tensor_scalar(prob[:, i % 3, 0:n], prob[:, i % 3, 0:n], r, gates[:, t, c:c + 1], ALU.mult, ALU.mult)
                    inc(ins, scaled)

                def copy_T(i):
                    if i % 2:
                        n, r = item_width(i), item_rows(i)
                        dve.wait_ge(pT_psum.sem, pT_psum.at(l, i + 1))
                        if i >= 3:
                            dve.wait_ge(pv.sem, pv.at(l, i - 2))
                        inc(dve.tensor_copy(probT[0:r, i % 3, 0:n], bank(3 + i % 3, n, 0, r)), pT_dve)

                def o_copy(t):
                    dve.wait_ge(pv.sem, pv.at(l, len(ITEMS) * (t + 1)))
                    inc(dve.tensor_copy(rows[:, t, 0:768], banks[:, 6 * 512:6 * 512 + 768]), o_rows)

                for i in range(NI + 3):
                    if i < NI:
                        dve.wait_ge(qk.sem, qk.at(l, i + 1))
                        inc(dve.tensor_reduce(neg_max[:, i % 8:i % 8 + 1], bank(i % 3, item_keys(i)), AX.X, ALU.max, negate=True), maxed)
                    if 1 <= i <= NI:
                        scale(i - 1)
                    if 2 <= i <= NI + 1:
                        copy_T(i - 2)
                    if i >= 3 and (i - 2) % len(ITEMS) == 0:
                        o_copy((i - 2) // len(ITEMS) - 1)
                lo_parts(1, None)
                for k in range(KD):
                    dve.wait_ge(mT_hi.sem, mT_hi.at(l, k // 2 * 2 + 2))
                    inc(dve.scalar_tensor_tensor(m_lo[:, k, :], bank(k // 2, MEM, k % 2 * MEM), vecs[:, 16 + k:17 + k],
                                                 m_hi[:, k, :].bitcast(F32), ALU.mult, ALU.subtract), mT_lo)
                post_and_pre(0, 1, gain_row)

                for u in range(4):
                    wait_unit(dve, l, U_XK + u)
                    inc(dve.tensor_copy(xkT[:, 2 * u:2 * u + 2, :].rearrange("p a m -> p (a m)"), bank(u)), xk_ready)
                for b in range(4):
                    wait_xv(dve, l, b)
                    inc(dve.tensor_copy(xv[:, b // 2, 512 * (b % 2):512 * (b % 2) + 512], bank(4 + b)), xv_ready)
                lo_parts(2, 8)
                for m in range(KD):
                    wait_cols(dve, l, xq_psum, m // 2, U_XQ + m // 2, m % 2)
                    inc(dve.tensor_scalar(xqT[:, m, :], bank(m % 4), 256 ** -0.5, None, ALU.mult), xq_ready)

                def xscale(i):
                    dve.wait_ge(xexped.sem, xexped.at(l, i + 1))
                    r = rden[:, i % 8:i % 8 + 1]
                    link(dve.reciprocal(r, den[:, i % 8:i % 8 + 1]))
                    inc(dve.tensor_scalar(xprob[:, i % 2, :], xprob[:, i % 2, :], r, None, ALU.mult), xscaled)

                def lo_o(j):
                    dve.wait_ge(xo_hi.sem, xo_hi.at(l, j + 1))
                    inc(dve.tensor_tensor(a_lo[:, j, :], bank(4 + j % 4), a_hi[:, j, :].bitcast(F32), ALU.subtract), xo_lo)

                for i in range(17):
                    if i < 16:
                        dve.wait_ge(xs.sem, xs.at(l, i + 1))
                        inc(dve.tensor_reduce(neg_max[:, i % 8:i % 8 + 1], bank(i % 2, MEM), AX.X, ALU.max, negate=True), xmaxed)
                    if i:
                        xscale(i - 1)
                    if i % 4 == 3 and i > 4:
                        lo_o(2 * (i // 4) - 2)
                        lo_o(2 * (i // 4) - 1)
                lo_o(6)
                lo_o(7)
                post_and_pre(1, 2, gain_row)
                lo_parts(3, 24)

                def gate(f):
                    dve.wait_ge(gelued.sem, gelued.at(l, f + 1))
                    jp, b = divmod(f, 2)
                    wait_cols(dve, l, up_psum, 2 * jp + 1, U_UP + 2 * jp + 1, b)
                    inc(dve.tensor_tensor(gT[:, f, :], gel[:, f % 3, :], bank(jp % 2 * 4 + 2 + b), ALU.mult), gT_done)

                for f in range(NF + 1):
                    if f < NF:
                        jp, b = divmod(f, 2)
                        src = banks[:, 512 * (jp % 2 * 4 + b):512 * (jp % 2 * 4 + b) + 512]
                        cv = conv[:, f % 3, :]
                        wait_cols(dve, l, up_psum, 2 * jp, U_UP + 2 * jp, b)
                        if f >= 3:
                            dve.wait_ge(gelued.sem, gelued.at(l, f - 2))
                        wcol = lambda i: vecs[:, 64 + 22 * i + f:65 + 22 * i + f]
                        link(dve.tensor_scalar(cv, src, wcol(2), None, ALU.mult))
                        link(dve.scalar_tensor_tensor(cv[:, 1:S], src[:, 0:S - 1], wcol(1), cv[:, 1:S], ALU.mult, ALU.add))
                        inc(dve.scalar_tensor_tensor(cv[:, 2:S], src[:, 0:S - 2], wcol(0), cv[:, 2:S], ALU.mult, ALU.add), conved)
                    if f:
                        gate(f - 1)
                for i in range(11):
                    dve.wait_ge(g_hi.sem, g_hi.at(l, i + 1))
                    inc(dve.tensor_tensor(a_lo[:, 2 * i % 8:2 * i % 8 + 2, :], gT[:, 2 * i:2 * i + 2, :],
                                          a_hi[:, 2 * i % 8:2 * i % 8 + 2, :].bitcast(F32), ALU.subtract), g_lo)
                post_and_pre(2, None, gain_row_ffn)
                dve.sem_clear(dve_chain)
                count[0] = 0

        @block.tensor
        def _(pe):
            pe.wait_ge(pro_const, 1)

            def three(dst, st_hi, st_lo, mv_hi, mv_lo, first, last):
                pe.matmul(dst, st_lo, mv_hi, start=first, stop=False)
                pe.matmul(dst, st_hi, mv_lo, start=False, stop=False)
                return pe.matmul(dst, st_hi, mv_hi, start=False, stop=last)

            with pe.Fori(0, DEPTH) as l:
                def unit(u):
                    pe.wait_ge(lo_made.sem, lo_made.at(l, u + 1))
                    return unit_view(w_hi, u), unit_view(w_lo, u)

                def transpose_rows(inst):
                    for k in range(KD):
                        if k >= 4:
                            pe.wait_ge(aT_lo.sem, aT_lo.at(l, KD * inst + k - 3))
                        for t in range(T):
                            ins = pe.transpose(bank(4 + k % 4, P, P * t), rows[:, t, P * k:P * k + P], ident[:])
                        inc(ins, aT_psum)

                def rows_gemm(first, n_units, post, ready):
                    for i in range(n_units):
                        hi, lo = unit(first + i)
                        ready(i)
                        for t in range(T):
                            for n in range(2):
                                for k in range(2):
                                    a = (2 * i + k) % KD
                                    st = slice(P * t, P * t + P)
                                    ins = three(bank(2 * t + n), a_hi[:, a, st], a_lo[:, a, st],
                                                hi[:, k, 512 * n:512 * n + 512], lo[:, k, 512 * n:512 * n + 512],
                                                i == 0 and k == 0, i == n_units - 1 and k == 1)
                            if i == n_units - 1 and t < T - 1:
                                inc(ins, out_psum)
                        inc(ins, unit_used)

                pe.wait_ge(vecs_landed.sem, vecs_landed.at(l, 128))
                pe.wait_ge(h_done.sem, h_done.at(l, 0))
                for i, (v, n) in enumerate(((vec_a, 64), (vec_b, 88))):
                    inc(pe.transpose(bank(i, P), v, ident[:]), vecs_T)

                pe.wait_ge(rows_done.sem, rows_done.at(l, 4))
                transpose_rows(0)
                for c in range(6):
                    for kh in range(2):
                        u = U_IN + 2 * c + kh
                        hi, lo = unit(u)
                        for t in range(T):
                            if c >= 2 and kh == 0:
                                done = proj_act if t < 2 else proj_dve
                                pe.wait_ge(done.sem, done.at(l, 2 * (c - 2) + t % 2 + 1))
                            for k in range(4):
                                if c == 0 and t == 0 or c == 1 and kh == 0 and t == 0 and k == 0:
                                    pe.wait_ge(aT_lo.sem, aT_lo.at(l, 4 * kh + k + 1 if c == 0 else KD))
                                a = 4 * kh + k
                                st = slice(P * t, P * t + P)
                                ins = three(bank(c % 2 * 4 + t, IN_W[c]), a_hi[:, a, st], a_lo[:, a, st],
                                            hi[:, k, :], lo[:, k, :], kh == 0 and k == 0, kh == 1 and k == 3)
                            if kh == 1 and t < 3:
                                inc(ins, proj_psum)
                        inc(ins, unit_used)

                pe.wait_ge(proj_act.sem, proj_act.at(l, 12))
                pe.wait_ge(proj_dve.sem, proj_dve.at(l, 12))
                pe.wait_ge(roped.sem, roped.at(l, 4))
                pairs_q = [MQ, MQ + P, NQ, NQ + P, NQ + 2 * P, NQ + 3 * P, SQ, SQ + P]
                pairs_k = [MK, MK + P, SK, SK + P]
                for b, col in enumerate([None] * 4 + pairs_q + pairs_k + [NKS, NKW]):
                    if b == 8:
                        pe.wait_ge(xb_ready.sem, xb_ready.at(l, 1))
                    if b >= 10:
                        done = blk_act if b % 2 == 0 else blk_dve
                        pe.wait_ge(done.sem, done.at(l, (b - 10) // 2 + 1))
                    for t in range(T):
                        src = twice[:, t, b].rearrange("p a d -> p (a d)") if b < 4 else proj[:, t, col:col + P]
                        ins = pe.transpose(bank(blk_bank(b), P, P * t), src, ident[:])
                    inc(ins, blk_psum)

                pe.wait_ge(blk_act.sem, blk_act.at(l, 7))
                pe.wait_ge(blk_dve.sem, blk_dve.at(l, 7))
                for i in range(2):
                    pe.wait_ge(xb_ready.sem, xb_ready.at(l, i + 1))
                    for kh in range(2):
                        u = U_CMP + 2 * i + kh
                        hi, lo = unit(u)
                        for k in range(8):
                            q = 8 * kh + k
                            st = slice(62 * q, 62 * q + 62)
                            ins = three(bank(4 + i, 256, 0, 62), xb_hi[:, st], xb_lo[:, st], hi[:, k, :], lo[:, k, :],
                                        q == 0, q == 15)
                        inc(ins, unit_used)
                pe.wait_ge(w2_landed.sem, w2_landed.at(l, 32))
                for i in range(2):
                    pe.wait_ge(cmp_gelu.sem, cmp_gelu.at(l, i + 1))
                    if i:
                        pe.wait_ge(cgT_ready.sem, cgT_ready.at(l, 1))
                    for c in range(2):
                        ins = pe.transpose(bank(6, P, P * c), cg[:, i, P * c:P * c + P], ident[:])
                    inc(ins, cgT_psum)
                    pe.wait_ge(cgT_ready.sem, cgT_ready.at(l, i + 1))
                    if i:
                        pe.wait_ge(kc_roped.sem, kc_roped.at(l, 1))
                    for g in range(2):
                        for c in range(2):
                            ins = pe.matmul(bank(7, HD, HD * g, NCMP), cgT[:, c, NCMP * g:NCMP * g + NCMP], w2[:, i, c, :],
                                            start=c == 0, stop=c == 1)
                    inc(ins, cmp2_psum)
                inc(pe.transpose(bank(6, NCMP), kc_rows[0:NCMP].rearrange("p g d -> p (g d)"), ident[0:NCMP, 0:NCMP]), kcT_psum)
                pe.wait_ge(vc_ready.sem, vc_ready.at(l, 1))
                pe.wait_ge(kcT_ready.sem, kcT_ready.at(l, 1))

                for hh in range(4):
                    b0, pair = 64 * (hh % 2), hh // 2
                    if hh:
                        pe.wait_ge(sb_prob.sem, sb_prob.at(l, hh))
                    for k in range(T):
                        ins = pe.matmul(bank(k, SB_W[k]), kT[b0:b0 + HD, 2 + pair, P * k:P * k + P],
                                        qT[b0:b0 + HD, 6 + pair, P * k:S], start=True, stop=True)
                    inc(ins, sb_z)
                    pe.wait_ge(sb_masked.sem, sb_masked.at(l, hh + 1))
                    for k in range(T):
                        pe.matmul(bank(k, P), ident_r[:], strictT[:], start=False, stop=False, skip_group_check=True)
                        ins = pe.matmul(bank(k, SB_W[k]), neg_tri[:], sb_sp[:, SB_OFF[k]:SB_OFF[k] + SB_W[k]],
                                        start=False, stop=False, skip_group_check=True)
                        for j in range(k + 1, T):
                            ins = pe.matmul(bank(k, SB_W[j], P * (j - k)), neg_ones[:], sb_sp[:, SB_OFF[j]:SB_OFF[j] + SB_W[j]],
                                            start=False, stop=False, skip_group_check=True)
                    inc(ins, sb_log)
                    pe.wait_ge(sb_prob.sem, sb_prob.at(l, hh + 1))
                    for t in range(T):
                        for k in range(t + 1):
                            at = SB_OFF[k] + P * (t - k)
                            ins = pe.matmul(banks[:, 6 * 512 + 256 * t + HD * hh:6 * 512 + 256 * t + HD * hh + HD],
                                            sb_tmp[:, at:at + P], proj[:, k, SV + HD * hh:SV + HD * hh + HD],
                                            start=k == 0, stop=k == t)
                    inc(ins, sb_pv)

                pe.wait_ge(sb_rows.sem, sb_rows.at(l, 1))

                def scores(i):
                    t, (head, kind) = i // len(ITEMS), ITEMS[i % len(ITEMS)]
                    g = (head - 4) // 4
                    b0, pair = (HD * (head % 2), head // 2) if kind == "moba" else (HD * g, 2 + (head - 4) % 4)
                    n = item_keys(i)
                    if i >= 3:
                        pe.wait_ge(exped.sem, exped.at(l, i - 2))
                    keys = {"moba": lambda: kT[b0:b0 + HD, head // 2, 0:n], "sel": lambda: kT[b0:b0 + HD, 4, 0:n],
                            "win": lambda: kT[b0:b0 + HD, 5, 0:n], "cmp": lambda: kcT[b0:b0 + HD, :]}[kind]()
                    pe.matmul(bank(i % 3, n), qT[b0:b0 + HD, pair, P * t:P * t + P], keys, start=True, stop=False)
                    if kind == "cmp":
                        inc(pe.matmul(bank(i % 3, CMPP), ident_r[:], cmp_mask[:, t, :], start=False, stop=True), qk)
                    else:
                        inc(pe.matmul(bank(i % 3, P, n - P), ident_r[:], causal[:], start=False, stop=True), qk)

                def transposes(i):
                    t, (head, kind) = i // len(ITEMS), ITEMS[i % len(ITEMS)]
                    pe.wait_ge(scaled.sem, scaled.at(l, i + 1))
                    if i >= 3:
                        j = i - 3
                        done = pT_dve if j % 2 else pT_act
                        pe.wait_ge(done.sem, done.at(l, j // 2 + 1))
                    if kind == "cmp":
                        ins = pe.transpose(bank(3 + i % 3, P, 0, CMPP), prob[:, i % 3, 0:CMPP], ident[:])
                    else:
                        for k in range(t + 1):
                            ins = pe.transpose(bank(3 + i % 3, P, P * k), prob[:, i % 3, P * k:P * k + P], ident[:])
                    inc(ins, pT_psum)

                def values(i):
                    t, (head, kind) = i // len(ITEMS), ITEMS[i % len(ITEMS)]
                    g = (head - 4) // 4
                    done = pT_dve if i % 2 else pT_act
                    pe.wait_ge(done.sem, done.at(l, i // 2 + 1))
                    if i % len(ITEMS) == 0 and t:
                        pe.wait_ge(o_rows.sem, o_rows.at(l, t))
                    dst = banks[:, 6 * 512 + HD * head:6 * 512 + HD * head + HD]
                    if kind == "cmp":
                        ins = pe.matmul(dst, probT[0:NCMP, i % 3, 0:P], vc_rows[0:NCMP, g, :], start=True, stop=False)
                    else:
                        col = {"moba": MV + HD * head, "sel": NVS + HD * g, "win": NVW + HD * g}[kind]
                        for k in range(t + 1):
                            ins = pe.matmul(dst, probT[:, i % 3, P * k:P * k + P], proj[:, k, col:col + HD],
                                            start=kind == "moba" and k == 0, stop=kind in ("moba", "win") and k == t)
                    inc(ins, pv)

                for i in range(NI + 3):
                    if i < NI:
                        scores(i)
                    if 2 <= i < NI + 2:
                        transposes(i - 2)
                    if i >= 3:
                        values(i - 3)

                pe.wait_ge(o_rows.sem, o_rows.at(l, T))
                transpose_rows(1)
                pe.wait_ge(mem_normed.sem, mem_normed.at(l, 2))
                for k in range(KD):
                    for t in range(2):
                        ins = pe.transpose(bank(k // 2, P, k % 2 * MEM + P * t), mem_rows[:, t, P * k:P * k + P], ident[:])
                    inc(ins, mT_psum)
                pe.wait_ge(mT_lo.sem, mT_lo.at(l, KD))
                rows_gemm(U_OUT, 4, 0, lambda i: pe.wait_ge(aT_lo.sem, aT_lo.at(l, 16)) if i == 0 else None)

                for u in range(4):
                    pe.wait_ge(h_done.sem, h_done.at(l, u // 2 + 1))
                    hi, lo = unit(U_XK + u)
                    for m in range(2):
                        for k in range(KD):
                            mm = slice(P * m, P * m + P)
                            ins = three(bank(u, MEM, MEM * m), hi[:, k, mm], lo[:, k, mm], m_hi[:, k, :], m_lo[:, k, :], k == 0, k == KD - 1)
                    inc(ins, unit_used)
                pe.wait_ge(h_done.sem, h_done.at(l, 4))
                for u in range(4):
                    hi, lo = unit(U_XV + u)
                    for t in range(2):
                        for n in range(2):
                            for k in range(2):
                                a, st, nn = 2 * u + k, slice(P * t, P * t + P), slice(512 * n, 512 * n + 512)
                                ins = three(bank(4 + 2 * t + n), m_hi[:, a, st], m_lo[:, a, st], hi[:, k, nn], lo[:, k, nn],
                                            u == 0 and k == 0, u == 3 and k == 1)
                            if u == 3 and 2 * t + n < 3:
                                inc(ins, xv_psum)
                    inc(ins, unit_used)
                pe.wait_ge(rows_done.sem, rows_done.at(l, 8))
                pe.wait_ge(xv_ready.sem, xv_ready.at(l, 4))
                transpose_rows(2)

                def cols_gemm(u, b, done):
                    hi, lo = unit(u)
                    for m in range(2):
                        for k in range(KD):
                            mm = slice(P * m, P * m + P)
                            ins = three(bank(b + m), hi[:, k, mm], lo[:, k, mm], a_hi[:, k, :], a_lo[:, k, :], k == 0, k == KD - 1)
                        inc(ins, (done, unit_used)[m])

                pe.wait_ge(aT_lo.sem, aT_lo.at(l, 24))
                pe.wait_ge(xk_ready.sem, xk_ready.at(l, 4))
                for u in range(4):
                    if u >= 2:
                        pe.wait_ge(xq_ready.sem, xq_ready.at(l, 2 * (u - 2) + 2))
                    cols_gemm(U_XQ + u, 2 * (u % 2), xq_psum)
                pe.wait_ge(xq_ready.sem, xq_ready.at(l, 8))

                def xscores(i):
                    head, t = divmod(i, 4)
                    if i >= 2:
                        pe.wait_ge(xexped.sem, xexped.at(l, i - 1))
                    for c in range(2):
                        ins = pe.matmul(bank(i % 2, MEM), xqT[:, 2 * head + c, P * t:P * t + P], xkT[:, 2 * head + c, :],
                                        start=c == 0, stop=c == 1)
                    inc(ins, xs)

                def xtransposes(i):
                    pe.wait_ge(xscaled.sem, xscaled.at(l, i + 1))
                    if i >= 2:
                        pe.wait_ge(xpT_ready.sem, xpT_ready.at(l, i - 1))
                    for m in range(2):
                        ins = pe.transpose(bank(2 + i % 2, P, P * m), xprob[:, i % 2, P * m:P * m + P], ident[:])
                    inc(ins, xpT_psum)

                def xvalues(head):
                    pe.wait_ge(xpT_ready.sem, xpT_ready.at(l, 4 * head + 4))
                    for d in range(2):
                        j = 2 * head + d
                        if j >= 4:
                            pe.wait_ge(xo_lo.sem, xo_lo.at(l, j - 3))
                        for m in range(2):
                            ins = pe.matmul(bank(4 + j % 4), xv[:, m, P * j:P * j + P], xprobT[:, head % 2, m, :],
                                            start=m == 0, stop=m == 1)
                        inc(ins, xo_psum)

                for i in range(17):
                    if i < 16:
                        xscores(i)
                    if i:
                        xtransposes(i - 1)
                    if i % 4 == 1 and i > 4:
                        xvalues(i // 4 - 1)
                xvalues(3)
                pe.wait_ge(xo_lo.sem, xo_lo.at(l, 8))
                rows_gemm(U_XO, 4, 1, lambda i: None)

                pe.wait_ge(rows_done.sem, rows_done.at(l, 12))
                transpose_rows(3)
                pe.wait_ge(aT_lo.sem, aT_lo.at(l, 32))
                for jp in range(11):
                    if jp >= 2:
                        pe.wait_ge(gT_done.sem, gT_done.at(l, 2 * (jp - 2) + 2))
                    cols_gemm(U_UP + 2 * jp, jp % 2 * 4, up_psum)
                    cols_gemm(U_UP + 2 * jp + 1, jp % 2 * 4 + 2, up_psum)
                pe.wait_ge(gT_done.sem, gT_done.at(l, NF))
                rows_gemm(U_DOWN, 11, 2, lambda i: pe.wait_ge(g_lo.sem, g_lo.at(l, i + 1)))


            for s in signals.values():
                if id(s) in made:
                    assert made[id(s)] == s.per_layer, [n for n in signals if signals[n] is s] + [made[id(s)]]


_INS = ["x", "mem", "positions", "norm_mix_pre", "norm_mix_post", "w_in", "w_out", "cmp_pe_k", "cmp_pe_v",
        "cmp_wk1", "cmp_wk2", "cmp_wv1", "cmp_wv2", "norm_x_pre", "norm_x_post", "norm_mem",
        "x_wq", "x_wk", "x_wv", "x_wo", "norm_ffn_pre", "norm_ffn_post", "ffn_w_up", "ffn_conv_w",
        "ffn_conv_b", "ffn_w_down"]


def kernel(**inputs):
    import concourse.bacc as bacc
    from concourse.bass_utils import run_bass_kernel_spmd

    nc = bacc.Bacc("TRN2", target_bir_lowering=False, num_devices=1)
    arrays, args = {}, []
    for name in _INS:
        a = np.ascontiguousarray(inputs[name])
        arrays["in_" + name] = a
        args.append(nc.dram_tensor("in_" + name, a.shape, mybir.dt.from_np(a.dtype), kind="ExternalInput").ap())
    out = nc.dram_tensor("out_dram", (1, S, D), F32, kind="ExternalOutput").ap()
    build(nc, *args, out)
    r = run_bass_kernel_spmd(nc, [arrays], core_ids=[0])
    return r.results[0]["out_dram"]
```

```python
import numpy as np
import concourse.bass as bass
from concourse import mybir
from contextlib import ExitStack

F32 = mybir.dt.float32
F32R = mybir.dt.float32r
I32 = mybir.dt.int32
ACT = mybir.ActivationFunctionType
ALU = mybir.AluOpType
AX = mybir.AxisListType

P = 128
D = 1024
S = 512
T = S // P
KD = D // P
DEPTH = 2
HD = 64
NPROJ = 2840
FF = 2816
NF = FF // P
MEM = 256
EPS = 1e-6
NEG = -1e30
NCMP = 31
CMPP = 32

MQ, MK, MV = 0, 256, 512
NQ, NKC, NVC, NKS, NVS, NKW, NVW = 768, 1280, 1408, 1536, 1664, 1792, 1920
NG, SQ, SK, SV = 2048, 2072, 2328, 2584

RING = 2
UW = 2048
U_IN, U_CMP, U_OUT, U_XK, U_XV, U_XQ, U_XO, U_UP, U_DOWN = 0, 12, 16, 20, 24, 28, 32, 36, 58
UNITS = 70
assert UNITS % RING == 0
IN_W = [512] * 5 + [280]

GROUPS = [(m, "moba") for m in range(2)] + [(m, k) for m in range(2, 6) for k in ("cmp", "sel", "win")]
GI = 2 * T
NI = GI * len(GROUPS)
LAG_T, LAG_COPY, LAG_PV = 3, 4, 12
PT_STEP, PT_ALL = 512, 3 * 512 + P
SB_OFF = [0, 512, 1024, 896]
SB_W = [512, 384, 256, 128]
SB_ALL = 1280


def item(i):
    g, r = divmod(i, GI)
    return (*GROUPS[g], r // 2, r % 2)


def item_keys(i):
    _, kind, t, _ = item(i)
    return CMPP if kind == "cmp" else P * (t + 1)


def blk_bank(b):
    return b if b < 4 else (4, 5, 6, 7, 0, 1)[(b - 4) % 6]


def row_broadcast(vec, l):
    return vec[l].unsqueeze(0).broadcast_to([P, vec.shape[1]])


def down_pieces(i):
    return [2 * i, 2 * i + 1] if i < 10 else [10 + i]


def row_broadcast(vec, l):
    return vec[l].unsqueeze(0).broadcast_to([P, vec.shape[1]])


class Signal:

    def __init__(self, sem, per_layer, start=0):
        self.sem, self.per_layer, self.start, self.seen = sem, per_layer, start, 0

    def at(self, l, n):
        return l * self.per_layer + (n + self.start)


def build(nc, x, mem, positions, norm_mix_pre, norm_mix_post, w_in, w_out, cmp_pe_k, cmp_pe_v,
          cmp_wk1, cmp_wk2, cmp_wv1, cmp_wv2, norm_x_pre, norm_x_post, norm_mem,
          x_wq, x_wk, x_wv, x_wo, norm_ffn_pre, norm_ffn_post, ffn_w_up, ffn_conv_w, ffn_conv_b,
          ffn_w_down, out):
    ctx = ExitStack()
    with ctx:
        place = [(nc.sbuf_base + 63) // 64 * 64]

        def region(nbytes):
            at = place[0]
            place[0] += (nbytes + 31) // 32 * 32
            assert place[0] <= nc.sbuf_usable_end, place
            return at

        def view(name, shape, dt, offset):
            return nc.alloc_sbuf_tensor_at(name, shape, dt, offset=offset)

        def new(name, shape, dt=F32):
            return view(name, shape, dt, region(int(np.prod(shape[1:])) * 4))

        raw = new("raw", [P, RING, UW])
        w_hi = new("w_hi", [P, RING, UW], F32R)
        w_lo = new("w_lo", [P, RING, UW], F32R)
        h = new("h", [P, T, D])
        X = region(2 * KD * S * 4)
        a_hi = view("a_hi", [P, KD, S], F32R, X)
        a_lo = view("a_lo", [P, KD, S], F32R, X + KD * S * 4)
        qT = view("qT", [P, 8, S], F32, X)
        kT = view("kT", [P, 6, S], F32, X + KD * S * 4)
        Y = region(T * NPROJ * 4)
        proj = view("proj", [P, T, NPROJ], F32, Y)
        m_hi = view("m_hi", [P, KD, MEM], F32R, Y)
        m_lo = view("m_lo", [P, KD, MEM], F32R, Y + 8192)
        xqT = view("xqT", [P, KD, S], F32, Y + 16384)
        xkT = view("xkT", [P, KD, MEM], F32, Y + 32768)
        gain_row = view("gain_row", [P, D], F32, Y + 40960)
        gT = view("gT", [P, NF, S], F32, Y)
        R = region(T * D * 4)
        rows = view("rows", [P, T, D], F32, R)
        oT = view("oT", [P, KD, S], F32, R)
        rope_tmp = view("rope_tmp", [P, 4, T * 64], F32, R)
        twice = view("twice", [P, T, 4, 2, HD], F32, R + 4096)
        xb = view("xb", [P, 16 * 62], F32, R)
        xb_hi = view("xb_hi", [P, 16 * 62], F32R, R + 3968)
        xb_lo = view("xb_lo", [P, 16 * 62], F32R, R + 7936)
        w2 = view("w2", [P, 2, 2, HD], F32, R + 11904)
        cg = view("cg", [P, 2, 256], F32, R + 12928)
        cgT = view("cgT", [P, 2, 62], F32, R + 14976)
        kc_rows = view("kc_rows", [32, 2, HD], F32, R + 15488)
        rope_tmp2 = view("rope_tmp2", [32, 4, 16], F32, R + 16000)
        vec_rows = view("vec_rows", [P, 2, P], F32, R + 8192)
        vec_a, vec_b = vec_rows[:, 0, :], vec_rows[:, 1, :]
        M = region(2 * D * 4)
        mem_rows = view("mem_rows", [P, 2, D], F32, M)
        xv = view("xv", [P, 2, D], F32, M)
        gain_row_ffn = view("gain_row_ffn", [P, D], F32, M)
        W = region(4 * PT_ALL * 4 + 4 * S * 4)
        probT = view("probT", [P, 4, PT_ALL], F32, W)
        prob = view("prob", [P, 4, S], F32, W + 4 * PT_ALL * 4)
        sb_sp = view("sb_sp", [P, 2, SB_ALL], F32, W)
        sb_tmp = view("sb_tmp", [P, 4, SB_ALL], F32, W + 2 * SB_ALL * 4)
        squares = view("squares", [P, D], F32, W)
        xprob = view("xprob", [P, 2, MEM], F32, W)
        xprobT = view("xprobT", [P, 2, 2, S], F32, W + 4096)
        conv = view("conv", [P, 3, S], F32, W)
        gel = view("gel", [P, 3, S], F32, W + 3 * S * 4)
        stage = view("stage", [P, 5, P], F32, W)

        ident = new("ident", [P, P])
        ident_r = new("ident_r", [P, P], F32R)
        causal = new("causal", [P, P], F32R)
        strictT = new("strictT", [P, P], F32R)
        strict_mul = new("strict_mul", [P, P])
        neg_tri = new("neg_tri", [P, P])
        neg_ones = new("neg_ones", [P, P])
        cmp_mask = new("cmp_mask", [P, T, CMPP], F32R)
        cmp_valid = new("cmp_valid", [P, T])
        vecs = new("vecs", [P, 152])
        sums = new("sums", [P, 40])
        est = new("est", [P, 40])
        rstd = new("rstd", [P, 40])
        nt = new("nt", [P, 2])
        eps_t = new("eps_t", [P, 1])
        cos_t = new("cos_t", [P, 5, 8])
        sin_t = new("sin_t", [P, 5, 8])
        kcT = new("kcT", [P, CMPP])
        vc_rows = new("vc_rows", [32, 2, HD])
        gates = new("gates", [P, T, 24])
        neg_max = new("neg_max", [P, 8])
        den = new("den", [P, 8])
        rden = new("rden", [P, 8])
        pos_i = view("pos_i", [P, 5], I32, R)
        pos_f = view("pos_f", [P, 5], F32, R + 32)
        ang = view("ang", [P, 2, 40], F32, R + 64)
        turns = view("turns", [P, 2, 40], F32, R + 64 + 320)

        banks = ctx.enter_context(nc.psum_tensor("banks", [P, 8 * 512], F32))

        def bank(b, n=512, at=0, rows_=P):
            return banks[0:rows_, b * 512 + at:b * 512 + at + n]

        signals = {}

        def signal(name, per_layer, start=0):
            s = Signal(ctx.enter_context(nc.semaphore(name)), per_layer, start)
            signals[name] = s
            return s

        def plain(name):
            return ctx.enter_context(nc.semaphore(name))

        pro_x, pro_pos, pro_const, pro_rope, pro_dve, pro_act, pro_pool = (
            plain(n) for n in ("pro_x", "pro_pos", "pro_const", "pro_rope", "pro_dve", "pro_act", "pro_pool"))
        stored = plain("stored")
        dve_chain, act_chain = plain("dve_chain"), plain("act_chain")
        raw_landed = [plain(f"raw_landed{i}") for i in range(RING)]
        hi_made = signal("hi_made", UNITS)
        lo_made = signal("lo_made", UNITS, RING)
        unit_used = signal("unit_used", UNITS, RING)
        vecs_landed = signal("vecs_landed", 128)
        w2_landed = signal("w2_landed", 32)
        mem_landed = signal("mem_landed", 16)
        gain_landed = [signal(f"gain_landed{i}", 16) for i in range(3)]
        vecs_T = signal("vecs_T", 2)
        vecs_ready = signal("vecs_ready", 2)
        pre_est = signal("pre_est", 12)
        post_est = signal("post_est", 12)
        mem_est = signal("mem_est", 2)
        mem_normed = signal("mem_normed", 2)
        h_done = signal("h_done", 12, 1)
        rows_done = signal("rows_done", 12)
        aT_psum = signal("aT_psum", 24)
        aT_hi = signal("aT_hi", 24)
        aT_lo = signal("aT_lo", 24)
        mT_psum = signal("mT_psum", KD)
        mT_hi = signal("mT_hi", KD)
        mT_lo = signal("mT_lo", KD)
        proj_psum = signal("proj_psum", 18)
        proj_act = signal("proj_act", 12)
        proj_dve = signal("proj_dve", 12)
        roped = signal("roped", 4)
        gated = signal("gated", 1)
        blk_psum = signal("blk_psum", 18)
        blk_act = signal("blk_act", 7)
        blk_dve = signal("blk_dve", 7)
        xb_ready = signal("xb_ready", 2)
        cmp_gelu = signal("cmp_gelu", 2)
        cgT_psum = signal("cgT_psum", 2)
        cgT_ready = signal("cgT_ready", 2)
        cmp2_psum = signal("cmp2_psum", 2)
        kc_roped = signal("kc_roped", 1)
        vc_ready = signal("vc_ready", 1)
        kcT_psum = signal("kcT_psum", 1)
        kcT_ready = signal("kcT_ready", 1)
        sb_z = signal("sb_z", 4)
        sb_l = signal("sb_l", 4)
        sb_masked = signal("sb_masked", 4)
        sb_log = signal("sb_log", 4)
        sb_prob = signal("sb_prob", 4)
        sb_pv = signal("sb_pv", 2)
        qk = signal("qk", NI)
        maxed = signal("maxed", NI)
        exped = signal("exped", NI)
        scaled = signal("scaled", NI)
        pT_psum = signal("pT_psum", NI)
        pT_act = signal("pT_act", NI // 2)
        pT_dve = signal("pT_dve", NI // 2)
        pv = signal("pv", len(GROUPS))
        oT_done = signal("oT_done", 8)
        o_hi = signal("o_hi", 4)
        o_lo = signal("o_lo", 4)
        out_psum = signal("out_psum", 9)
        xk_ready = signal("xk_ready", 4)
        xv_psum = signal("xv_psum", 3)
        xv_ready = signal("xv_ready", 4)
        xq_psum = signal("xq_psum", 4)
        xq_ready = signal("xq_ready", 8)
        xs = signal("xs", 16)
        xmaxed = signal("xmaxed", 16)
        xexped = signal("xexped", 16)
        xscaled = signal("xscaled", 16)
        xpT_psum = signal("xpT_psum", 16)
        xpT_ready = signal("xpT_ready", 16)
        xo_psum = signal("xo_psum", 8)
        xo_hi = signal("xo_hi", 8)
        xo_lo = signal("xo_lo", 8)
        up_psum = signal("up_psum", 2 * 11)
        conved = signal("conved", NF)
        gelued = signal("gelued", NF)
        gT_done = signal("gT_done", NF)
        g_hi = signal("g_hi", 12)
        g_lo = signal("g_lo", 12)

        made = {}

        def inc(ins, s):
            made[id(s)] = made.get(id(s), 0) + 1
            return ins.then_inc(s.sem, 1)

        def unit_source(l, u):
            if u < U_CMP:
                c, kh = divmod(u, 2)
                return w_in[l].rearrange("(k p) n -> p k n", p=P)[:, 4 * kh:4 * kh + 4, 512 * c:512 * c + IN_W[c]]
            if u < U_OUT:
                w = (cmp_wk1, cmp_wv1)[(u - U_CMP) // 2]
                kh = (u - U_CMP) % 2
                return w[l].rearrange("(k p) n -> p k n", p=P)[:, 8 * kh:8 * kh + 8, :]
            if u >= U_DOWN:
                k = down_pieces(u - U_DOWN)
                return ffn_w_down[l].rearrange("(k p) n -> p k n", p=P)[:, k[0]:k[-1] + 1, :]
            for w, first, last in ((w_out, U_OUT, U_XK), (x_wv, U_XV, U_XQ), (x_wo, U_XO, U_UP)):
                if first <= u < last:
                    k = 2 * (u - first)
                    return w[l].rearrange("(k p) n -> p k n", p=P)[:, k:k + 2, :]
            for w, first, last in ((x_wk, U_XK, U_XV), (x_wq, U_XQ, U_XO)):
                if first <= u < last:
                    m = 256 * (u - first)
                    return w[l].rearrange("(k p) n -> p k n", p=P)[:, :, m:m + 256]
            m = 256 * ((u - U_UP) // 2) + FF * ((u - U_UP) % 2)
            return ffn_w_up[l].rearrange("(k p) n -> p k n", p=P)[:, :, m:m + 256]

        def unit_view(buf, u):
            if u < U_CMP:
                n = IN_W[u // 2]
                return buf[:, u % RING, 0:4 * n].rearrange("p (k n) -> p k n", k=4)
            if u >= U_DOWN:
                n = len(down_pieces(u - U_DOWN))
                return buf[:, u % RING, 0:D * n].rearrange("p (k n) -> p k n", k=n)
            two = U_OUT <= u < U_XK or U_XV <= u < U_XQ or U_XO <= u < U_UP
            return buf[:, u % RING, :].rearrange("p (k n) -> p k n", k=2 if two else 8)

        def unit_width(u):
            if u >= U_DOWN:
                return D * len(down_pieces(u - U_DOWN))
            return 4 * IN_W[u // 2] if u < U_CMP else UW

        def wait_unit(eng, l, u):
            eng.wait_ge(unit_used.sem, unit_used.at(l, u + 1))

        def wait_proj(eng, l, c, t):
            if t < 3:
                eng.wait_ge(proj_psum.sem, proj_psum.at(l, 3 * c + t + 1))
            else:
                wait_unit(eng, l, U_IN + 2 * c + 1)

        def wait_out(eng, l, post, t):
            if t < 3:
                eng.wait_ge(out_psum.sem, out_psum.at(l, 3 * post + t + 1))
            else:
                wait_unit(eng, l, (U_XK, U_UP, UNITS)[post] - 1)

        def wait_xv(eng, l, b):
            if b < 3:
                eng.wait_ge(xv_psum.sem, xv_psum.at(l, b + 1))
            else:
                wait_unit(eng, l, U_XQ - 1)

        def wait_cols(eng, l, done, n, u, m):
            if m == 0:
                eng.wait_ge(done.sem, done.at(l, n + 1))
            else:
                wait_unit(eng, l, u)

        def proj_parts(c, t):
            b = c % 2 * 4 + t
            pairs = proj[:, t, NQ:NQ + 512].rearrange("p (m g d) -> p g m d", g=2, d=HD)
            if c == 1:
                return [(bank(b, 256), proj[:, t, MV:MV + 256]),
                        (bank(b, 256, 256).rearrange("p (m d) -> p m d", d=HD), pairs[:, 0])]
            if c == 2:
                return [(bank(b, 256).rearrange("p (m d) -> p m d", d=HD), pairs[:, 1]),
                        (bank(b, 256, 256).rearrange("p (m d) -> p m d", d=HD).unsqueeze(2).broadcast_to([P, 4, 2, HD]),
                         twice[:, t])]
            return [(bank(b, IN_W[c]), proj[:, t, 512 * c:512 * c + IN_W[c]])]

        CMP_STEPS = [3, 6, 9, 12]

        def copy_T(eng, l, i, done):
            _, kind, t, hp = item(i)
            g = i // GI
            eng.wait_ge(pT_psum.sem, pT_psum.at(l, i + 1))
            if g >= 2:
                eng.wait_ge(pv.sem, pv.at(l, g - 1))
            buf = probT[:, 2 * (g % 2) + hp, :]
            if kind == "cmp":
                src, dst = bank(3 + i % 3, P, 0, CMPP), buf[0:CMPP, P * t:P * t + P]
            else:
                src = bank(3 + i % 3, P * (t + 1)).rearrange("p (k q) -> p k q", q=P)
                dst = buf[:, P * t:P * t + 384 * t + P].rearrange("p (k q) -> p k q", q=P)[:, 0:3 * t + 1:3, :] if t else \
                    buf[:, 0:P].rearrange("p (k q) -> p k q", q=P)
            if done is pT_act:
                inc(eng.activation(dst, src, ACT.Copy), done)
            else:
                inc(eng.tensor_copy(dst, src), done)

        block = ctx.enter_context(nc.Block())

        @block.sync
        def _(sp):
            sp.dma_start(h[:], x[0].rearrange("(t p) d -> p t d", p=P)).then_inc(pro_x, 16)
            with sp.Fori(0, DEPTH) as l:
                for u in range(UNITS):
                    sp.wait_ge(lo_made.sem, l * UNITS + (u + 1))
                    sp.dma_start(unit_view(raw, u), unit_source(l, u)).then_inc(raw_landed[u % RING], 16)
            sp.wait_ge(h_done.sem, h_done.at(DEPTH, 0))
            sp.dma_start(out[0].rearrange("(t p) d -> p t d", p=P), h[:]).then_inc(stored, 16)
            sp.wait_ge(stored, 16)

        @block.gpsimd
        def _(pool):
            def link(ins, n):
                ins.then_inc(pro_pool, 1)
                pool.wait_ge(pro_pool, n)
            link(pool.memset(stage[:, 0:4, :], 0.0), 1)
            pool.memset(vec_rows[:], 0.0).then_inc(pro_pool, 1)
            pool.memset(ident[:], 0.0).then_inc(pro_pool, 1)
            pool.memset(strict_mul[:], 1.0).then_inc(pro_pool, 1)
            pool.memset(neg_tri[:], -1.0).then_inc(pro_pool, 1)
            pool.memset(neg_ones[:], -1.0).then_inc(pro_pool, 1)
            pool.memset(kcT[:], 0.0).then_inc(pro_pool, 1)
            link(pool.memset(cmp_valid[:], 1.0), 8)
            pool.affine_select(out=ident[:], in_=ident[:], compare_op=ALU.not_equal, fill=1.0, base=0,
                               pattern=[[-1, P]], channel_multiplier=1).then_inc(pro_pool, 1)
            pool.affine_select(out=stage[:, 1, :], in_=stage[:, 1, :], compare_op=ALU.is_ge, fill=NEG, base=0,
                               pattern=[[-1, P]], channel_multiplier=1).then_inc(pro_pool, 1)
            pool.affine_select(out=stage[:, 2, :], in_=stage[:, 2, :], compare_op=ALU.is_ge, fill=NEG, base=-1,
                               pattern=[[1, P]], channel_multiplier=-1).then_inc(pro_pool, 1)
            pool.affine_select(out=stage[:, 3, :].rearrange("p (t j) -> p t j", t=T),
                               in_=stage[:, 3, :].rearrange("p (t j) -> p t j", t=T),
                               compare_op=ALU.is_ge, fill=NEG, base=-31,
                               pattern=[[P, T], [-16, CMPP]], channel_multiplier=1).then_inc(pro_pool, 1)
            pool.affine_select(out=strict_mul[:], in_=strict_mul[:], compare_op=ALU.is_ge, fill=0.0, base=-1,
                               pattern=[[1, P]], channel_multiplier=-1).then_inc(pro_pool, 1)
            pool.affine_select(out=neg_tri[:], in_=neg_tri[:], compare_op=ALU.is_ge, fill=0.0, base=0,
                               pattern=[[-1, P]], channel_multiplier=1).then_inc(pro_pool, 1)
            link(pool.affine_select(out=cmp_valid[:], in_=cmp_valid[:], compare_op=ALU.is_ge, fill=0.0, base=-31,
                                    pattern=[[P, T]], channel_multiplier=1), 15)
            pool.tensor_copy(ident_r[:], ident[:]).then_inc(pro_pool, 1)
            pool.tensor_copy(causal[:], stage[:, 1, :]).then_inc(pro_pool, 1)
            pool.tensor_copy(strictT[:], stage[:, 2, :]).then_inc(pro_pool, 1)
            pool.tensor_copy(cmp_mask[:].rearrange("p t j -> p (t j)"), stage[:, 3, :]).then_inc(pro_pool, 1)
            pool.wait_ge(pro_pool, 19)
            pool.memset(nt[:, 0:1], 0.0).then_inc(lo_made.sem, RING)
            pool.memset(nt[:, 1:2], 0.0).then_inc(unit_used.sem, RING)
            pool.memset(den[:], 0.0).then_inc(pro_const, 1)
            with pool.Fori(0, DEPTH) as l:
                for u in range(UNITS):
                    n = unit_width(u)
                    pool.wait_ge(hi_made.sem, hi_made.at(l, u + 1))
                    inc(pool.tensor_tensor(w_lo[:, u % RING, 0:n], raw[:, u % RING, 0:n],
                                           w_hi[:, u % RING, 0:n].bitcast(F32), ALU.subtract), lo_made)

        @block.scalar
        def _(act):
            count = [0]

            def link(ins):
                count[0] += 1
                ins.then_inc(act_chain, 1)
                act.wait_ge(act_chain, count[0])

            def rms_estimate(src, junk, c, done):
                link(act.activation(junk, src, ACT.Square, accum_out=sums[:, c:c + 1]))
                link(act.activation(est[:, c:c + 1], sums[:, c:c + 1], ACT.Ln, scale=1.0 / D, bias=eps_t[:]))
                inc(act.activation(est[:, c:c + 1], est[:, c:c + 1], ACT.Exp, scale=-0.5), done)

            act.dma_start(pos_i[:, 0:4], positions.rearrange("b (t p) -> p (b t)", p=P), allow_slow_non_contiguous=True).then_inc(pro_pos, 16)
            act.wait_ge(pro_dve, 1)
            act.dma_start(pos_i[0:NCMP, 4:5],
                          positions[:, 16:S].rearrange("b (j c) -> (b j) c", c=16)[:, 15:16], allow_slow_non_contiguous=True).then_inc(pro_pos, 16)
            act.wait_ge(pro_rope, 1)
            act.activation(sin_t[:].rearrange("p a b -> p (a b)"), ang[:, 0, :], ACT.Sin).then_inc(pro_act, 1)
            act.activation(cos_t[:].rearrange("p a b -> p (a b)"), ang[:, 1, :], ACT.Sin).then_inc(pro_act, 1)
            act.wait_ge(pro_act, 2)
            act.wait_ge(pro_x, 16)
            act.wait_ge(pro_const, 1)

            act.preload_act_table_set("natural_log_exp_and_others")
            with act.Fori(0, DEPTH) as l:
                next_unit = [0]

                def cast_to(n):
                    while next_unit[0] < min(n, UNITS):
                        u = next_unit[0]
                        w = unit_width(u)
                        act.wait_ge(raw_landed[u % RING], l * (16 * UNITS // RING) + 16 * (u // RING + 1))
                        act.wait_ge(unit_used.sem, l * UNITS + (u + 1))
                        inc(act.activation(w_hi[:, u % RING, 0:w], raw[:, u % RING, 0:w], ACT.Copy), hi_made)
                        next_unit[0] += 1

                def hi_parts(inst, gain):
                    for k in range(KD):
                        act.wait_ge(aT_psum.sem, aT_psum.at(l, KD * inst + k + 1))
                        scale = vecs[:, gain + k:gain + k + 1] if gain is not None else 1.0
                        inc(act.activation(a_hi[:, k, :], bank(4 + k % 4), ACT.Copy, scale=scale), aT_hi)

                def post_and_pre(post, pre, casts=(0, 0, 0, 0, 0)):
                    for t in range(T + 1):
                        cast_to(casts[t])
                        if t < T:
                            wait_out(act, l, post, t)
                            rms_estimate(banks[:, 1024 * t:1024 * t + 1024], rows[:, t, :], 12 + T * post + t, post_est)
                        if pre is not None and t:
                            act.wait_ge(h_done.sem, h_done.at(l, T * post + t))
                            rms_estimate(h[:, t - 1, :], rows[:, t - 1, :], T * pre + t - 1, pre_est)

                act.wait_ge(h_done.sem, h_done.at(l, 0))
                g = 0
                for vec in (norm_mix_pre, norm_x_pre, norm_mem, norm_ffn_pre):
                    act.dma_start(vec_a[g:g + 8, :], vec[l].rearrange("(k p) -> k p", p=P)).then_inc(vecs_landed.sem, 16)
                    g += 8
                for vec in (cmp_pe_k, cmp_pe_v):
                    act.dma_start(vec_a[g:g + 16, :], vec[l].rearrange("(q a) d -> q (a d)", a=2)).then_inc(vecs_landed.sem, 16)
                    g += 16
                act.dma_start(vec_b[0:66, :], ffn_conv_w[l].rearrange("w (f p) -> (w f) p", p=P)).then_inc(vecs_landed.sem, 16)
                act.dma_start(vec_b[66:88, :], ffn_conv_b[l].rearrange("(f p) -> f p", p=P)).then_inc(vecs_landed.sem, 16)
                act.dma_start(mem_rows[:], mem[0].rearrange("(t p) d -> p t d", p=P)).then_inc(mem_landed.sem, 16)
                cast_to(2)
                act.wait_ge(vecs_ready.sem, vecs_ready.at(l, 2))
                for t in range(T):
                    rms_estimate(h[:, t, :], rows[:, t, :], t, pre_est)
                hi_parts(0, 0)
                act.wait_ge(mem_landed.sem, mem_landed.at(l, 16))
                for t in range(2):
                    rms_estimate(mem_rows[:, t, :], squares[:], 32 + t, mem_est)

                for c in range(6):
                    cast_to(2 * c + 3)
                    for t in (0, 1):
                        wait_proj(act, l, c, t)
                        for src, dst in proj_parts(c, t):
                            ins = act.activation(dst, src, ACT.Copy)
                        inc(ins, proj_act)
                    cast_to(2 * c + 4)
                act.wait_ge(proj_act.sem, proj_act.at(l, 12))
                act.wait_ge(proj_dve.sem, proj_dve.at(l, 12))
                inc(act.activation(gates[:], proj[:, :, NG:NG + 24], ACT.Exp, scale=-1.0), gated)
                act.wait_ge(blk_psum.sem, blk_psum.at(l, 4))
                for i, w in enumerate((cmp_wk2, cmp_wv2)):
                    act.dma_start(w2[:, i], w[l].rearrange("(c p) n -> p c n", p=P)).then_inc(w2_landed.sem, 16)

                for b in range(4, 18, 2):
                    act.wait_ge(blk_psum.sem, blk_psum.at(l, b + 1))
                    i = b - 4
                    dst = qT[:, i, :] if i < 8 else kT[:, i - 8, :]
                    inc(act.activation(dst, bank(blk_bank(b)), ACT.Copy, scale=HD ** -0.5 if i < 8 else 1.0), blk_act)
                for i in range(2):
                    cast_to(U_CMP + 2 * i + 3)
                    wait_unit(act, l, U_CMP + 2 * i + 1)
                    inc(act.activation(cg[0:62, i, :], bank(4 + i, 256, 0, 62), ACT.Gelu_apprx_tanh), cmp_gelu)

                cast_to(U_OUT + 2)
                act.preload_act_table_set("natural_log_exp_and_others")

                def copy_o(m, b, done, n):
                    act.wait_ge(done.sem, done.at(l, n))
                    inc(act.activation(oT[:, m, :], bank(b), ACT.Copy), oT_done)

                for i in range(NI + LAG_PV):
                    if i < NI:
                        n = item_keys(i)
                        act.wait_ge(maxed.sem, maxed.at(l, i + 1))
                        if i >= 4:
                            act.wait_ge(pT_psum.sem, pT_psum.at(l, i - 3))
                        inc(act.activation(prob[:, i % 4, 0:n], bank(i % 3, n), ACT.Exp,
                                           bias=neg_max[:, i % 8:i % 8 + 1], accum_out=den[:, i % 8:i % 8 + 1]), exped)
                    if 0 <= i - LAG_COPY < NI and (i - LAG_COPY) % 2 == 0:
                        copy_T(act, l, i - LAG_COPY, pT_act)
                    g, r = divmod(i - LAG_PV, GI)
                    if r == 1 and g >= 0 and (g == len(GROUPS) - 1 or GROUPS[g][0] != GROUPS[g + 1][0]):
                        copy_o(GROUPS[g][0], 6 + GROUPS[g][0] % 2, pv, g + 1)

                def sb_softplus(hh):
                    src, tmp = banks[:, 1536 * (hh % 2):1536 * (hh % 2) + SB_ALL], sb_tmp[:, hh, :]
                    act.wait_ge(sb_z.sem, sb_z.at(l, hh + 1))
                    link(act.activation(tmp, src, ACT.Abs))
                    link(act.activation(tmp, tmp, ACT.Exp, scale=-1.0))
                    inc(act.activation(tmp, tmp, ACT.Ln, bias=1.0), sb_l)

                def sb_exp(hh):
                    act.wait_ge(sb_log.sem, sb_log.at(l, hh + 1))
                    inc(act.activation(sb_tmp[:, hh, :], banks[:, 1536 * (hh % 2):1536 * (hh % 2) + SB_ALL], ACT.Exp), sb_prob)

                sb_softplus(0)
                sb_softplus(1)
                sb_exp(0)
                sb_softplus(2)
                sb_exp(1)
                sb_softplus(3)
                sb_exp(2)
                copy_o(6, 6, sb_pv, 1)
                sb_exp(3)
                copy_o(7, 7, sb_pv, 2)
                act.wait_ge(oT_done.sem, oT_done.at(l, 8))
                for j in range(4):
                    inc(act.activation(a_hi[:, 2 * j:2 * j + 2, :], oT[:, 2 * j:2 * j + 2, :], ACT.Copy), o_hi)
                act.dma_start(gain_row[:], row_broadcast(norm_mix_post, l)).then_inc(gain_landed[0].sem, 16)
                for k in range(KD):
                    act.wait_ge(mT_psum.sem, mT_psum.at(l, k // 2 * 2 + 2))
                    inc(act.activation(m_hi[:, k, :], bank(k // 2, MEM, k % 2 * MEM), ACT.Copy,
                                       scale=vecs[:, 16 + k:17 + k]), mT_hi)
                cast_to(U_OUT + 4)
                post_and_pre(0, 1, (0, U_XK + 1, U_XK + 2, U_XK + 2, U_XK + 2))
                cast_to(U_XQ + 2)
                hi_parts(1, 8)
                act.dma_start(gain_row[:], row_broadcast(norm_x_post, l)).then_inc(gain_landed[1].sem, 16)
                cast_to(U_XO + 2)
                def copy_xT(i):
                    act.wait_ge(xpT_psum.sem, xpT_psum.at(l, i + 1))
                    if i // 4 >= 2:
                        act.wait_ge(xo_psum.sem, xo_psum.at(l, 2 * (i // 4 - 1)))
                    inc(act.activation(xprobT[:, i // 4 % 2, :, P * (i % 4):P * (i % 4) + P],
                                       bank(2 + i % 2, MEM).rearrange("p (m q) -> p m q", m=2), ACT.Copy), xpT_ready)

                def hi_o(j):
                    act.wait_ge(xo_psum.sem, xo_psum.at(l, j + 1))
                    inc(act.activation(a_hi[:, j, :], bank(4 + j % 4), ACT.Copy), xo_hi)

                for i in range(16):
                    act.wait_ge(xmaxed.sem, xmaxed.at(l, i + 1))
                    if i >= 2:
                        act.wait_ge(xpT_psum.sem, xpT_psum.at(l, i - 1))
                    inc(act.activation(xprob[:, i % 2, :], bank(i % 2, MEM), ACT.Exp,
                                       bias=neg_max[:, i % 8:i % 8 + 1], accum_out=den[:, i % 8:i % 8 + 1]), xexped)
                    if i:
                        copy_xT(i - 1)
                    if i % 4 == 2 and i > 4:
                        hi_o(2 * (i // 4) - 2)
                        hi_o(2 * (i // 4) - 1)
                copy_xT(15)
                hi_o(6)
                hi_o(7)
                act.wait_ge(xo_psum.sem, xo_psum.at(l, 8))
                act.dma_start(gain_row_ffn[:], row_broadcast(norm_ffn_post, l)).then_inc(gain_landed[2].sem, 16)
                cast_to(U_XO + 4)
                post_and_pre(1, 2, (0, U_UP + 1, U_UP + 2, U_UP + 2, U_UP + 2))
                hi_parts(2, 24)

                for f in range(NF):
                    cast_to(U_UP + f + 3)
                    act.wait_ge(conved.sem, conved.at(l, f + 1))
                    if f >= 3:
                        act.wait_ge(gT_done.sem, gT_done.at(l, f - 2))
                    inc(act.activation(gel[:, f % 3, :], conv[:, f % 3, :], ACT.Gelu_apprx_tanh,
                                       bias=vecs[:, 130 + f:131 + f]), gelued)
                act.preload_act_table_set("natural_log_exp_and_others")
                for i in range(12):
                    k = down_pieces(i)
                    act.wait_ge(gT_done.sem, gT_done.at(l, k[-1] + 1))
                    act.wait_ge(unit_used.sem, unit_used.at(l, U_DOWN if i < 4 else U_DOWN + (k[-1] - 8) // 2 + 1))
                    inc(act.activation(a_hi[:, k[0] % 8:k[0] % 8 + len(k), :], gT[:, k[0]:k[-1] + 1, :], ACT.Copy), g_hi)
                    cast_to(U_DOWN + i + 2)
                post_and_pre(2, None)
                act.sem_clear(act_chain)
                count[0] = 0

        @block.vector
        def _(dve):
            count = [0]

            def link(ins):
                count[0] += 1
                ins.then_inc(dve_chain, 1)
                dve.wait_ge(dve_chain, count[0])

            dve.memset(eps_t[:], EPS)
            dve.memset(pos_i[:, 4:5], 0).then_inc(pro_dve, 1)
            dve.wait_ge(pro_pos, 32)
            link(dve.tensor_copy(pos_f[:], pos_i[:]))
            for j in range(8):
                freq = float(np.float32(500000.0) ** np.float32(-j / 8))
                ins = dve.tensor_scalar(ang[:, 0, :].rearrange("p (t j) -> p t j", j=8)[:, :, j], pos_f[:], freq, None, ALU.mult)
            link(ins)
            link(dve.tensor_copy(ang[:, 1, :], ang[:, 0, :]))
            inv = float(1 / (2 * np.pi))
            link(dve.tensor_scalar(turns[:, 0, :], ang[:, 0, :], inv, None, ALU.mult))
            link(dve.tensor_scalar(turns[:, 1, :], ang[:, 0, :], inv, 0.25, ALU.mult, ALU.add))
            big = 12582912.0
            link(dve.tensor_scalar(turns[:], turns[:], big, None, ALU.add))
            link(dve.tensor_scalar(turns[:], turns[:], big, None, ALU.subtract))
            c1 = 6.28125
            c2 = float(np.float32(round((2 * np.pi - c1) * 2 ** 19) / 2 ** 19))
            c3 = float(2 * np.pi - c1 - c2)
            for c in (c1, c2, c3):
                link(dve.scalar_tensor_tensor(ang[:], turns[:], -c, ang[:], ALU.mult, ALU.add))
            link(dve.tensor_scalar(ang[:, 1, :], ang[:, 1, :], float(np.pi / 2), None, ALU.add))
            dve.tensor_scalar(ang[:], ang[:], 3.1415925, -3.1415925, ALU.min, ALU.max).then_inc(pro_rope, 1)
            dve.wait_ge(pro_act, 2)
            dve.wait_ge(pro_x, 16)
            dve.wait_ge(pro_const, 1)

            def newton(c):
                link(dve.tensor_scalar(sums[:, c:c + 1], sums[:, c:c + 1], -0.5 / D, -0.5 * EPS, ALU.mult, ALU.add))
                link(dve.scalar_tensor_tensor(rstd[:, c:c + 1], est[:, c:c + 1], sums[:, c:c + 1], est[:, c:c + 1], ALU.mult, ALU.mult))
                link(dve.scalar_tensor_tensor(rstd[:, c:c + 1], rstd[:, c:c + 1], 1.5, est[:, c:c + 1], ALU.add, ALU.mult))

            def rope(dst, cs, sn, tmp):
                x1, x2 = dst[..., 0:8], dst[..., 8:16]
                dve.tensor_tensor(tmp[0], x1, cs, ALU.mult)
                dve.tensor_tensor(tmp[1], x2, sn, ALU.mult)
                dve.tensor_tensor(tmp[2], x2, cs, ALU.mult)
                link(dve.tensor_tensor(tmp[3], x1, sn, ALU.mult))
                dve.tensor_tensor(x1, tmp[0], tmp[1], ALU.subtract)
                return dve.tensor_tensor(x2, tmp[2], tmp[3], ALU.add)

            dve.sem_clear(dve_chain)
            count[0] = 0
            dve.memset(sums[:], 0.0).then_inc(h_done.sem, 1)
            with dve.Fori(0, DEPTH) as l:
                for i, (v, n) in enumerate(((vec_a, 64), (vec_b, 88))):
                    dve.wait_ge(vecs_T.sem, vecs_T.at(l, i + 1))
                    inc(dve.tensor_copy(vecs[:, 64 * i:64 * i + n], bank(i, n)), vecs_ready)

                def pre_norm(pre, t):
                    dve.wait_ge(pre_est.sem, pre_est.at(l, T * pre + t + 1))
                    newton(T * pre + t)
                    inc(dve.tensor_scalar(rows[:, t, :], h[:, t, :], rstd[:, T * pre + t:T * pre + t + 1], None, ALU.mult), rows_done)

                def lo_parts(inst, gain):
                    for k in range(KD):
                        dve.wait_ge(aT_hi.sem, aT_hi.at(l, KD * inst + k + 1))
                        if gain is None:
                            ins = dve.tensor_tensor(a_lo[:, k, :], bank(4 + k % 4), a_hi[:, k, :].bitcast(F32), ALU.subtract)
                        else:
                            ins = dve.scalar_tensor_tensor(a_lo[:, k, :], bank(4 + k % 4), vecs[:, gain + k:gain + k + 1],
                                                           a_hi[:, k, :].bitcast(F32), ALU.mult, ALU.subtract)
                        inc(ins, aT_lo)

                def post_and_pre(post, pre, gain):
                    dve.wait_ge(gain_landed[post].sem, gain_landed[post].at(l, 16))
                    for t in range(T + 1):
                        if t < T:
                            c = 12 + T * post + t
                            dve.wait_ge(post_est.sem, post_est.at(l, T * post + t + 1))
                            newton(c)
                            link(dve.scalar_tensor_tensor(rows[:, t, :], banks[:, 1024 * t:1024 * t + 1024], rstd[:, c:c + 1],
                                                          gain[:], ALU.mult, ALU.mult))
                            inc(dve.tensor_tensor(h[:, t, :], h[:, t, :], rows[:, t, :], ALU.add), h_done)
                        if pre is not None and t:
                            pre_norm(pre, t - 1)

                for t in range(T):
                    pre_norm(0, t)
                lo_parts(0, 0)
                for t in range(2):
                    dve.wait_ge(mem_est.sem, mem_est.at(l, t + 1))
                    newton(32 + t)
                    inc(dve.tensor_scalar(mem_rows[:, t, :], mem_rows[:, t, :], rstd[:, 32 + t:33 + t], None, ALU.mult), mem_normed)

                def rope_heads(col, n, table_heads):
                    dve.wait_ge(proj_act.sem, proj_act.at(l, 2 * ((col + 64 * n - 1) // 512) + 2))
                    dst = proj[:, :, col:col + 64 * n].rearrange("p t (m d) -> p t m d", d=HD)
                    shape = [P, T, n, 8]
                    cs = cos_t[:, 0:4, :].unsqueeze(2).broadcast_to(shape)
                    sn = sin_t[:, 0:4, :].unsqueeze(2).broadcast_to(shape)
                    tmp = [rope_tmp[:, i, 0:T * n * 8].rearrange("p (t m d) -> p t m d", t=T, d=8) for i in range(4)]
                    inc(rope(dst, cs, sn, tmp), roped)
                    dve.wait_ge(roped.sem, roped.at(l, table_heads))

                for c in range(6):
                    for t in (2, 3):
                        wait_proj(dve, l, c, t)
                        for src, dst in proj_parts(c, t):
                            ins = dve.tensor_copy(dst, src)
                        inc(ins, proj_dve)
                    dve.wait_ge(proj_dve.sem, proj_dve.at(l, 2 * c + 2))
                    if c == 0:
                        rope_heads(MQ, 8, 1)
                    if c == 2:
                        rope_heads(NQ, 8, 2)
                    if c == 3:
                        rope_heads(NKS, 2, 3)
                        rope_heads(NKW, 2, 4)
                dve.wait_ge(gated.sem, gated.at(l, 1))
                link(dve.tensor_scalar(gates[:], gates[:], 1.0, None, ALU.add))
                link(dve.reciprocal(gates[:], gates[:]))

                for i in range(2):
                    dve.wait_ge(blk_psum.sem, blk_psum.at(l, 4))
                    if i:
                        wait_unit(dve, l, U_CMP + 1)
                    for g in range(2):
                        for a in range(2):
                            pp = slice(64 * a, 64 * a + 64)
                            src = banks[pp, 512 * (2 * i + g):512 * (2 * i + g) + 512].rearrange("p (j r) -> p r j", r=16)
                            dst = xb[pp, :].rearrange("p (q g j) -> p q g j", q=16, g=2)
                            for half in range(2):
                                q = slice(8 * half, 8 * half + 8)
                                pe = vecs[pp, 32 + 16 * i + 8 * half:40 + 16 * i + 8 * half].unsqueeze(2).broadcast_to([64, 8, NCMP])
                                ins = dve.tensor_tensor(dst[:, q, g, :], src[:, a:16:2, half:half + NCMP], pe, ALU.add)
                    link(ins)
                    link(dve.tensor_copy(xb_hi[:], xb[:]))
                    inc(dve.tensor_tensor(xb_lo[:], xb[:], xb_hi[:].bitcast(F32), ALU.subtract), xb_ready)
                    if i == 0:
                        for b in range(5, 18, 2):
                            dve.wait_ge(blk_psum.sem, blk_psum.at(l, b + 1))
                            j = b - 4
                            if j < 8:
                                inc(dve.tensor_scalar(qT[:, j, :], bank(blk_bank(b)), HD ** -0.5, None, ALU.mult), blk_dve)
                            else:
                                inc(dve.tensor_copy(kT[:, j - 8, :], bank(blk_bank(b))), blk_dve)
                def compressed(step):
                    i, part = divmod(step, 2)
                    if part == 0:
                        dve.wait_ge(cgT_psum.sem, cgT_psum.at(l, i + 1))
                        if i:
                            dve.wait_ge(kcT_psum.sem, kcT_psum.at(l, 1))
                            inc(dve.tensor_copy(kcT[:, 0:NCMP], bank(7, NCMP, 384)), kcT_ready)
                        inc(dve.tensor_copy(cgT[:], bank(7, 256).rearrange("p (c j) -> p c j", c=2)[:, :, 0:62]), cgT_ready)
                    else:
                        dve.wait_ge(cmp2_psum.sem, cmp2_psum.at(l, i + 1))
                        src = bank(7, 128, 256, NCMP).rearrange("p (g d) -> p g d", g=2)
                        if i == 0:
                            link(dve.tensor_copy(kc_rows[0:NCMP], src))
                            shape = [NCMP, 2, 8]
                            cs = cos_t[0:NCMP, 4:5, :].broadcast_to(shape)
                            sn = sin_t[0:NCMP, 4:5, :].broadcast_to(shape)
                            tmp = [rope_tmp2[0:NCMP, j, :].rearrange("p (g d) -> p g d", g=2) for j in range(4)]
                            inc(rope(kc_rows[0:NCMP], cs, sn, tmp), kc_roped)
                        else:
                            inc(dve.tensor_copy(vc_rows[0:NCMP], src), vc_ready)

                def scale(i):
                    m, kind, t, hp = item(i)
                    n = item_keys(i)
                    dve.wait_ge(exped.sem, exped.at(l, i + 1))
                    link(dve.reciprocal(rden[:, i % 8:i % 8 + 1], den[:, i % 8:i % 8 + 1]))
                    r = rden[:, i % 8:i % 8 + 1]
                    if kind == "moba":
                        ins = dve.tensor_scalar(prob[:, i % 4, 0:n], prob[:, i % 4, 0:n], r, None, ALU.mult)
                    else:
                        c = 3 * (2 * m + hp - 4) + ("cmp", "sel", "win").index(kind)
                        if kind == "cmp":
                            link(dve.tensor_tensor(r, r, cmp_valid[:, t:t + 1], ALU.mult))
                        ins = dve.tensor_scalar(prob[:, i % 4, 0:n], prob[:, i % 4, 0:n], r, gates[:, t, c:c + 1], ALU.mult, ALU.mult)
                    inc(ins, scaled)

                for i in range(NI + LAG_COPY):
                    if i < NI:
                        dve.wait_ge(qk.sem, qk.at(l, i + 1))
                        inc(dve.tensor_reduce(neg_max[:, i % 8:i % 8 + 1], bank(i % 3, item_keys(i)), AX.X, ALU.max, negate=True), maxed)
                    if 1 <= i <= NI:
                        scale(i - 1)
                    if i >= LAG_COPY and (i - LAG_COPY) % 2:
                        copy_T(dve, l, i - LAG_COPY, pT_dve)
                    if i in CMP_STEPS:
                        compressed(CMP_STEPS.index(i))

                for hh in range(4):
                    dve.wait_ge(sb_l.sem, sb_l.at(l, hh + 1))
                    if hh >= 2:
                        dve.wait_ge(sb_log.sem, sb_log.at(l, hh - 1))
                    sp = sb_sp[:, hh % 2, :]
                    link(dve.scalar_tensor_tensor(sp, banks[:, 1536 * (hh % 2):1536 * (hh % 2) + SB_ALL], 0.0,
                                                  sb_tmp[:, hh, :], ALU.max, ALU.add))
                    for k in range(T):
                        s = slice(SB_OFF[k], SB_OFF[k] + P)
                        ins = dve.tensor_tensor(sp[:, s], sp[:, s], strict_mul[:], ALU.mult)
                    inc(ins, sb_masked)
                for j in range(4):
                    dve.wait_ge(o_hi.sem, o_hi.at(l, j + 1))
                    inc(dve.tensor_tensor(a_lo[:, 2 * j:2 * j + 2, :], oT[:, 2 * j:2 * j + 2, :],
                                          a_hi[:, 2 * j:2 * j + 2, :].bitcast(F32), ALU.subtract), o_lo)
                for k in range(KD):
                    dve.wait_ge(mT_hi.sem, mT_hi.at(l, k // 2 * 2 + 2))
                    inc(dve.scalar_tensor_tensor(m_lo[:, k, :], bank(k // 2, MEM, k % 2 * MEM), vecs[:, 16 + k:17 + k],
                                                 m_hi[:, k, :].bitcast(F32), ALU.mult, ALU.subtract), mT_lo)
                post_and_pre(0, 1, gain_row)

                for u in range(4):
                    wait_unit(dve, l, U_XK + u)
                    inc(dve.tensor_copy(xkT[:, 2 * u:2 * u + 2, :].rearrange("p a m -> p (a m)"), bank(u)), xk_ready)
                for b in range(4):
                    wait_xv(dve, l, b)
                    inc(dve.tensor_copy(xv[:, b // 2, 512 * (b % 2):512 * (b % 2) + 512], bank(4 + b)), xv_ready)
                lo_parts(1, 8)
                for m in range(KD):
                    wait_cols(dve, l, xq_psum, m // 2, U_XQ + m // 2, m % 2)
                    inc(dve.tensor_scalar(xqT[:, m, :], bank(m % 4), 256 ** -0.5, None, ALU.mult), xq_ready)

                def xscale(i):
                    dve.wait_ge(xexped.sem, xexped.at(l, i + 1))
                    r = rden[:, i % 8:i % 8 + 1]
                    link(dve.reciprocal(r, den[:, i % 8:i % 8 + 1]))
                    inc(dve.tensor_scalar(xprob[:, i % 2, :], xprob[:, i % 2, :], r, None, ALU.mult), xscaled)

                def lo_o(j):
                    dve.wait_ge(xo_hi.sem, xo_hi.at(l, j + 1))
                    inc(dve.tensor_tensor(a_lo[:, j, :], bank(4 + j % 4), a_hi[:, j, :].bitcast(F32), ALU.subtract), xo_lo)

                for i in range(17):
                    if i < 16:
                        dve.wait_ge(xs.sem, xs.at(l, i + 1))
                        inc(dve.tensor_reduce(neg_max[:, i % 8:i % 8 + 1], bank(i % 2, MEM), AX.X, ALU.max, negate=True), xmaxed)
                    if i:
                        xscale(i - 1)
                    if i % 4 == 3 and i > 4:
                        lo_o(2 * (i // 4) - 2)
                        lo_o(2 * (i // 4) - 1)
                lo_o(6)
                lo_o(7)
                post_and_pre(1, 2, gain_row)
                lo_parts(2, 24)

                def gate(f):
                    dve.wait_ge(gelued.sem, gelued.at(l, f + 1))
                    jp, b = divmod(f, 2)
                    wait_cols(dve, l, up_psum, 2 * jp + 1, U_UP + 2 * jp + 1, b)
                    inc(dve.tensor_tensor(gT[:, f, :], gel[:, f % 3, :], bank(jp % 2 * 4 + 2 + b), ALU.mult), gT_done)

                for f in range(NF + 1):
                    if f < NF:
                        jp, b = divmod(f, 2)
                        src = banks[:, 512 * (jp % 2 * 4 + b):512 * (jp % 2 * 4 + b) + 512]
                        cv = conv[:, f % 3, :]
                        wait_cols(dve, l, up_psum, 2 * jp, U_UP + 2 * jp, b)
                        if f >= 3:
                            dve.wait_ge(gelued.sem, gelued.at(l, f - 2))
                        wcol = lambda i: vecs[:, 64 + 22 * i + f:65 + 22 * i + f]
                        link(dve.tensor_scalar(cv, src, wcol(2), None, ALU.mult))
                        link(dve.scalar_tensor_tensor(cv[:, 1:S], src[:, 0:S - 1], wcol(1), cv[:, 1:S], ALU.mult, ALU.add))
                        inc(dve.scalar_tensor_tensor(cv[:, 2:S], src[:, 0:S - 2], wcol(0), cv[:, 2:S], ALU.mult, ALU.add), conved)
                    if f:
                        gate(f - 1)
                for i in range(12):
                    dve.wait_ge(g_hi.sem, g_hi.at(l, i + 1))
                    k = down_pieces(i)
                    s8 = slice(k[0] % 8, k[0] % 8 + len(k))
                    inc(dve.tensor_tensor(a_lo[:, s8, :], gT[:, k[0]:k[-1] + 1, :], a_hi[:, s8, :].bitcast(F32), ALU.subtract), g_lo)
                post_and_pre(2, None, gain_row_ffn)
                dve.sem_clear(dve_chain)
                count[0] = 0

        @block.tensor
        def _(pe):
            pe.wait_ge(pro_const, 1)

            def three(dst, st_hi, st_lo, mv_hi, mv_lo, first, last):
                pe.matmul(dst, st_lo, mv_hi, start=first, stop=False)
                pe.matmul(dst, st_hi, mv_lo, start=False, stop=False)
                return pe.matmul(dst, st_hi, mv_hi, start=False, stop=last)

            with pe.Fori(0, DEPTH) as l:
                def unit(u):
                    pe.wait_ge(lo_made.sem, lo_made.at(l, u + 1))
                    return unit_view(w_hi, u), unit_view(w_lo, u)

                def transpose_rows(inst):
                    for k in range(KD):
                        if k >= 4:
                            pe.wait_ge(aT_lo.sem, aT_lo.at(l, KD * inst + k - 3))
                        for t in range(T):
                            ins = pe.transpose(bank(4 + k % 4, P, P * t), rows[:, t, P * k:P * k + P], ident[:])
                        inc(ins, aT_psum)

                def rows_gemm(first, n_units, post, ready):
                    for i in range(n_units):
                        hi, lo = unit(first + i)
                        ready(i)
                        for t in range(T):
                            for n in range(2):
                                pieces = down_pieces(i)
                                if post < 2:
                                    pieces = [2 * i, 2 * i + 1]
                                for k in range(len(pieces)):
                                    a = pieces[k] % KD
                                    st = slice(P * t, P * t + P)
                                    ins = three(bank(2 * t + n), a_hi[:, a, st], a_lo[:, a, st],
                                                hi[:, k, 512 * n:512 * n + 512], lo[:, k, 512 * n:512 * n + 512],
                                                i == 0 and k == 0, i == n_units - 1 and k == len(pieces) - 1)
                            if i == n_units - 1 and t < T - 1:
                                inc(ins, out_psum)
                        inc(ins, unit_used)

                pe.wait_ge(vecs_landed.sem, vecs_landed.at(l, 128))
                pe.wait_ge(h_done.sem, h_done.at(l, 0))
                for i, (v, n) in enumerate(((vec_a, 64), (vec_b, 88))):
                    inc(pe.transpose(bank(i, P), v, ident[:]), vecs_T)

                pe.wait_ge(rows_done.sem, rows_done.at(l, 4))
                transpose_rows(0)
                for c in range(6):
                    for kh in range(2):
                        u = U_IN + 2 * c + kh
                        hi, lo = unit(u)
                        for t in range(T):
                            if c >= 2 and kh == 0:
                                done = proj_act if t < 2 else proj_dve
                                pe.wait_ge(done.sem, done.at(l, 2 * (c - 2) + t % 2 + 1))
                            for k in range(4):
                                if c == 0 and t == 0 or c == 1 and kh == 0 and t == 0 and k == 0:
                                    pe.wait_ge(aT_lo.sem, aT_lo.at(l, 4 * kh + k + 1 if c == 0 else KD))
                                a = 4 * kh + k
                                st = slice(P * t, P * t + P)
                                ins = three(bank(c % 2 * 4 + t, IN_W[c]), a_hi[:, a, st], a_lo[:, a, st],
                                            hi[:, k, :], lo[:, k, :], kh == 0 and k == 0, kh == 1 and k == 3)
                            if kh == 1 and t < 3:
                                inc(ins, proj_psum)
                        inc(ins, unit_used)

                pe.wait_ge(proj_act.sem, proj_act.at(l, 12))
                pe.wait_ge(proj_dve.sem, proj_dve.at(l, 12))
                pe.wait_ge(roped.sem, roped.at(l, 4))
                pairs_q = [MQ, MQ + P, NQ, NQ + P, NQ + 2 * P, NQ + 3 * P, SQ, SQ + P]
                pairs_k = [MK, MK + P, SK, SK + P]
                for b, col in enumerate([None] * 4 + pairs_q + pairs_k + [NKS, NKW]):
                    if b == 8:
                        pe.wait_ge(xb_ready.sem, xb_ready.at(l, 1))
                    if b >= 10:
                        done = blk_act if b % 2 == 0 else blk_dve
                        pe.wait_ge(done.sem, done.at(l, (b - 10) // 2 + 1))
                    for t in range(T):
                        src = twice[:, t, b].rearrange("p a d -> p (a d)") if b < 4 else proj[:, t, col:col + P]
                        ins = pe.transpose(bank(blk_bank(b), P, P * t), src, ident[:])
                    inc(ins, blk_psum)

                pe.wait_ge(blk_act.sem, blk_act.at(l, 7))
                pe.wait_ge(blk_dve.sem, blk_dve.at(l, 7))
                for i in range(2):
                    pe.wait_ge(xb_ready.sem, xb_ready.at(l, i + 1))
                    for kh in range(2):
                        u = U_CMP + 2 * i + kh
                        hi, lo = unit(u)
                        for k in range(8):
                            q = 8 * kh + k
                            st = slice(62 * q, 62 * q + 62)
                            ins = three(bank(4 + i, 256, 0, 62), xb_hi[:, st], xb_lo[:, st], hi[:, k, :], lo[:, k, :],
                                        q == 0, q == 15)
                        inc(ins, unit_used)
                def compressed(step):
                    i, part = divmod(step, 2)
                    if part == 0:
                        if i:
                            pe.wait_ge(kc_roped.sem, kc_roped.at(l, 1))
                        pe.wait_ge(cmp_gelu.sem, cmp_gelu.at(l, i + 1))
                        for c in range(2):
                            ins = pe.transpose(bank(7, P, P * c), cg[:, i, P * c:P * c + P], ident[:])
                        inc(ins, cgT_psum)
                        if i:
                            inc(pe.transpose(bank(7, NCMP, 384), kc_rows[0:NCMP].rearrange("p g d -> p (g d)"), ident[0:NCMP, 0:NCMP]), kcT_psum)
                    else:
                        pe.wait_ge(w2_landed.sem, w2_landed.at(l, 32))
                        pe.wait_ge(cgT_ready.sem, cgT_ready.at(l, i + 1))
                        for g in range(2):
                            for c in range(2):
                                ins = pe.matmul(bank(7, HD, 256 + HD * g, NCMP), cgT[:, c, NCMP * g:NCMP * g + NCMP], w2[:, i, c, :],
                                                start=c == 0, stop=c == 1)
                        inc(ins, cmp2_psum)

                def scores(i):
                    m, kind, t, hp = item(i)
                    head = 2 * m + hp
                    g = (head - 4) // 4
                    b0, pair = (HD * hp, m) if kind == "moba" else (HD * g, 2 + (head - 4) % 4)
                    n = item_keys(i)
                    if i >= 3:
                        pe.wait_ge(exped.sem, exped.at(l, i - 2))
                    if kind == "cmp" and GROUPS.index((m, kind)) == 2 and t == 0 and hp == 0:
                        pe.wait_ge(kcT_ready.sem, kcT_ready.at(l, 1))
                    keys = {"moba": kT[b0:b0 + HD, m % 2, 0:n], "sel": kT[b0:b0 + HD, 4, 0:n],
                            "win": kT[b0:b0 + HD, 5, 0:n], "cmp": kcT[b0:b0 + HD, :]}[kind]
                    pe.matmul(bank(i % 3, n), qT[b0:b0 + HD, pair, P * t:P * t + P], keys, start=True, stop=False)
                    if kind == "cmp":
                        inc(pe.matmul(bank(i % 3, CMPP), ident_r[:], cmp_mask[:, t, :], start=False, stop=True), qk)
                    else:
                        inc(pe.matmul(bank(i % 3, P, n - P), ident_r[:], causal[:], start=False, stop=True), qk)

                def transposes(i):
                    _, kind, t, _ = item(i)
                    pe.wait_ge(scaled.sem, scaled.at(l, i + 1))
                    if i >= 3:
                        j = i - 3
                        done = pT_dve if j % 2 else pT_act
                        pe.wait_ge(done.sem, done.at(l, j // 2 + 1))
                    if kind == "cmp":
                        ins = pe.transpose(bank(3 + i % 3, P, 0, CMPP), prob[:, i % 4, 0:CMPP], ident[:])
                    else:
                        for k in range(t + 1):
                            ins = pe.transpose(bank(3 + i % 3, P, P * k), prob[:, i % 4, P * k:P * k + P], ident[:])
                    inc(ins, pT_psum)

                def values(g):
                    m, kind = GROUPS[g]
                    for done in (pT_act, pT_dve):
                        pe.wait_ge(done.sem, done.at(l, T * (g + 1)))
                    first = kind in ("moba", "cmp")
                    if first and m >= 2:
                        pe.wait_ge(oT_done.sem, oT_done.at(l, m - 1))
                    for k in range(1 if kind == "cmp" else T):
                        for hp in range(2):
                            head = 2 * m + hp
                            kg = (head - 4) // 4
                            dst = bank(6 + m % 2, S - P * k, P * k)[HD * hp:HD * hp + HD]
                            if kind == "cmp":
                                ins = pe.matmul(dst, vc_rows[0:NCMP, kg, :], probT[0:NCMP, 2 * (g % 2) + hp, 0:S], start=True, stop=False)
                            else:
                                col = {"moba": MV + HD * head, "sel": NVS + HD * kg, "win": NVW + HD * kg}[kind]
                                ins = pe.matmul(dst, proj[:, k, col:col + HD], probT[:, 2 * (g % 2) + hp, PT_STEP * k:PT_STEP * k + S - P * k],
                                                start=first and k == 0, stop=kind in ("moba", "win") and k == T - 1)
                    inc(ins, pv)

                for i in range(NI + LAG_PV):
                    if i < NI:
                        scores(i)
                    if LAG_T <= i < NI + LAG_T:
                        transposes(i - LAG_T)
                    if i >= LAG_PV and (i - LAG_PV) % GI == 0:
                        values((i - LAG_PV) // GI)
                    if i in CMP_STEPS:
                        compressed(CMP_STEPS.index(i))

                pe.wait_ge(oT_done.sem, oT_done.at(l, 6))

                def sb_bank(hh, k, n, at=0):
                    c = 1536 * (hh % 2) + SB_OFF[k] + at
                    return banks[:, c:c + n]

                def sb_scores(hh):
                    b0, pair = 64 * (hh % 2), hh // 2
                    if hh >= 2:
                        pe.wait_ge(sb_prob.sem, sb_prob.at(l, hh - 1))
                    for k in range(T):
                        ins = pe.matmul(sb_bank(hh, k, SB_W[k]), kT[b0:b0 + HD, 2 + pair, P * k:P * k + P],
                                        qT[b0:b0 + HD, 6 + pair, P * k:S], start=k < 3, stop=True, skip_group_check=True)
                    inc(ins, sb_z)

                def sb_logs(hh):
                    sp = sb_sp[:, hh % 2, :]
                    pe.wait_ge(sb_masked.sem, sb_masked.at(l, hh + 1))
                    for k in range(T):
                        pe.matmul(sb_bank(hh, k, P), ident_r[:], strictT[:], start=False, stop=False, skip_group_check=True)
                        ins = pe.matmul(sb_bank(hh, k, SB_W[k]), neg_tri[:], sp[:, SB_OFF[k]:SB_OFF[k] + SB_W[k]],
                                        start=False, stop=False, skip_group_check=True)
                        for j in range(k + 1, T):
                            ins = pe.matmul(sb_bank(hh, k, SB_W[j], P * (j - k)), neg_ones[:], sp[:, SB_OFF[j]:SB_OFF[j] + SB_W[j]],
                                            start=False, stop=False, skip_group_check=True)
                    inc(ins, sb_log)

                def sb_values(m):
                    pe.wait_ge(sb_prob.sem, sb_prob.at(l, 2 * m + 2))
                    for k in range(T):
                        for hp in range(2):
                            hh = 2 * m + hp
                            ins = pe.matmul(bank(6 + m, S - P * k, P * k)[HD * hp:HD * hp + HD], proj[:, k, SV + HD * hh:SV + HD * hh + HD],
                                            sb_tmp[:, hh, SB_OFF[k]:SB_OFF[k] + SB_W[k]], start=k == 0, stop=k == T - 1)
                    inc(ins, sb_pv)

                sb_scores(0)
                sb_scores(1)
                sb_logs(0)
                sb_scores(2)
                sb_logs(1)
                sb_scores(3)
                sb_values(0)
                sb_logs(2)
                sb_logs(3)
                sb_values(1)

                pe.wait_ge(mem_normed.sem, mem_normed.at(l, 2))
                for k in range(KD):
                    for t in range(2):
                        ins = pe.transpose(bank(k // 2, P, k % 2 * MEM + P * t), mem_rows[:, t, P * k:P * k + P], ident[:])
                    inc(ins, mT_psum)
                pe.wait_ge(mT_lo.sem, mT_lo.at(l, KD))
                pe.wait_ge(oT_done.sem, oT_done.at(l, 8))
                rows_gemm(U_OUT, 4, 0, lambda i: pe.wait_ge(o_lo.sem, o_lo.at(l, i + 1)))

                for u in range(4):
                    pe.wait_ge(h_done.sem, h_done.at(l, u // 2 + 1))
                    hi, lo = unit(U_XK + u)
                    for m in range(2):
                        for k in range(KD):
                            mm = slice(P * m, P * m + P)
                            ins = three(bank(u, MEM, MEM * m), hi[:, k, mm], lo[:, k, mm], m_hi[:, k, :], m_lo[:, k, :], k == 0, k == KD - 1)
                    inc(ins, unit_used)
                pe.wait_ge(h_done.sem, h_done.at(l, 4))
                for u in range(4):
                    hi, lo = unit(U_XV + u)
                    for t in range(2):
                        for n in range(2):
                            for k in range(2):
                                a, st, nn = 2 * u + k, slice(P * t, P * t + P), slice(512 * n, 512 * n + 512)
                                ins = three(bank(4 + 2 * t + n), m_hi[:, a, st], m_lo[:, a, st], hi[:, k, nn], lo[:, k, nn],
                                            u == 0 and k == 0, u == 3 and k == 1)
                            if u == 3 and 2 * t + n < 3:
                                inc(ins, xv_psum)
                    inc(ins, unit_used)
                pe.wait_ge(rows_done.sem, rows_done.at(l, 8))
                pe.wait_ge(xv_ready.sem, xv_ready.at(l, 4))
                transpose_rows(1)

                def cols_gemm(u, b, done):
                    hi, lo = unit(u)
                    for m in range(2):
                        for k in range(KD):
                            mm = slice(P * m, P * m + P)
                            ins = three(bank(b + m), hi[:, k, mm], lo[:, k, mm], a_hi[:, k, :], a_lo[:, k, :], k == 0, k == KD - 1)
                        inc(ins, (done, unit_used)[m])

                pe.wait_ge(aT_lo.sem, aT_lo.at(l, 16))
                pe.wait_ge(xk_ready.sem, xk_ready.at(l, 4))
                for u in range(4):
                    if u >= 2:
                        pe.wait_ge(xq_ready.sem, xq_ready.at(l, 2 * (u - 2) + 2))
                    cols_gemm(U_XQ + u, 2 * (u % 2), xq_psum)
                pe.wait_ge(xq_ready.sem, xq_ready.at(l, 8))

                def xscores(i):
                    head, t = divmod(i, 4)
                    if i >= 2:
                        pe.wait_ge(xexped.sem, xexped.at(l, i - 1))
                    for c in range(2):
                        ins = pe.matmul(bank(i % 2, MEM), xqT[:, 2 * head + c, P * t:P * t + P], xkT[:, 2 * head + c, :],
                                        start=c == 0, stop=c == 1)
                    inc(ins, xs)

                def xtransposes(i):
                    pe.wait_ge(xscaled.sem, xscaled.at(l, i + 1))
                    if i >= 2:
                        pe.wait_ge(xpT_ready.sem, xpT_ready.at(l, i - 1))
                    for m in range(2):
                        ins = pe.transpose(bank(2 + i % 2, P, P * m), xprob[:, i % 2, P * m:P * m + P], ident[:])
                    inc(ins, xpT_psum)

                def xvalues(head):
                    pe.wait_ge(xpT_ready.sem, xpT_ready.at(l, 4 * head + 4))
                    for d in range(2):
                        j = 2 * head + d
                        if j >= 4:
                            pe.wait_ge(xo_lo.sem, xo_lo.at(l, j - 3))
                        for m in range(2):
                            ins = pe.matmul(bank(4 + j % 4), xv[:, m, P * j:P * j + P], xprobT[:, head % 2, m, :],
                                            start=m == 0, stop=m == 1)
                        inc(ins, xo_psum)

                for i in range(17):
                    if i < 16:
                        xscores(i)
                    if i:
                        xtransposes(i - 1)
                    if i % 4 == 1 and i > 4:
                        xvalues(i // 4 - 1)
                xvalues(3)
                pe.wait_ge(xo_lo.sem, xo_lo.at(l, 8))
                rows_gemm(U_XO, 4, 1, lambda i: None)

                pe.wait_ge(rows_done.sem, rows_done.at(l, 12))
                transpose_rows(2)
                pe.wait_ge(aT_lo.sem, aT_lo.at(l, 24))
                for jp in range(11):
                    if jp >= 2:
                        pe.wait_ge(gT_done.sem, gT_done.at(l, 2 * (jp - 2) + 2))
                    cols_gemm(U_UP + 2 * jp, jp % 2 * 4, up_psum)
                    cols_gemm(U_UP + 2 * jp + 1, jp % 2 * 4 + 2, up_psum)
                pe.wait_ge(gT_done.sem, gT_done.at(l, NF))
                rows_gemm(U_DOWN, 12, 2, lambda i: pe.wait_ge(g_lo.sem, g_lo.at(l, i + 1)))


            for s in signals.values():
                if id(s) in made:
                    assert made[id(s)] == s.per_layer, [n for n in signals if signals[n] is s] + [made[id(s)]]


_INS = ["x", "mem", "positions", "norm_mix_pre", "norm_mix_post", "w_in", "w_out", "cmp_pe_k", "cmp_pe_v",
        "cmp_wk1", "cmp_wk2", "cmp_wv1", "cmp_wv2", "norm_x_pre", "norm_x_post", "norm_mem",
        "x_wq", "x_wk", "x_wv", "x_wo", "norm_ffn_pre", "norm_ffn_post", "ffn_w_up", "ffn_conv_w",
        "ffn_conv_b", "ffn_w_down"]


def kernel(**inputs):
    import concourse.bacc as bacc
    from concourse.bass_utils import run_bass_kernel_spmd

    nc = bacc.Bacc("TRN2", target_bir_lowering=False, num_devices=1)
    arrays, args = {}, []
    for name in _INS:
        a = np.ascontiguousarray(inputs[name])
        arrays["in_" + name] = a
        args.append(nc.dram_tensor("in_" + name, a.shape, mybir.dt.from_np(a.dtype), kind="ExternalInput").ap())
    out = nc.dram_tensor("out_dram", (1, S, D), F32, kind="ExternalOutput").ap()
    build(nc, *args, out)
    r = run_bass_kernel_spmd(nc, [arrays], core_ids=[0])
    return r.results[0]["out_dram"]
```

```python
import numpy as np
import concourse.bass as bass
from concourse import mybir
from contextlib import ExitStack

F32 = mybir.dt.float32
F32R = mybir.dt.float32r
I32 = mybir.dt.int32
ACT = mybir.ActivationFunctionType
ALU = mybir.AluOpType
AX = mybir.AxisListType

P = 128
D = 1024
S = 512
T = S // P
KD = D // P
DEPTH = 2
HD = 64
NPROJ = 2840
FF = 2816
NF = FF // P
MEM = 256
EPS = 1e-6
NEG = -1e30
NCMP = 31
CMPP = 32

MQ, MK, MV = 0, 256, 512
NQ, NKC, NVC, NKS, NVS, NKW, NVW = 768, 1280, 1408, 1536, 1664, 1792, 1920
NG, SQ, SK, SV = 2048, 2072, 2328, 2584

RING = 2
UW = 2048
U_IN, U_CMP, U_OUT, U_XK, U_XV, U_XQ, U_XO, U_UP, U_DOWN = 0, 12, 16, 20, 24, 28, 32, 36, 58
UNITS = 70
assert UNITS % RING == 0
IN_W = [512] * 5 + [280]

GROUPS = [(m, "moba") for m in range(2)] + [(m, k) for m in range(2, 6) for k in ("sel", "cmp", "win")]
ITEMS = [(g, t, hp) for g, (_, kind) in enumerate(GROUPS)
         for t in range(1 if kind == "cmp" else T) for hp in range(1 if kind == "cmp" else 2)]
NI = len(ITEMS)
LAST = [max(i for i in range(NI) if ITEMS[i][0] == g) for g in range(len(GROUPS))]
LAG_SCALE, LAG_T, LAG_COPY, LAG_V = 1, 3, 3, 7
PIECES = sorted((LAST[g] + LAG_V + (6 if kind == "cmp" else 2 * k), g, k)
                for g, (_, kind) in enumerate(GROUPS) for k in range(1 if kind == "cmp" else T))
STEPS = PIECES[-1][0] + 1
PROBS = 5
PT_STEP, PT_ALL = 512, 3 * 512 + P
XLAG_T, XLAG_V = 3, 5
XPIECES = {4 * head + 3 + XLAG_V + 2 * d: 2 * head + d for head in range(4) for d in range(2)}
XSTEPS = max(XPIECES) + 1
SB_OFF = [0, 512, 1024, 896]
SB_W = [512, 384, 256, 128]
SB_ALL = 1280


def full_groups(g):
    return sum(kind != "cmp" for _, kind in GROUPS[:g])


def item_keys(i):
    g, t, _ = ITEMS[i]
    return 2 * T * CMPP if GROUPS[g][1] == "cmp" else P * (t + 1)


def blk_bank(b):
    return b if b < 4 else 4 + b % 4


def down_pieces(i):
    return [2 * i, 2 * i + 1] if i < 10 else [10 + i]


def aT_bank(inst, k):
    return (0 if inst else 4) + k % 4


def up_bank(jp, half):
    return (jp + 1) % 2 * 4 + 2 * half


def row_broadcast(vec, l):
    return vec[l].unsqueeze(0).broadcast_to([P, vec.shape[1]])


class Signal:

    def __init__(self, sem, per_layer, start=0):
        self.sem, self.per_layer, self.start = sem, per_layer, start

    def at(self, l, n):
        return l * self.per_layer + (n + self.start)


def build(nc, x, mem, positions, norm_mix_pre, norm_mix_post, w_in, w_out, cmp_pe_k, cmp_pe_v,
          cmp_wk1, cmp_wk2, cmp_wv1, cmp_wv2, norm_x_pre, norm_x_post, norm_mem,
          x_wq, x_wk, x_wv, x_wo, norm_ffn_pre, norm_ffn_post, ffn_w_up, ffn_conv_w, ffn_conv_b,
          ffn_w_down, out):
    ctx = ExitStack()
    with ctx:
        place = [(nc.sbuf_base + 63) // 64 * 64]

        def region(nbytes):
            at = place[0]
            place[0] += (nbytes + 31) // 32 * 32
            assert place[0] <= nc.sbuf_usable_end, place
            return at

        def view(name, shape, dt, offset):
            return nc.alloc_sbuf_tensor_at(name, shape, dt, offset=offset)

        def new(name, shape, dt=F32):
            return view(name, shape, dt, region(int(np.prod(shape[1:])) * 4))

        raw = new("raw", [P, RING, UW])
        w_hi = new("w_hi", [P, RING, UW], F32R)
        w_lo = new("w_lo", [P, RING, UW], F32R)
        h = new("h", [P, T, D])
        X = region(2 * KD * S * 4)
        a_hi = view("a_hi", [P, KD, S], F32R, X)
        a_lo = view("a_lo", [P, KD, S], F32R, X + KD * S * 4)
        qT = view("qT", [P, 8, S], F32, X)
        kT = view("kT", [P, 6, S], F32, X + KD * S * 4)
        cprobT = view("cprobT", [P, 2, 2, P], F32, X + (KD + 6) * S * 4)
        vc_tiles = view("vc_tiles", [P, T, 2, HD], F32, X + (KD + 7) * S * 4)
        Y = region(T * NPROJ * 4)
        proj = view("proj", [P, T, NPROJ], F32, Y)
        m_hi = view("m_hi", [P, KD, MEM], F32R, Y)
        m_lo = view("m_lo", [P, KD, MEM], F32R, Y + 8192)
        xqT = view("xqT", [P, KD, S], F32, Y + 16384)
        xkT = view("xkT", [P, KD, MEM], F32, Y + 32768)
        gain_row = view("gain_row", [P, D], F32, Y + 40960)
        gT = view("gT", [P, NF, S], F32, Y)
        R = region(T * D * 4)
        rows = view("rows", [P, T, D], F32, R)
        oT = view("oT", [P, KD, S], F32, R)
        rope_tmp = view("rope_tmp", [P, 4, T * 64], F32, R)
        twice = view("twice", [P, T, 4, 2, HD], F32, R + 4096)
        w2 = view("w2", [P, 2, 2, HD], F32, R + 11904)
        cg = view("cg", [P, 2, 256], F32, R + 12928)
        cgT = view("cgT", [P, 2, 2, T, CMPP], F32, R + 8192)
        kc_rows = view("kc_rows", [32, 2, HD], F32, R + 15488)
        rope_tmp2 = view("rope_tmp2", [32, 4, 16], F32, R + 16000)
        vec_rows = new("vec_rows", [P, 2, P])
        vec_a, vec_b = vec_rows[:, 0, :], vec_rows[:, 1, :]
        M = region(2 * D * 4)
        memT = view("memT", [P, KD, MEM], F32, M)
        xv = view("xv", [P, 2, D], F32, M)
        gain_row_ffn = view("gain_row_ffn", [P, D], F32, M)
        W = region(4 * PT_ALL * 4 + PROBS * S * 4)
        probT = view("probT", [P, 4, PT_ALL], F32, W)
        prob = view("prob", [P, PROBS, S], F32, W + 4 * PT_ALL * 4)
        sb_sp = view("sb_sp", [P, 2, SB_ALL], F32, W)
        sb_tmp = [view(f"sb_tmp{hh}", [P, SB_ALL], F32, W + (4 if hh < 2 else 2) * PT_ALL * 4 + hh % 2 * SB_ALL * 4) for hh in range(4)]
        assert 2 * SB_ALL <= 2 * PT_ALL and 2 * SB_ALL <= PROBS * S
        xb, xb_hi, xb_lo = ([view(f"{name}{i}", [P, 16 * 62], dt, W + 3968 * (3 * i + j)) for i in range(2)]
                            for j, (name, dt) in enumerate((("xb", F32), ("xb_hi", F32R), ("xb_lo", F32R))))
        mem_rows = view("mem_rows", [P, 2, D], F32, W + 6 * 3968)
        squares = view("squares", [P, D], F32, W)
        xprob = view("xprob", [P, PROBS, MEM], F32, W)
        xprobT = view("xprobT", [P, 2, 2, S], F32, W + PROBS * MEM * 4)
        conv = view("conv", [P, 3, S], F32, W)
        gel = view("gel", [P, 3, S], F32, W + 3 * S * 4)
        first_hi = view("first_hi", [P, 4, S], F32R, W + 6 * S * 4)
        first_lo = view("first_lo", [P, 4, S], F32R, W + 10 * S * 4)
        stage = view("stage", [P, 5, P], F32, W)

        ident = new("ident", [P, P])
        ident_r = new("ident_r", [P, P], F32R)
        causal = new("causal", [P, P], F32R)
        strictT = new("strictT", [P, P], F32R)
        strict_mul = new("strict_mul", [P, P])
        neg_tri = new("neg_tri", [P, P])
        neg_ones = new("neg_ones", [P, P])
        cmp_mask = new("cmp_mask", [P, T, CMPP], F32R)
        cmp_valid = new("cmp_valid", [P, T])
        vecs = new("vecs", [P, 152])
        sums = new("sums", [P, 40])
        est = new("est", [P, 40])
        rstd = new("rstd", [P, 40])
        nt = new("nt", [P, 2])
        eps_t = new("eps_t", [P, 1])
        cos_t = new("cos_t", [P, 5, 8])
        sin_t = new("sin_t", [P, 5, 8])
        kcT = new("kcT", [P, CMPP])
        cmp_gates = new("cmp_gates", [P, T, 8])
        c_max = new("c_max", [P, 2, T])
        c_den = new("c_den", [P, 2, T])
        gates = new("gates", [P, T, 24])
        neg_max = new("neg_max", [P, 8])
        den = new("den", [P, 8])
        rden = new("rden", [P, 8])
        pos_i = view("pos_i", [P, 5], I32, R)
        pos_f = view("pos_f", [P, 5], F32, R + 32)
        ang = view("ang", [P, 2, 40], F32, R + 64)
        turns = view("turns", [P, 2, 40], F32, R + 64 + 320)

        banks = ctx.enter_context(nc.psum_tensor("banks", [P, 8 * 512], F32))

        def bank(b, n=512, at=0, rows_=P):
            return banks[0:rows_, b * 512 + at:b * 512 + at + n]

        signals = {}

        def signal(name, per_layer, start=0):
            s = Signal(ctx.enter_context(nc.semaphore(name)), per_layer, start)
            signals[name] = s
            return s

        def plain(name):
            return ctx.enter_context(nc.semaphore(name))

        pro_x, pro_pos, pro_const, pro_rope, pro_dve, pro_act, pro_pool = (
            plain(n) for n in ("pro_x", "pro_pos", "pro_const", "pro_rope", "pro_dve", "pro_act", "pro_pool"))
        stored = plain("stored")
        dve_chain, act_chain = plain("dve_chain"), plain("act_chain")
        raw_landed = [plain(f"raw_landed{i}") for i in range(RING)]
        hi_made = signal("hi_made", 2 * UNITS)
        lo_made = signal("lo_made", 2 * UNITS, 2 * RING)
        unit_used = signal("unit_used", UNITS, RING)
        vecs_landed = signal("vecs_landed", 128)
        w2_landed = signal("w2_landed", 32)
        mem_landed = signal("mem_landed", 16)
        gain_landed = [signal(f"gain_landed{i}", 16) for i in range(3)]
        vecs_T = signal("vecs_T", 2)
        vecs_ready = signal("vecs_ready", 2)
        pre_est = signal("pre_est", 12)
        post_est = signal("post_est", 12)
        mem_est = signal("mem_est", 2)
        mem_normed = signal("mem_normed", 2)
        pre_rstd = signal("pre_rstd", 1)
        h_done = signal("h_done", 12, T)
        normed = signal("normed", 2 * (T - 1))
        rows_done = signal("rows_done", 8)
        aT_psum = signal("aT_psum", 24)
        aT_hi = signal("aT_hi", 24)
        aT_lo = signal("aT_lo", 24)
        mT_hi = signal("mT_hi", KD)
        mT_lo = signal("mT_lo", KD)
        proj_psum = signal("proj_psum", 18)
        proj_act = signal("proj_act", 12)
        proj_dve = signal("proj_dve", 12)
        roped = signal("roped", 4)
        gated = signal("gated", 1)
        blk_psum = signal("blk_psum", 22)
        blk_act = signal("blk_act", 9)
        blk_dve = signal("blk_dve", 9)
        xb_ready = signal("xb_ready", 2)
        cmp_gelu = signal("cmp_gelu", 2)
        cgT_psum = signal("cgT_psum", 2)
        cgT_ready = signal("cgT_ready", 2)
        cmp2_psum = signal("cmp2_psum", 2)
        kc_roped = signal("kc_roped", 1)
        vc_ready = signal("vc_ready", 1)
        kcT_psum = signal("kcT_psum", 1)
        kcT_ready = signal("kcT_ready", 1)
        sb_z = signal("sb_z", 4)
        sb_l = signal("sb_l", 4)
        sb_masked = signal("sb_masked", 4)
        sb_log = signal("sb_log", 4)
        sb_prob = signal("sb_prob", 4)
        sb_pv = signal("sb_pv", 2)
        qk = signal("qk", NI)
        maxed = signal("maxed", NI)
        exped = signal("exped", NI)
        scaled = signal("scaled", NI)
        pT_psum = signal("pT_psum", NI)
        pT_copied = signal("pT_copied", NI)
        pv = signal("pv", len(GROUPS))
        oT_done = signal("oT_done", 8)
        o_hi = signal("o_hi", 4)
        o_lo = signal("o_lo", 4)
        out_psum = signal("out_psum", 9)
        xk_ready = signal("xk_ready", 4)
        xv_psum = signal("xv_psum", 3)
        xv_ready = signal("xv_ready", 4)
        xq_psum = signal("xq_psum", 4)
        xq_ready = signal("xq_ready", 8)
        xs = signal("xs", 16)
        xmaxed = signal("xmaxed", 16)
        xexped = signal("xexped", 16)
        xscaled = signal("xscaled", 16)
        xpT_psum = signal("xpT_psum", 16)
        xpT_ready = signal("xpT_ready", 16)
        xo_psum = signal("xo_psum", 8)
        xo_hi = signal("xo_hi", 8)
        xo_lo = signal("xo_lo", 8)
        up_psum = signal("up_psum", 2 * 11)
        conved = signal("conved", NF)
        gelued = signal("gelued", NF)
        gT_done = signal("gT_done", NF)
        g_hi = signal("g_hi", 12)
        g_lo = signal("g_lo", 12)

        made = {}

        def inc(ins, s):
            made[id(s)] = made.get(id(s), 0) + 1
            return ins.then_inc(s.sem, 1)

        def unit_source(l, u):
            if u < U_CMP:
                c, kh = divmod(u, 2)
                return w_in[l].rearrange("(k p) n -> p k n", p=P)[:, 4 * kh:4 * kh + 4, 512 * c:512 * c + IN_W[c]]
            if u < U_OUT:
                w = (cmp_wk1, cmp_wv1)[(u - U_CMP) // 2]
                kh = (u - U_CMP) % 2
                return w[l].rearrange("(k p) n -> p k n", p=P)[:, 8 * kh:8 * kh + 8, :]
            if u >= U_DOWN:
                k = down_pieces(u - U_DOWN)
                return ffn_w_down[l].rearrange("(k p) n -> p k n", p=P)[:, k[0]:k[-1] + 1, :]
            for w, first, last in ((w_out, U_OUT, U_XK), (x_wv, U_XV, U_XQ), (x_wo, U_XO, U_UP)):
                if first <= u < last:
                    k = 2 * (u - first)
                    return w[l].rearrange("(k p) n -> p k n", p=P)[:, k:k + 2, :]
            for w, first, last in ((x_wk, U_XK, U_XV), (x_wq, U_XQ, U_XO)):
                if first <= u < last:
                    m = 256 * (u - first)
                    return w[l].rearrange("(k p) n -> p k n", p=P)[:, :, m:m + 256]
            m = 256 * ((u - U_UP) // 2) + FF * ((u - U_UP) % 2)
            return ffn_w_up[l].rearrange("(k p) n -> p k n", p=P)[:, :, m:m + 256]

        def unit_view(buf, u):
            if u < U_CMP:
                n = IN_W[u // 2]
                return buf[:, u % RING, 0:4 * n].rearrange("p (k n) -> p k n", k=4)
            if u >= U_DOWN:
                n = len(down_pieces(u - U_DOWN))
                return buf[:, u % RING, 0:D * n].rearrange("p (k n) -> p k n", k=n)
            two = U_OUT <= u < U_XK or U_XV <= u < U_XQ or U_XO <= u < U_UP
            return buf[:, u % RING, :].rearrange("p (k n) -> p k n", k=2 if two else 8)

        def unit_width(u):
            if u >= U_DOWN:
                return D * len(down_pieces(u - U_DOWN))
            return 4 * IN_W[u // 2] if u < U_CMP else UW

        def wait_unit(eng, l, u):
            eng.wait_ge(unit_used.sem, unit_used.at(l, u + 1))

        def wait_proj(eng, l, c, t):
            if t < 3:
                eng.wait_ge(proj_psum.sem, proj_psum.at(l, 3 * c + t + 1))
            else:
                wait_unit(eng, l, U_IN + 2 * c + 1)

        def wait_out(eng, l, post, t):
            if t < 3:
                eng.wait_ge(out_psum.sem, out_psum.at(l, 3 * post + t + 1))
            else:
                wait_unit(eng, l, (U_XK, U_UP, UNITS)[post] - 1)

        def wait_xv(eng, l, b):
            if b < 3:
                eng.wait_ge(xv_psum.sem, xv_psum.at(l, b + 1))
            else:
                wait_unit(eng, l, U_XQ - 1)

        def wait_cols(eng, l, done, n, u, m):
            if m == 0:
                eng.wait_ge(done.sem, done.at(l, n + 1))
            else:
                wait_unit(eng, l, u)

        def proj_parts(c, t):
            b = c % 2 * 4 + t
            pairs = proj[:, t, NQ:NQ + 512].rearrange("p (m g d) -> p g m d", g=2, d=HD)
            if c == 1:
                return [(bank(b, 256), proj[:, t, MV:MV + 256]),
                        (bank(b, 256, 256).rearrange("p (m d) -> p m d", d=HD), pairs[:, 0])]
            if c == 2:
                return [(bank(b, 256).rearrange("p (m d) -> p m d", d=HD), pairs[:, 1]),
                        (bank(b, 256, 256).rearrange("p (m d) -> p m d", d=HD).unsqueeze(2).broadcast_to([P, 4, 2, HD]),
                         twice[:, t])]
            return [(bank(b, IN_W[c]), proj[:, t, 512 * c:512 * c + IN_W[c]])]

        CMP_STEPS = [3, 7, 11, 15]

        def pt_bank(i):
            return 3 + i % 3

        def probs(i):
            p = prob[:, i % PROBS, 0:item_keys(i)]
            return p.rearrange("p (h t j) -> p h t j", h=2, j=CMPP) if GROUPS[ITEMS[i][0]][1] == "cmp" else p

        def mem_pieces(b):
            return memT[:, 2 * (b - 18):2 * (b - 18) + 2, :].rearrange("p k m -> p (k m)")

        def down_parts(k, n=1):
            if k < 4:
                return first_hi[:, k:k + n, :], first_lo[:, k:k + n, :]
            return a_hi[:, (k - 4) % KD:(k - 4) % KD + n, :], a_lo[:, (k - 4) % KD:(k - 4) % KD + n, :]

        block = ctx.enter_context(nc.Block())

        @block.sync
        def _(sp):
            sp.dma_start(h[:], x[0].rearrange("(t p) d -> p t d", p=P)).then_inc(pro_x, 16)
            sp.wait_ge(pro_pool, 8)
            with sp.Fori(0, DEPTH) as l:
                g = 0
                for vec in (norm_mix_pre, norm_x_pre, norm_mem, norm_ffn_pre):
                    sp.dma_start(vec_a[g:g + 8, :], vec[l].rearrange("(k p) -> k p", p=P)).then_inc(vecs_landed.sem, 16)
                    g += 8
                for vec in (cmp_pe_k, cmp_pe_v):
                    sp.dma_start(vec_a[g:g + 16, :], vec[l].rearrange("(q a) d -> q (a d)", a=2)).then_inc(vecs_landed.sem, 16)
                    g += 16
                sp.dma_start(vec_b[0:66, :], ffn_conv_w[l].rearrange("w (f p) -> (w f) p", p=P)).then_inc(vecs_landed.sem, 16)
                sp.dma_start(vec_b[66:88, :], ffn_conv_b[l].rearrange("(f p) -> f p", p=P)).then_inc(vecs_landed.sem, 16)
                for u in range(UNITS):
                    sp.wait_ge(lo_made.sem, l * 2 * UNITS + 2 * (u + 1))
                    sp.dma_start(unit_view(raw, u), unit_source(l, u)).then_inc(raw_landed[u % RING], 16)
            sp.wait_ge(h_done.sem, h_done.at(DEPTH, 0))
            sp.dma_start(out[0].rearrange("(t p) d -> p t d", p=P), h[:]).then_inc(stored, 16)
            sp.wait_ge(stored, 16)

        @block.gpsimd
        def _(pool):
            def link(ins, n):
                ins.then_inc(pro_pool, 1)
                pool.wait_ge(pro_pool, n)
            link(pool.memset(stage[:, 0:4, :], 0.0), 1)
            pool.memset(vec_rows[:], 0.0).then_inc(pro_pool, 1)
            pool.memset(ident[:], 0.0).then_inc(pro_pool, 1)
            pool.memset(strict_mul[:], 1.0).then_inc(pro_pool, 1)
            pool.memset(neg_tri[:], -1.0).then_inc(pro_pool, 1)
            pool.memset(neg_ones[:], -1.0).then_inc(pro_pool, 1)
            pool.memset(kcT[:], 0.0).then_inc(pro_pool, 1)
            link(pool.memset(cmp_valid[:], 1.0), 8)
            pool.affine_select(out=ident[:], in_=ident[:], compare_op=ALU.not_equal, fill=1.0, base=0,
                               pattern=[[-1, P]], channel_multiplier=1).then_inc(pro_pool, 1)
            pool.affine_select(out=stage[:, 1, :], in_=stage[:, 1, :], compare_op=ALU.is_ge, fill=NEG, base=0,
                               pattern=[[-1, P]], channel_multiplier=1).then_inc(pro_pool, 1)
            pool.affine_select(out=stage[:, 2, :], in_=stage[:, 2, :], compare_op=ALU.is_ge, fill=NEG, base=-1,
                               pattern=[[1, P]], channel_multiplier=-1).then_inc(pro_pool, 1)
            pool.affine_select(out=stage[:, 3, :].rearrange("p (t j) -> p t j", t=T),
                               in_=stage[:, 3, :].rearrange("p (t j) -> p t j", t=T),
                               compare_op=ALU.is_ge, fill=NEG, base=-31,
                               pattern=[[P, T], [-16, CMPP]], channel_multiplier=1).then_inc(pro_pool, 1)
            pool.affine_select(out=strict_mul[:], in_=strict_mul[:], compare_op=ALU.is_ge, fill=0.0, base=-1,
                               pattern=[[1, P]], channel_multiplier=-1).then_inc(pro_pool, 1)
            pool.affine_select(out=neg_tri[:], in_=neg_tri[:], compare_op=ALU.is_ge, fill=0.0, base=0,
                               pattern=[[-1, P]], channel_multiplier=1).then_inc(pro_pool, 1)
            link(pool.affine_select(out=cmp_valid[:], in_=cmp_valid[:], compare_op=ALU.is_ge, fill=0.0, base=-31,
                                    pattern=[[P, T]], channel_multiplier=1), 15)
            pool.tensor_copy(ident_r[:], ident[:]).then_inc(pro_pool, 1)
            pool.tensor_copy(causal[:], stage[:, 1, :]).then_inc(pro_pool, 1)
            pool.tensor_copy(strictT[:], stage[:, 2, :]).then_inc(pro_pool, 1)
            pool.tensor_copy(cmp_mask[:].rearrange("p t j -> p (t j)"), stage[:, 3, :]).then_inc(pro_pool, 1)
            pool.wait_ge(pro_pool, 19)
            pool.memset(nt[:, 0:1], 0.0).then_inc(lo_made.sem, 2 * RING)
            pool.memset(nt[:, 1:2], 0.0).then_inc(unit_used.sem, RING)
            pool.memset(den[:], 0.0).then_inc(pro_const, 1)
            with pool.Fori(0, DEPTH) as l:
                def add_output(post):
                    for t in range(T - 1):
                        pool.wait_ge(normed.sem, normed.at(l, (T - 1) * (post - 1) + t + 1))
                        inc(pool.tensor_tensor(h[:, t, :], h[:, t, :], rows[:, t, :], ALU.add), h_done)

                for u in range(UNITS):
                    if u == U_UP + 1:
                        add_output(1)
                    n = unit_width(u) // 2
                    for half in range(2):
                        pool.wait_ge(hi_made.sem, hi_made.at(l, 2 * u + half + 1))
                        inc(pool.tensor_tensor(w_lo[:, u % RING, n * half:n * half + n], raw[:, u % RING, n * half:n * half + n],
                                               w_hi[:, u % RING, n * half:n * half + n].bitcast(F32), ALU.subtract), lo_made)
                add_output(2)

        @block.scalar
        def _(act):
            count = [0]

            def link(ins):
                count[0] += 1
                ins.then_inc(act_chain, 1)
                act.wait_ge(act_chain, count[0])

            def rms_estimate(src, junk, c, done):
                link(act.activation(junk, src, ACT.Square, accum_out=sums[:, c:c + 1]))
                link(act.activation(est[:, c:c + 1], sums[:, c:c + 1], ACT.Ln, scale=1.0 / D, bias=eps_t[:]))
                inc(act.activation(est[:, c:c + 1], est[:, c:c + 1], ACT.Exp, scale=-0.5), done)

            act.dma_start(pos_i[:, 0:4], positions.rearrange("b (t p) -> p (b t)", p=P), allow_slow_non_contiguous=True).then_inc(pro_pos, 16)
            act.wait_ge(pro_dve, 1)
            act.dma_start(pos_i[0:NCMP, 4:5],
                          positions[:, 16:S].rearrange("b (j c) -> (b j) c", c=16)[:, 15:16], allow_slow_non_contiguous=True).then_inc(pro_pos, 16)
            act.wait_ge(pro_rope, 1)
            act.activation(sin_t[:].rearrange("p a b -> p (a b)"), ang[:, 0, :], ACT.Sin).then_inc(pro_act, 1)
            act.activation(cos_t[:].rearrange("p a b -> p (a b)"), ang[:, 1, :], ACT.Sin).then_inc(pro_act, 1)
            act.wait_ge(pro_act, 2)
            act.wait_ge(pro_x, 16)
            act.wait_ge(pro_const, 1)

            act.preload_act_table_set("natural_log_exp_and_others")
            with act.Fori(0, DEPTH) as l:
                next_unit = [0]

                def cast_to(n):
                    while next_unit[0] < min(n, UNITS):
                        u = next_unit[0]
                        n_half = unit_width(u) // 2
                        act.wait_ge(raw_landed[u % RING], l * (16 * UNITS // RING) + 16 * (u // RING + 1))
                        act.wait_ge(unit_used.sem, l * UNITS + (u + 1))
                        for first in (0, n_half):
                            inc(act.activation(w_hi[:, u % RING, first:first + n_half], raw[:, u % RING, first:first + n_half], ACT.Copy), hi_made)
                        next_unit[0] += 1

                for i, n in enumerate((64, 88)):
                    act.wait_ge(vecs_T.sem, vecs_T.at(l, i + 1))
                    inc(act.activation(vecs[:, 64 * i:64 * i + n], bank(i, n), ACT.Copy), vecs_ready)
                act.wait_ge(vecs_ready.sem, vecs_ready.at(l, 2))
                cast_to(2)

                def hi_parts(inst, gain, pieces=range(KD)):
                    for k in pieces:
                        act.wait_ge(aT_psum.sem, aT_psum.at(l, KD * inst + k + 1))
                        inc(act.activation(a_hi[:, k, :], bank(aT_bank(inst, k)), ACT.Copy, scale=vecs[:, gain + k:gain + k + 1]), aT_hi)

                def post_and_pre(post, pre, casts=(0, 0, 0, 0, 0)):
                    for t in range(T + 1):
                        cast_to(casts[t])
                        if t < T:
                            wait_out(act, l, post, t)
                            rms_estimate(banks[:, 1024 * t:1024 * t + 1024], rows[:, t, :], 12 + T * post + t, post_est)
                        if pre is not None and t:
                            act.wait_ge(h_done.sem, h_done.at(l, T * post + t))
                            rms_estimate(h[:, t - 1, :], rows[:, t - 1, :], T * pre + t - 1, pre_est)

                act.wait_ge(h_done.sem, h_done.at(l, 0))
                act.dma_start(mem_rows[:], mem[0].rearrange("(t p) d -> p t d", p=P)).then_inc(mem_landed.sem, 16)
                hi_parts(0, 0)
                for t in range(T):
                    rms_estimate(h[:, t, :], rows[:, t, :], t, pre_est)
                act.wait_ge(mem_landed.sem, mem_landed.at(l, 16))
                for t in range(2):
                    rms_estimate(mem_rows[:, t, :], squares[:], 32 + t, mem_est)

                for c in range(6):
                    cast_to(2 * c + 3)
                    for t in (0, 1):
                        wait_proj(act, l, c, t)
                        if c == 0 and t == 0:
                            act.wait_ge(pre_rstd.sem, pre_rstd.at(l, 1))
                        for src, dst in proj_parts(c, t):
                            ins = act.activation(dst, src, ACT.Copy, scale=rstd[:, t:t + 1])
                        inc(ins, proj_act)
                    cast_to(2 * c + 4)
                act.wait_ge(proj_act.sem, proj_act.at(l, 12))
                act.wait_ge(proj_dve.sem, proj_dve.at(l, 12))
                inc(act.activation(gates[:], proj[:, :, NG:NG + 24], ACT.Exp, scale=-1.0), gated)
                act.wait_ge(blk_psum.sem, blk_psum.at(l, 4))
                for i, w in enumerate((cmp_wk2, cmp_wv2)):
                    act.dma_start(w2[:, i], w[l].rearrange("(c p) n -> p c n", p=P)).then_inc(w2_landed.sem, 16)

                for b in range(4, 22, 2):
                    cast_to(U_CMP + (3 if b < 12 else 4))
                    act.wait_ge(blk_psum.sem, blk_psum.at(l, b + 1))
                    i = b - 4
                    dst = qT[:, i, :] if i < 8 else kT[:, i - 8, :] if i < 14 else mem_pieces(b)
                    inc(act.activation(dst, bank(blk_bank(b)), ACT.Copy, scale=HD ** -0.5 if i < 8 else 1.0), blk_act)
                for i in range(2):
                    wait_unit(act, l, U_CMP + 2 * i + 1)
                    inc(act.activation(cg[0:62, i, :], bank(1 + 2 * i, 256, 0, 62), ACT.Gelu_apprx_tanh), cmp_gelu)

                act.preload_act_table_set("natural_log_exp_and_others")

                def copy_o(m, done, n):
                    act.wait_ge(done.sem, done.at(l, n))
                    inc(act.activation(oT[:, m, :], bank(6 + m % 2), ACT.Copy), oT_done)

                def exponentials(i):
                    act.wait_ge(maxed.sem, maxed.at(l, i + 1))
                    if i >= PROBS:
                        act.wait_ge(pT_psum.sem, pT_psum.at(l, i - PROBS + 1))
                    if GROUPS[ITEMS[i][0]][1] == "cmp":
                        inc(act.activation(probs(i), probs(i), ACT.Exp), exped)
                    else:
                        inc(act.activation(probs(i), bank(i % 3, item_keys(i)), ACT.Exp,
                                           bias=neg_max[:, i % 8:i % 8 + 1], accum_out=den[:, i % 8:i % 8 + 1]), exped)

                def copy_T(i):
                    g, t, hp = ITEMS[i]
                    kind = GROUPS[g][1]
                    act.wait_ge(pT_psum.sem, pT_psum.at(l, i + 1))
                    if kind == "cmp":
                        if g >= 6:
                            act.wait_ge(pv.sem, pv.at(l, g - 5))
                        src, dst = bank(pt_bank(i), 2 * P).rearrange("p (h q) -> p h q", h=2), cprobT[:, g // 3 % 2]
                    else:
                        turn = full_groups(g)
                        if turn >= 2:
                            last = max(j for j in range(g) if full_groups(j) == turn - 2 and GROUPS[j][1] != "cmp")
                            act.wait_ge(pv.sem, pv.at(l, last + 1))
                        buf = probT[:, 2 * (turn % 2) + hp, :]
                        src = bank(pt_bank(i), P * (t + 1)).rearrange("p (k q) -> p k q", q=P)
                        dst = buf[:, P * t:P * t + 384 * t + P].rearrange("p (k q) -> p k q", q=P)[:, 0:3 * t + 1:3 if t else 1, :]
                    inc(act.activation(dst, src, ACT.Copy), pT_copied)

                def sb_softplus(hh):
                    src, tmp = banks[:, 1536 * (hh % 2):1536 * (hh % 2) + SB_ALL], sb_tmp[hh][:]
                    act.wait_ge(sb_z.sem, sb_z.at(l, hh + 1))
                    link(act.activation(tmp, src, ACT.Abs))
                    link(act.activation(tmp, tmp, ACT.Exp, scale=-1.0))
                    inc(act.activation(tmp, tmp, ACT.Ln, bias=1.0), sb_l)

                def o_parts(j):
                    inc(act.activation(a_hi[:, 2 * j:2 * j + 2, :], oT[:, 2 * j:2 * j + 2, :], ACT.Copy), o_hi)

                def sb_exp(hh):
                    act.wait_ge(sb_log.sem, sb_log.at(l, hh + 1))
                    inc(act.activation(sb_tmp[hh][:], banks[:, 1536 * (hh % 2):1536 * (hh % 2) + SB_ALL], ACT.Exp), sb_prob)

                for i in range(STEPS + 1):
                    if i < NI:
                        exponentials(i)
                    if i in (8, 16):
                        cast_to(U_OUT + i // 8)
                    if 0 <= i - LAG_COPY < NI:
                        copy_T(i - LAG_COPY)
                    if i == NI + LAG_COPY - 1:
                        sb_softplus(0)
                    for step, g, k in PIECES:
                        if step == i - 1 and k == T - 1 and GROUPS[g][1] in ("moba", "win"):
                            copy_o(GROUPS[g][0], pv, g + 1)

                sb_softplus(1)
                sb_exp(0)
                sb_softplus(2)
                sb_exp(1)
                sb_softplus(3)
                sb_exp(2)
                act.wait_ge(sb_z.sem, sb_z.at(l, 4))
                act.wait_ge(oT_done.sem, oT_done.at(l, 6))
                o_parts(0)
                o_parts(1)
                copy_o(6, sb_pv, 1)
                sb_exp(3)
                o_parts(2)
                copy_o(7, sb_pv, 2)
                act.wait_ge(oT_done.sem, oT_done.at(l, 8))
                o_parts(3)
                act.dma_start(gain_row[:], row_broadcast(norm_mix_post, l)).then_inc(gain_landed[0].sem, 16)
                for k in range(KD):
                    inc(act.activation(m_hi[:, k, :], memT[:, k, :], ACT.Copy, scale=vecs[:, 16 + k:17 + k]), mT_hi)
                cast_to(U_OUT + 4)
                post_and_pre(0, 1, (U_XK + 1, U_XK + 1, U_XK + 1, U_XK + 2, U_XK + 3))
                cast_to(U_XQ + 1)
                hi_parts(1, 8, range(4))
                for b in range(4):
                    wait_xv(act, l, b)
                    inc(act.activation(xv[:, b // 2, 512 * (b % 2):512 * (b % 2) + 512], bank(4 + b), ACT.Copy), xv_ready)
                hi_parts(1, 8, range(4, KD))
                cast_to(U_XQ + 2)
                act.dma_start(gain_row[:], row_broadcast(norm_x_post, l)).then_inc(gain_landed[1].sem, 16)
                cast_to(U_XO + 2)
                def copy_xT(i):
                    head, t = divmod(i, 4)
                    act.wait_ge(xpT_psum.sem, xpT_psum.at(l, i + 1))
                    if head >= 2:
                        act.wait_ge(xo_psum.sem, xo_psum.at(l, 2 * head - 2))
                    inc(act.activation(xprobT[:, head % 2, :, P * t:P * t + P],
                                       bank(3 + i % 2, MEM).rearrange("p (m q) -> p m q", m=2), ACT.Copy), xpT_ready)

                for i in range(XSTEPS + 1):
                    if i < 16:
                        act.wait_ge(xmaxed.sem, xmaxed.at(l, i + 1))
                        if i >= PROBS:
                            act.wait_ge(xpT_psum.sem, xpT_psum.at(l, i - PROBS + 1))
                        inc(act.activation(xprob[:, i % PROBS, :], bank(i % 3, MEM), ACT.Exp,
                                           bias=neg_max[:, i % 8:i % 8 + 1], accum_out=den[:, i % 8:i % 8 + 1]), xexped)
                    if 0 <= i - XLAG_T < 16:
                        copy_xT(i - XLAG_T)
                    if i - 1 in XPIECES:
                        j = XPIECES[i - 1]
                        act.wait_ge(xo_psum.sem, xo_psum.at(l, j + 1))
                        inc(act.activation(a_hi[:, j, :], bank(5 + j % 3), ACT.Copy), xo_hi)
                act.wait_ge(xo_psum.sem, xo_psum.at(l, 8))
                act.dma_start(gain_row_ffn[:], row_broadcast(norm_ffn_post, l)).then_inc(gain_landed[2].sem, 16)
                cast_to(U_XO + 4)
                post_and_pre(1, 2, (U_UP + 1,) * (T + 1))
                cast_to(U_UP + 2)
                hi_parts(2, 24)

                def g_parts(i):
                    k = down_pieces(i)
                    act.wait_ge(gT_done.sem, gT_done.at(l, k[-1] + 1))
                    if i >= 2:
                        act.wait_ge(unit_used.sem, unit_used.at(l, U_DOWN if i < 6 else U_DOWN + (k[-1] - 8) // 2 + 1))
                    inc(act.activation(down_parts(k[0], len(k))[0], gT[:, k[0]:k[-1] + 1, :], ACT.Copy), g_hi)

                for f in range(NF):
                    cast_to(min(U_UP + f + 3, U_DOWN + 1))
                    act.wait_ge(conved.sem, conved.at(l, f + 1))
                    if f >= 3:
                        act.wait_ge(gT_done.sem, gT_done.at(l, f - 2))
                    inc(act.activation(gel[:, f % 3, :], conv[:, f % 3, :], ACT.Gelu_apprx_tanh,
                                       bias=vecs[:, 130 + f:131 + f]), gelued)
                    if f in (12, 14):
                        g_parts((f - 12) // 2)
                act.preload_act_table_set("natural_log_exp_and_others")
                for i in range(2, 12):
                    g_parts(i)
                    cast_to(U_DOWN + i + 1)
                post_and_pre(2, None)
                act.sem_clear(act_chain)
                count[0] = 0

        @block.vector
        def _(dve):
            count = [0]

            def link(ins):
                count[0] += 1
                ins.then_inc(dve_chain, 1)
                dve.wait_ge(dve_chain, count[0])

            dve.memset(eps_t[:], EPS)
            dve.memset(pos_i[:, 4:5], 0).then_inc(pro_dve, 1)
            dve.wait_ge(pro_pos, 32)
            link(dve.tensor_copy(pos_f[:], pos_i[:]))
            for j in range(8):
                freq = float(np.float32(500000.0) ** np.float32(-j / 8))
                ins = dve.tensor_scalar(ang[:, 0, :].rearrange("p (t j) -> p t j", j=8)[:, :, j], pos_f[:], freq, None, ALU.mult)
            link(ins)
            link(dve.tensor_copy(ang[:, 1, :], ang[:, 0, :]))
            inv = float(1 / (2 * np.pi))
            link(dve.tensor_scalar(turns[:, 0, :], ang[:, 0, :], inv, None, ALU.mult))
            link(dve.tensor_scalar(turns[:, 1, :], ang[:, 0, :], inv, 0.25, ALU.mult, ALU.add))
            big = 12582912.0
            link(dve.tensor_scalar(turns[:], turns[:], big, None, ALU.add))
            link(dve.tensor_scalar(turns[:], turns[:], big, None, ALU.subtract))
            c1 = 6.28125
            c2 = float(np.float32(round((2 * np.pi - c1) * 2 ** 19) / 2 ** 19))
            c3 = float(2 * np.pi - c1 - c2)
            for c in (c1, c2, c3):
                link(dve.scalar_tensor_tensor(ang[:], turns[:], -c, ang[:], ALU.mult, ALU.add))
            link(dve.tensor_scalar(ang[:, 1, :], ang[:, 1, :], float(np.pi / 2), None, ALU.add))
            dve.tensor_scalar(ang[:], ang[:], 3.1415925, -3.1415925, ALU.min, ALU.max).then_inc(pro_rope, 1)
            dve.wait_ge(pro_act, 2)
            dve.wait_ge(pro_x, 16)
            dve.wait_ge(pro_const, 1)

            def newton(c, n=1, step=1):
                s, e, y = (v[:, c:c + step * (n - 1) + 1:step] for v in (sums, est, rstd))
                link(dve.tensor_scalar(s, s, -0.5 / D, -0.5 * EPS, ALU.mult, ALU.add))
                link(dve.tensor_tensor(y, e, e, ALU.mult))
                link(dve.tensor_tensor(y, y, s, ALU.mult))
                return dve.scalar_tensor_tensor(y, y, 1.5, e, ALU.add, ALU.mult)

            def rope(dst, cs, sn, tmp):
                x1, x2 = dst[..., 0:8], dst[..., 8:16]
                dve.tensor_tensor(tmp[0], x1, cs, ALU.mult)
                dve.tensor_tensor(tmp[1], x2, sn, ALU.mult)
                dve.tensor_tensor(tmp[2], x2, cs, ALU.mult)
                link(dve.tensor_tensor(tmp[3], x1, sn, ALU.mult))
                dve.tensor_tensor(x1, tmp[0], tmp[1], ALU.subtract)
                return dve.tensor_tensor(x2, tmp[2], tmp[3], ALU.add)

            dve.sem_clear(dve_chain)
            count[0] = 0
            dve.memset(sums[:], 0.0).then_inc(h_done.sem, T)
            with dve.Fori(0, DEPTH) as l:
                def lo_parts(inst, gain):
                    for k in range(KD):
                        dve.wait_ge(aT_hi.sem, aT_hi.at(l, KD * inst + k + 1))
                        inc(dve.scalar_tensor_tensor(a_lo[:, k, :], bank(aT_bank(inst, k)), vecs[:, gain + k:gain + k + 1],
                                                     a_hi[:, k, :].bitcast(F32), ALU.mult, ALU.subtract), aT_lo)

                def post_and_pre(post, pre, gain):
                    def pre_rows(t):
                        inc(dve.tensor_scalar(rows[:, t, :], h[:, t, :], rstd[:, T * pre + t:T * pre + t + 1], None, ALU.mult), rows_done)

                    dve.wait_ge(gain_landed[post].sem, gain_landed[post].at(l, 16))
                    first = 12 + T * post
                    dve.wait_ge(post_est.sem, post_est.at(l, T * post + 1))
                    link(newton(first))
                    for t in range(T):
                        ins = dve.scalar_tensor_tensor(rows[:, t, :], banks[:, 1024 * t:1024 * t + 1024], rstd[:, first + t:first + t + 1],
                                                       gain[:], ALU.mult, ALU.mult)
                        if post and t < T - 1:
                            inc(ins, normed)
                        else:
                            link(ins)
                            if post:
                                dve.wait_ge(h_done.sem, h_done.at(l, T * post + t))
                            inc(dve.tensor_tensor(h[:, t, :], h[:, t, :], rows[:, t, :], ALU.add), h_done)
                        if t < T - 1:
                            dve.wait_ge(post_est.sem, post_est.at(l, T * post + t + 2))
                        if pre is not None and t:
                            dve.wait_ge(pre_est.sem, pre_est.at(l, T * pre + t))
                            assert T * pre + t - 1 + 10 == first + t + 1
                        columns = [first + t + 1] * (t < T - 1) + [T * pre + t - 1 if pre else 0] * (pre is not None and t > 0)
                        if columns:
                            link(newton(min(columns), len(columns), 10))
                        if pre is not None and t:
                            pre_rows(t - 1)
                    if pre is not None:
                        dve.wait_ge(pre_est.sem, pre_est.at(l, T * pre + T))
                        link(newton(T * pre + T - 1))
                        pre_rows(T - 1)

                dve.wait_ge(vecs_ready.sem, vecs_ready.at(l, 2))
                lo_parts(0, 0)
                dve.wait_ge(pre_est.sem, pre_est.at(l, T))
                inc(newton(0, T), pre_rstd)
                dve.wait_ge(pre_rstd.sem, pre_rstd.at(l, 1))
                dve.wait_ge(mem_est.sem, mem_est.at(l, 2))
                link(newton(32, 2))
                for t in range(2):
                    inc(dve.tensor_scalar(mem_rows[:, t, :], mem_rows[:, t, :], rstd[:, 32 + t:33 + t], None, ALU.mult), mem_normed)

                def rope_heads(col, n, table_heads):
                    dve.wait_ge(proj_act.sem, proj_act.at(l, 2 * ((col + 64 * n - 1) // 512) + 2))
                    dst = proj[:, :, col:col + 64 * n].rearrange("p t (m d) -> p t m d", d=HD)
                    shape = [P, T, n, 8]
                    cs = cos_t[:, 0:4, :].unsqueeze(2).broadcast_to(shape)
                    sn = sin_t[:, 0:4, :].unsqueeze(2).broadcast_to(shape)
                    tmp = [rope_tmp[:, i, 0:T * n * 8].rearrange("p (t m d) -> p t m d", t=T, d=8) for i in range(4)]
                    inc(rope(dst, cs, sn, tmp), roped)
                    dve.wait_ge(roped.sem, roped.at(l, table_heads))

                def compressor_operand(i):
                    dve.wait_ge(blk_psum.sem, blk_psum.at(l, 4))
                    for g in range(2):
                        for a in range(2):
                            pp = slice(64 * a, 64 * a + 64)
                            src = banks[pp, 512 * (2 * i + g):512 * (2 * i + g) + 512].rearrange("p (j r) -> p r j", r=16)
                            dst = xb[i][pp, :].rearrange("p (q g j) -> p q g j", q=16, g=2)
                            for half in range(2):
                                q = slice(8 * half, 8 * half + 8)
                                pe = vecs[pp, 32 + 16 * i + 8 * half:40 + 16 * i + 8 * half].unsqueeze(2).broadcast_to([64, 8, NCMP])
                                ins = dve.tensor_tensor(dst[:, q, g, :], src[:, a:16:2, half:half + NCMP], pe, ALU.add)
                    link(ins)
                    link(dve.tensor_copy(xb_hi[i][:], xb[i][:]))
                    inc(dve.tensor_tensor(xb_lo[i][:], xb[i][:], xb_hi[i][:].bitcast(F32), ALU.subtract), xb_ready)

                for c in range(6):
                    if c == 5:
                        compressor_operand(0)
                    for t in (2, 3):
                        wait_proj(dve, l, c, t)
                        for src, dst in proj_parts(c, t):
                            ins = dve.tensor_scalar(dst, src, rstd[:, t:t + 1], None, ALU.mult)
                        inc(ins, proj_dve)
                    dve.wait_ge(proj_dve.sem, proj_dve.at(l, 2 * c + 2))
                    if c == 0:
                        rope_heads(MQ, 8, 1)
                    if c == 2:
                        rope_heads(NQ, 8, 2)
                    if c == 3:
                        rope_heads(NKS, 2, 3)
                        rope_heads(NKW, 2, 4)
                compressor_operand(1)
                for b in range(5, 22, 2):
                    dve.wait_ge(blk_psum.sem, blk_psum.at(l, b + 1))
                    j = b - 4
                    if j < 8:
                        inc(dve.tensor_scalar(qT[:, j, :], bank(blk_bank(b)), HD ** -0.5, None, ALU.mult), blk_dve)
                    else:
                        inc(dve.tensor_copy(kT[:, j - 8, :] if j < 14 else mem_pieces(b), bank(blk_bank(b))), blk_dve)
                dve.wait_ge(gated.sem, gated.at(l, 1))
                link(dve.tensor_scalar(gates[:], gates[:], 1.0, None, ALU.add))
                link(dve.reciprocal(gates[:], gates[:]))
                link(dve.tensor_tensor(cmp_gates[:], gates[:].rearrange("p t (h c) -> p t h c", c=3)[:, :, :, 0],
                                       cmp_valid[:].unsqueeze(2).broadcast_to([P, T, 8]), ALU.mult))

                def compressed(step):
                    i, part = divmod(step, 2)
                    if part == 0:
                        dve.wait_ge(cgT_psum.sem, cgT_psum.at(l, i + 1))
                        if i:
                            dve.wait_ge(kcT_psum.sem, kcT_psum.at(l, 1))
                            inc(dve.tensor_copy(kcT[:, 0:NCMP], bank(7, NCMP, 384)), kcT_ready)
                        src = bank(7, 256).rearrange("p (c j) -> p c j", c=2)[:, :, 0:62].rearrange("p c (g j) -> p c g j", g=2)
                        if i == 0:
                            dve.memset(cgT[:, :, :, :, NCMP:CMPP], 0.0)
                        for c in range(2):
                            ins = dve.tensor_copy(cgT[:, c, :, :, 0:NCMP], src[:, c].unsqueeze(2).broadcast_to([P, 2, T, NCMP]))
                        inc(ins, cgT_ready)
                    else:
                        dve.wait_ge(cmp2_psum.sem, cmp2_psum.at(l, i + 1))
                        src = bank(7, 128, 256).rearrange("p (g d) -> p g d", g=2)
                        if i == 0:
                            link(dve.tensor_copy(kc_rows[0:NCMP], src[0:NCMP]))
                            shape = [NCMP, 2, 8]
                            cs = cos_t[0:NCMP, 4:5, :].broadcast_to(shape)
                            sn = sin_t[0:NCMP, 4:5, :].broadcast_to(shape)
                            tmp = [rope_tmp2[0:NCMP, j, :].rearrange("p (g d) -> p g d", g=2) for j in range(4)]
                            inc(rope(kc_rows[0:NCMP], cs, sn, tmp), kc_roped)
                        else:
                            link(dve.memset(vc_tiles[:], 0.0))
                            for t in range(T):
                                pp = slice(CMPP * t, CMPP * t + CMPP)
                                ins = dve.tensor_copy(vc_tiles[pp, t], src[pp])
                            inc(ins, vc_ready)

                def row_max(i):
                    dve.wait_ge(qk.sem, qk.at(l, i + 1))
                    if GROUPS[ITEMS[i][0]][1] == "cmp":
                        src = bank(i % 3, item_keys(i)).rearrange("p (h t j) -> p h t j", h=2, j=CMPP)
                        if i >= PROBS:
                            dve.wait_ge(pT_psum.sem, pT_psum.at(l, i - PROBS + 1))
                        link(dve.tensor_reduce(c_max[:], src, AX.X, ALU.max))
                        inc(dve.tensor_tensor(probs(i), src, c_max[:].unsqueeze(3).broadcast_to([P, 2, T, CMPP]), ALU.subtract), maxed)
                    else:
                        inc(dve.tensor_reduce(neg_max[:, i % 8:i % 8 + 1], bank(i % 3, item_keys(i)), AX.X, ALU.max, negate=True), maxed)

                def row_sum(i):
                    g = ITEMS[i][0]
                    m, kind = GROUPS[g]
                    dve.wait_ge(exped.sem, exped.at(l, i + 1))
                    if kind == "cmp":
                        link(dve.tensor_reduce(c_den[:], probs(i), AX.X, ALU.add))
                        link(dve.reciprocal(c_den[:], c_den[:]))
                        ins = dve.tensor_tensor(c_den[:], c_den[:], cmp_gates[:, :, 2 * m - 4:2 * m - 2].rearrange("p t h -> p h t"), ALU.mult)
                    else:
                        ins = dve.reciprocal(rden[:, i % 8:i % 8 + 1], den[:, i % 8:i % 8 + 1])
                    count[0] += 1
                    ins.then_inc(dve_chain, 1)

                def scale(i, sum_made):
                    g, t, hp = ITEMS[i]
                    m, kind = GROUPS[g]
                    dve.wait_ge(dve_chain, sum_made)
                    if kind == "cmp":
                        ins = dve.tensor_tensor(probs(i), probs(i), c_den[:].unsqueeze(3).broadcast_to([P, 2, T, CMPP]), ALU.mult)
                    elif kind == "moba":
                        ins = dve.tensor_scalar(probs(i), probs(i), rden[:, i % 8:i % 8 + 1], None, ALU.mult)
                    else:
                        c = 3 * (2 * m + hp - 4) + (1 if kind == "sel" else 2)
                        ins = dve.tensor_scalar(probs(i), probs(i), rden[:, i % 8:i % 8 + 1], gates[:, t, c:c + 1], ALU.mult, ALU.mult)
                    inc(ins, scaled)

                for i in range(NI + LAG_SCALE):
                    if i >= LAG_SCALE:
                        row_sum(i - LAG_SCALE)
                        sum_made = count[0]
                    if i < NI:
                        row_max(i)
                    if i >= LAG_SCALE:
                        scale(i - LAG_SCALE, sum_made)
                    if i in CMP_STEPS:
                        compressed(CMP_STEPS.index(i))

                for hh in range(4):
                    dve.wait_ge(sb_l.sem, sb_l.at(l, hh + 1))
                    if hh == 0:
                        dve.wait_ge(pv.sem, pv.at(l, len(GROUPS) - 2))
                    if hh >= 2:
                        dve.wait_ge(sb_log.sem, sb_log.at(l, hh - 1))
                    sp = sb_sp[:, hh % 2, :]
                    link(dve.scalar_tensor_tensor(sp, banks[:, 1536 * (hh % 2):1536 * (hh % 2) + SB_ALL], 0.0,
                                                  sb_tmp[hh][:], ALU.max, ALU.add))
                    for k in range(T):
                        s = slice(SB_OFF[k], SB_OFF[k] + P)
                        ins = dve.tensor_tensor(sp[:, s], sp[:, s], strict_mul[:], ALU.mult)
                    inc(ins, sb_masked)
                for j in range(4):
                    dve.wait_ge(o_hi.sem, o_hi.at(l, j + 1))
                    inc(dve.tensor_tensor(a_lo[:, 2 * j:2 * j + 2, :], oT[:, 2 * j:2 * j + 2, :],
                                          a_hi[:, 2 * j:2 * j + 2, :].bitcast(F32), ALU.subtract), o_lo)
                for k in range(KD):
                    dve.wait_ge(mT_hi.sem, mT_hi.at(l, k + 1))
                    inc(dve.scalar_tensor_tensor(m_lo[:, k, :], memT[:, k, :], vecs[:, 16 + k:17 + k],
                                                 m_hi[:, k, :].bitcast(F32), ALU.mult, ALU.subtract), mT_lo)
                post_and_pre(0, 1, gain_row)

                for u in range(4):
                    wait_unit(dve, l, U_XK + u)
                    inc(dve.tensor_copy(xkT[:, 2 * u:2 * u + 2, :].rearrange("p a m -> p (a m)"), bank(u)), xk_ready)
                lo_parts(1, 8)
                for m in range(KD):
                    wait_cols(dve, l, xq_psum, m // 2, U_XQ + m // 2, m % 2)
                    inc(dve.tensor_scalar(xqT[:, m, :], bank(4 + m % 4), 256 ** -0.5, None, ALU.mult), xq_ready)

                def xscale(i):
                    dve.wait_ge(xexped.sem, xexped.at(l, i + 1))
                    r = rden[:, i % 8:i % 8 + 1]
                    link(dve.reciprocal(r, den[:, i % 8:i % 8 + 1]))
                    inc(dve.tensor_scalar(xprob[:, i % PROBS, :], xprob[:, i % PROBS, :], r, None, ALU.mult), xscaled)

                for i in range(XSTEPS + 1):
                    if i < 16:
                        dve.wait_ge(xs.sem, xs.at(l, i + 1))
                        inc(dve.tensor_reduce(neg_max[:, i % 8:i % 8 + 1], bank(i % 3, MEM), AX.X, ALU.max, negate=True), xmaxed)
                    if 1 <= i <= 16:
                        xscale(i - 1)
                    if i - 1 in XPIECES:
                        j = XPIECES[i - 1]
                        dve.wait_ge(xo_hi.sem, xo_hi.at(l, j + 1))
                        inc(dve.tensor_tensor(a_lo[:, j, :], bank(5 + j % 3), a_hi[:, j, :].bitcast(F32), ALU.subtract), xo_lo)
                post_and_pre(1, 2, gain_row)
                lo_parts(2, 24)

                def g_rest(i):
                    dve.wait_ge(g_hi.sem, g_hi.at(l, i + 1))
                    k = down_pieces(i)
                    part_hi, part_lo = down_parts(k[0], len(k))
                    inc(dve.tensor_tensor(part_lo, gT[:, k[0]:k[-1] + 1, :], part_hi.bitcast(F32), ALU.subtract), g_lo)

                def gate(f):
                    dve.wait_ge(gelued.sem, gelued.at(l, f + 1))
                    jp, b = divmod(f, 2)
                    wait_cols(dve, l, up_psum, 2 * jp + 1, U_UP + 2 * jp + 1, b)
                    inc(dve.tensor_tensor(gT[:, f, :], gel[:, f % 3, :], bank(up_bank(jp, 1) + b), ALU.mult), gT_done)

                for f in range(NF + 1):
                    if f < NF:
                        jp, b = divmod(f, 2)
                        src = bank(up_bank(jp, 0) + b)
                        cv = conv[:, f % 3, :]
                        wait_cols(dve, l, up_psum, 2 * jp, U_UP + 2 * jp, b)
                        if f >= 3:
                            dve.wait_ge(gelued.sem, gelued.at(l, f - 2))
                        wcol = lambda i: vecs[:, 64 + 22 * i + f:65 + 22 * i + f]
                        link(dve.tensor_scalar(cv, src, wcol(2), None, ALU.mult))
                        link(dve.scalar_tensor_tensor(cv[:, 1:S], src[:, 0:S - 1], wcol(1), cv[:, 1:S], ALU.mult, ALU.add))
                        inc(dve.scalar_tensor_tensor(cv[:, 2:S], src[:, 0:S - 2], wcol(0), cv[:, 2:S], ALU.mult, ALU.add), conved)
                    if f:
                        gate(f - 1)
                    if f in (12, 14):
                        g_rest((f - 12) // 2)
                for i in range(2, 12):
                    g_rest(i)
                post_and_pre(2, None, gain_row_ffn)
                dve.sem_clear(dve_chain)
                count[0] = 0

        @block.tensor
        def _(pe):
            pe.wait_ge(pro_const, 1)

            def three(dst, st_hi, st_lo, mv_hi, mv_lo, first, last):
                pe.matmul(dst, st_lo, mv_hi, start=first, stop=False)
                pe.matmul(dst, st_hi, mv_lo, start=False, stop=False)
                return pe.matmul(dst, st_hi, mv_hi, start=False, stop=last)

            with pe.Fori(0, DEPTH) as l:
                def unit(u):
                    pe.wait_ge(lo_made.sem, lo_made.at(l, 2 * u + 1))
                    return unit_view(w_hi, u), unit_view(w_lo, u)

                def rest(u):
                    pe.wait_ge(lo_made.sem, lo_made.at(l, 2 * u + 2))

                def transpose_rows(inst, k):
                    if k >= 4:
                        pe.wait_ge(aT_lo.sem, aT_lo.at(l, KD * inst + k - 3))
                    src = (h, rows, rows)[inst]
                    for t in range(T):
                        ins = pe.transpose(bank(aT_bank(inst, k), P, P * t), src[:, t, P * k:P * k + P], ident[:])
                    inc(ins, aT_psum)

                def rows_gemm(first, n_units, post, ready, bank_free=None):
                    for i in range(n_units):
                        hi, lo = unit(first + i)
                        rest(first + i)
                        ready(i)
                        for t in range(T):
                            for n in range(2):
                                if bank_free:
                                    bank_free(i, 2 * t + n)
                                pieces = down_pieces(i)
                                if post < 2:
                                    pieces = [2 * i, 2 * i + 1]
                                for k in range(len(pieces)):
                                    st = slice(P * t, P * t + P)
                                    part_hi, part_lo = down_parts(pieces[k]) if post == 2 else (v[:, pieces[k]:pieces[k] + 1, :] for v in (a_hi, a_lo))
                                    ins = three(bank(2 * t + n), part_hi[:, 0, st], part_lo[:, 0, st],
                                                hi[:, k, 512 * n:512 * n + 512], lo[:, k, 512 * n:512 * n + 512],
                                                i == 0 and k == 0, i == n_units - 1 and k == len(pieces) - 1)
                            if i == n_units - 1 and t < T - 1:
                                inc(ins, out_psum)
                        inc(ins, unit_used)

                pe.wait_ge(vecs_landed.sem, vecs_landed.at(l, 128))
                pe.wait_ge(h_done.sem, h_done.at(l, -3))
                for i, v in enumerate((vec_a, vec_b)):
                    inc(pe.transpose(bank(i, P), v, ident[:]), vecs_T)

                pe.wait_ge(h_done.sem, h_done.at(l, 0))
                for k in range(4):
                    transpose_rows(0, k)
                pe.wait_ge(vecs_ready.sem, vecs_ready.at(l, 2))
                def block_transpose(b, src):
                    for t in range(T):
                        ins = pe.transpose(bank(blk_bank(b), P, P * t), src(t), ident[:])
                    inc(ins, blk_psum)

                for c in range(6):
                    for kh in range(2):
                        u = U_IN + 2 * c + kh
                        if u == U_IN + 11:
                            pe.wait_ge(proj_act.sem, proj_act.at(l, 10))
                            pe.wait_ge(proj_dve.sem, proj_dve.at(l, 10))
                            for b in range(4):
                                block_transpose(b, lambda t: twice[:, t, b].rearrange("p a d -> p (a d)"))
                        hi, lo = unit(u)
                        for t in range(T):
                            if c >= 2 and kh == 0:
                                done = proj_act if t < 2 else proj_dve
                                pe.wait_ge(done.sem, done.at(l, 2 * (c - 2) + t % 2 + 1))
                            for k in range(4):
                                if c == 0 and t == 0 or c == 1 and kh == 0 and t == 0 and k == 0:
                                    pe.wait_ge(aT_lo.sem, aT_lo.at(l, 4 * kh + k + 1 if c == 0 else KD))
                                if c == 0 and t == 0 and kh == 0:
                                    transpose_rows(0, k + 4)
                                if t == 0 and k == 2:
                                    rest(u)
                                a = 4 * kh + k
                                st = slice(P * t, P * t + P)
                                ins = three(bank(c % 2 * 4 + t, IN_W[c]), a_hi[:, a, st], a_lo[:, a, st],
                                            hi[:, k, :], lo[:, k, :], kh == 0 and k == 0, kh == 1 and k == 3)
                            if kh == 1 and t < 3:
                                inc(ins, proj_psum)
                        inc(ins, unit_used)

                def compress(i, kh):
                    pe.wait_ge(xb_ready.sem, xb_ready.at(l, i + 1))
                    hi, lo = unit(U_CMP + 2 * i + kh)
                    for k in range(8):
                        if k == 4:
                            rest(U_CMP + 2 * i + kh)
                        q = 8 * kh + k
                        st = slice(62 * q, 62 * q + 62)
                        ins = three(bank(1 + 2 * i, 256, 0, 62), xb_hi[i][:, st], xb_lo[i][:, st], hi[:, k, :], lo[:, k, :],
                                    q == 0, q == 15)
                    inc(ins, unit_used)

                compress(0, 0)
                pe.wait_ge(proj_act.sem, proj_act.at(l, 12))
                pe.wait_ge(proj_dve.sem, proj_dve.at(l, 12))
                pe.wait_ge(roped.sem, roped.at(l, 4))
                pairs_q = [MQ, MQ + P, NQ, NQ + P, NQ + 2 * P, NQ + 3 * P, SQ, SQ + P]
                pairs_k = [MK, MK + P, SK, SK + P, NKS, NKW]
                for b, col in enumerate(pairs_q + pairs_k, 4):
                    if b == 12:
                        compress(0, 1)
                    if b >= 8:
                        done = blk_act if b % 2 == 0 else blk_dve
                        pe.wait_ge(done.sem, done.at(l, (b - 8) // 2 + 1))
                    block_transpose(b, lambda t: proj[:, t, col:col + P])
                compress(1, 0)
                pe.wait_ge(mem_normed.sem, mem_normed.at(l, 2))
                for b in range(18, 22):
                    done = blk_act if b % 2 == 0 else blk_dve
                    pe.wait_ge(done.sem, done.at(l, (b - 8) // 2 + 1))
                    for k in range(2):
                        for t in range(2):
                            piece = 2 * (b - 18) + k
                            ins = pe.transpose(bank(blk_bank(b), P, MEM * k + P * t), mem_rows[:, t, P * piece:P * piece + P], ident[:])
                    inc(ins, blk_psum)
                compress(1, 1)
                pe.wait_ge(blk_act.sem, blk_act.at(l, 9))
                pe.wait_ge(blk_dve.sem, blk_dve.at(l, 9))

                def compressed(step):
                    i, part = divmod(step, 2)
                    if part == 0:
                        if i:
                            pe.wait_ge(kc_roped.sem, kc_roped.at(l, 1))
                        pe.wait_ge(cmp_gelu.sem, cmp_gelu.at(l, i + 1))
                        for c in range(2):
                            ins = pe.transpose(bank(7, P, P * c), cg[:, i, P * c:P * c + P], ident[:])
                        inc(ins, cgT_psum)
                        if i:
                            inc(pe.transpose(bank(7, NCMP, 384), kc_rows[0:NCMP].rearrange("p g d -> p (g d)"), ident[0:NCMP, 0:NCMP]), kcT_psum)
                    else:
                        pe.wait_ge(w2_landed.sem, w2_landed.at(l, 32))
                        pe.wait_ge(cgT_ready.sem, cgT_ready.at(l, i + 1))
                        for g in range(2):
                            for c in range(2):
                                ins = pe.matmul(bank(7, HD, 256 + HD * g), cgT[:, c, g].rearrange("p n j -> p (n j)"), w2[:, i, c, :],
                                                start=c == 0, stop=c == 1)
                        inc(ins, cmp2_psum)

                def query(m, kind, hp):
                    head = 2 * m + hp
                    return (HD * hp, m) if kind == "moba" else (HD * ((head - 4) // 4), 2 + (head - 4) % 4)

                def scores(i):
                    g, t, hp = ITEMS[i]
                    m, kind = GROUPS[g]
                    n = item_keys(i)
                    if i >= 3:
                        pe.wait_ge(exped.sem, exped.at(l, i - 2))
                    if i == 1:
                        pe.wait_ge(cmp_gelu.sem, cmp_gelu.at(l, 1))
                    if kind == "cmp":
                        if g == GROUPS.index((2, "cmp")):
                            pe.wait_ge(kcT_ready.sem, kcT_ready.at(l, 1))
                        for hp in range(2):
                            pe.matmul(bank(i % 3, P, P * hp), ident_r[:], cmp_mask[:].rearrange("p t j -> p (t j)"),
                                      start=True, stop=False, skip_group_check=True)
                            b0, pair = query(m, kind, hp)
                            for t in range(T):
                                ins = pe.matmul(bank(i % 3, CMPP, P * hp + CMPP * t), qT[b0:b0 + HD, pair, P * t:P * t + P],
                                                kcT[b0:b0 + HD, :], start=False, stop=True, skip_group_check=True)
                        inc(ins, qk)
                    else:
                        b0, pair = query(m, kind, hp)
                        keys = kT[b0:b0 + HD, {"moba": m, "sel": 4, "win": 5}[kind], 0:n]
                        pe.matmul(bank(i % 3, n), qT[b0:b0 + HD, pair, P * t:P * t + P], keys, start=True, stop=False)
                        inc(pe.matmul(bank(i % 3, P, n - P), ident_r[:], causal[:], start=False, stop=True), qk)

                def transposes(i):
                    pe.wait_ge(scaled.sem, scaled.at(l, i + 1))
                    if i >= 3:
                        pe.wait_ge(pT_copied.sem, pT_copied.at(l, i - 2))
                    if i == 0:
                        pe.wait_ge(cmp_gelu.sem, cmp_gelu.at(l, 2))
                    for k in range(item_keys(i) // P):
                        ins = pe.transpose(bank(pt_bank(i), P, P * k), prob[:, i % PROBS, P * k:P * k + P], ident[:])
                    inc(ins, pT_psum)

                def values(g, k):
                    m, kind = GROUPS[g]
                    if k == 0:
                        pe.wait_ge(pT_copied.sem, pT_copied.at(l, LAST[g] + 1))
                        if kind == "cmp" and m == 2:
                            pe.wait_ge(vc_ready.sem, vc_ready.at(l, 1))
                        if kind in ("moba", "sel") and m >= 2:
                            pe.wait_ge(oT_done.sem, oT_done.at(l, m - 1))
                    for hp in range(2):
                        kg = (2 * m + hp - 4) // 4
                        half = slice(HD * hp, HD * hp + HD)
                        if kind == "cmp":
                            for t in range(T):
                                ins = pe.matmul(bank(6 + m % 2, P, P * t)[half], vc_tiles[:, t, kg, :], cprobT[:, g // 3 % 2, hp, :],
                                                start=False, stop=False)
                        else:
                            col = {"moba": MV + HD * (2 * m + hp), "sel": NVS + HD * kg, "win": NVW + HD * kg}[kind]
                            ins = pe.matmul(bank(6 + m % 2, S - P * k, P * k)[half], proj[:, k, col:col + HD],
                                            probT[:, 2 * (full_groups(g) % 2) + hp, PT_STEP * k:PT_STEP * k + S - P * k],
                                            start=kind != "win" and k == 0, stop=kind != "sel" and k == T - 1)
                    if kind == "cmp" or k == T - 1:
                        inc(ins, pv)

                def sb_bank(hh, k, n, at=0):
                    c = 1536 * (hh % 2) + SB_OFF[k] + at
                    return banks[:, c:c + n]

                def sb_scores(hh):
                    b0, pair = 64 * (hh % 2), hh // 2
                    if hh == 0:
                        pe.wait_ge(exped.sem, exped.at(l, NI))
                    if hh == 1:
                        pe.wait_ge(pT_copied.sem, pT_copied.at(l, NI))
                    if hh >= 2:
                        pe.wait_ge(sb_prob.sem, sb_prob.at(l, hh - 1))
                    for k in range(T):
                        ins = pe.matmul(sb_bank(hh, k, SB_W[k]), kT[b0:b0 + HD, 2 + pair, P * k:P * k + P],
                                        qT[b0:b0 + HD, 6 + pair, P * k:S], start=k < 3, stop=True, skip_group_check=True)
                    inc(ins, sb_z)

                for i in range(STEPS):
                    if i < NI:
                        scores(i)
                    if LAG_T <= i < NI + LAG_T:
                        transposes(i - LAG_T)
                    if i == NI + 2:
                        sb_scores(0)
                    if i == NI + LAG_V:
                        sb_scores(1)
                    for step, g, k in PIECES:
                        if step == i:
                            values(g, k)
                    if i in CMP_STEPS:
                        compressed(CMP_STEPS.index(i))

                def sb_logs(hh):
                    sp = sb_sp[:, hh % 2, :]
                    pe.wait_ge(sb_masked.sem, sb_masked.at(l, hh + 1))
                    for k in range(T):
                        pe.matmul(sb_bank(hh, k, P), ident_r[:], strictT[:], start=False, stop=False, skip_group_check=True)
                        ins = pe.matmul(sb_bank(hh, k, SB_W[k]), neg_tri[:], sp[:, SB_OFF[k]:SB_OFF[k] + SB_W[k]],
                                        start=False, stop=False, skip_group_check=True)
                        for j in range(k + 1, T):
                            ins = pe.matmul(sb_bank(hh, k, SB_W[j], P * (j - k)), neg_ones[:], sp[:, SB_OFF[j]:SB_OFF[j] + SB_W[j]],
                                            start=False, stop=False, skip_group_check=True)
                    inc(ins, sb_log)

                def sb_values(m):
                    pe.wait_ge(sb_prob.sem, sb_prob.at(l, 2 * m + 2))
                    for k in range(T):
                        for hp in range(2):
                            hh = 2 * m + hp
                            ins = pe.matmul(bank(6 + m, S - P * k, P * k)[HD * hp:HD * hp + HD], proj[:, k, SV + HD * hh:SV + HD * hh + HD],
                                            sb_tmp[hh][:, SB_OFF[k]:SB_OFF[k] + SB_W[k]], start=k == 0, stop=k == T - 1)
                    inc(ins, sb_pv)

                sb_logs(0)
                sb_scores(2)
                sb_logs(1)
                sb_scores(3)
                sb_values(0)
                sb_logs(2)
                sb_logs(3)
                sb_values(1)

                pe.wait_ge(oT_done.sem, oT_done.at(l, 8))
                pe.wait_ge(sb_prob.sem, sb_prob.at(l, 4))
                rows_gemm(U_OUT, 4, 0, lambda i: pe.wait_ge(o_lo.sem, o_lo.at(l, i + 1)))

                pe.wait_ge(mT_lo.sem, mT_lo.at(l, KD))
                for u in range(4):
                    pe.wait_ge(h_done.sem, h_done.at(l, u // 2 + 1))
                    hi, lo = unit(U_XK + u)
                    for m in range(2):
                        for k in range(KD):
                            if m == 0 and k == 4:
                                rest(U_XK + u)
                            mm = slice(P * m, P * m + P)
                            ins = three(bank(u, MEM, MEM * m), hi[:, k, mm], lo[:, k, mm], m_hi[:, k, :], m_lo[:, k, :], k == 0, k == KD - 1)
                    inc(ins, unit_used)
                pe.wait_ge(h_done.sem, h_done.at(l, 4))
                for u in range(4):
                    hi, lo = unit(U_XV + u)
                    for k in range(2):
                        if k == 1:
                            rest(U_XV + u)
                        for t in range(2):
                            for n in range(2):
                                a, st, nn = 2 * u + k, slice(P * t, P * t + P), slice(512 * n, 512 * n + 512)
                                ins = three(bank(4 + 2 * t + n), m_hi[:, a, st], m_lo[:, a, st], hi[:, k, nn], lo[:, k, nn],
                                            u == 0 and k == 0, u == 3 and k == 1)
                                if u == 3 and k == 1 and 2 * t + n < 3:
                                    inc(ins, xv_psum)
                    inc(ins, unit_used)
                    if u == 2:
                        pe.wait_ge(rows_done.sem, rows_done.at(l, 4))
                        pe.wait_ge(xk_ready.sem, xk_ready.at(l, 4))
                        for k in range(4):
                            transpose_rows(1, k)

                def cols_gemm(u, b, done, inst=None):
                    if inst == 2:
                        for k in range(4):
                            transpose_rows(inst, k)
                    hi, lo = unit(u)
                    for m in range(2):
                        for k in range(KD):
                            if m == 0 and k == 4:
                                rest(u)
                            if inst is not None and m == 0:
                                pe.wait_ge(aT_lo.sem, aT_lo.at(l, KD * inst + k + 1))
                                if k < 4:
                                    transpose_rows(inst, k + 4)
                            mm = slice(P * m, P * m + P)
                            ins = three(bank(b + m), hi[:, k, mm], lo[:, k, mm], a_hi[:, k, :], a_lo[:, k, :], k == 0, k == KD - 1)
                        inc(ins, (done, unit_used)[m])

                for u in range(4):
                    if u >= 2:
                        pe.wait_ge(xq_ready.sem, xq_ready.at(l, 2 * (u - 2) + 2))
                    if u < 2:
                        pe.wait_ge(xv_ready.sem, xv_ready.at(l, 2 * u + 2))
                    cols_gemm(U_XQ + u, 4 + 2 * (u % 2), xq_psum, None if u else 1)
                pe.wait_ge(xq_ready.sem, xq_ready.at(l, 8))

                def xscores(i):
                    head, t = divmod(i, 4)
                    if i >= 3:
                        pe.wait_ge(xexped.sem, xexped.at(l, i - 2))
                    for c in range(2):
                        ins = pe.matmul(bank(i % 3, MEM), xqT[:, 2 * head + c, P * t:P * t + P], xkT[:, 2 * head + c, :],
                                        start=c == 0, stop=c == 1)
                    inc(ins, xs)

                def xtransposes(i):
                    pe.wait_ge(xscaled.sem, xscaled.at(l, i + 1))
                    if i >= 2:
                        pe.wait_ge(xpT_ready.sem, xpT_ready.at(l, i - 1))
                    for m in range(2):
                        ins = pe.transpose(bank(3 + i % 2, P, P * m), xprob[:, i % PROBS, P * m:P * m + P], ident[:])
                    inc(ins, xpT_psum)

                def xvalues(j):
                    head = j // 2
                    pe.wait_ge(xpT_ready.sem, xpT_ready.at(l, 4 * head + 4))
                    if j >= 3:
                        pe.wait_ge(xo_lo.sem, xo_lo.at(l, j - 2))
                    for m in range(2):
                        ins = pe.matmul(bank(5 + j % 3), xv[:, m, P * j:P * j + P], xprobT[:, head % 2, m, :],
                                        start=m == 0, stop=m == 1)
                    inc(ins, xo_psum)

                for i in range(XSTEPS):
                    if i < 16:
                        xscores(i)
                    if 0 <= i - XLAG_T < 16:
                        xtransposes(i - XLAG_T)
                    if i in XPIECES:
                        xvalues(XPIECES[i])

                def xo_bank(i, b):
                    if i == 0 and b >= 5:
                        pe.wait_ge(xo_lo.sem, xo_lo.at(l, max(j for j in range(KD) if 5 + j % 3 == b) + 1))

                rows_gemm(U_XO, 4, 1, lambda i: pe.wait_ge(xo_lo.sem, xo_lo.at(l, 2 * i + 2)), xo_bank)

                pe.wait_ge(rows_done.sem, rows_done.at(l, 8))
                for jp in range(11):
                    if jp >= 2:
                        pe.wait_ge(gT_done.sem, gT_done.at(l, 2 * (jp - 2) + 2))
                    cols_gemm(U_UP + 2 * jp, up_bank(jp, 0), up_psum, None if jp else 2)
                    cols_gemm(U_UP + 2 * jp + 1, up_bank(jp, 1), up_psum)

                def down_bank(i, b):
                    if i == 0 and b in (0, 4):
                        pe.wait_ge(gT_done.sem, gT_done.at(l, NF if b else NF - 2))

                rows_gemm(U_DOWN, 12, 2, lambda i: pe.wait_ge(g_lo.sem, g_lo.at(l, i + 1)), down_bank)


            for s in signals.values():
                if id(s) in made:
                    assert made[id(s)] == s.per_layer, [n for n in signals if signals[n] is s] + [made[id(s)]]


_INS = ["x", "mem", "positions", "norm_mix_pre", "norm_mix_post", "w_in", "w_out", "cmp_pe_k", "cmp_pe_v",
        "cmp_wk1", "cmp_wk2", "cmp_wv1", "cmp_wv2", "norm_x_pre", "norm_x_post", "norm_mem",
        "x_wq", "x_wk", "x_wv", "x_wo", "norm_ffn_pre", "norm_ffn_post", "ffn_w_up", "ffn_conv_w",
        "ffn_conv_b", "ffn_w_down"]


def kernel(**inputs):
    import concourse.bacc as bacc
    from concourse.bass_utils import run_bass_kernel_spmd

    nc = bacc.Bacc("TRN2", target_bir_lowering=False, num_devices=1)
    arrays, args = {}, []
    for name in _INS:
        a = np.ascontiguousarray(inputs[name])
        arrays["in_" + name] = a
        args.append(nc.dram_tensor("in_" + name, a.shape, mybir.dt.from_np(a.dtype), kind="ExternalInput").ap())
    out = nc.dram_tensor("out_dram", (1, S, D), F32, kind="ExternalOutput").ap()
    build(nc, *args, out)
    r = run_bass_kernel_spmd(nc, [arrays], core_ids=[0])
    return r.results[0]["out_dram"]
```
